# Optimizing a Trainium2 kernel written in Bass

```python
import jax, jax.numpy as jnp
from jax import lax
import numpy as np

D_MODEL = 1024
BATCH = 1
SEQ = 1024
DEPTH = 2

CHUNK = 64
CONV_WIDTH = 512
CONV_GROUPS = 8
CONV_K = 3
RWKV_WIDTH = 512
RWKV_HEAD = 64
RWKV_HEADS = RWKV_WIDTH // RWKV_HEAD
D_DECAY_LORA = 64
D_AAA_LORA = 64
D_GATE_LORA = 128
A_COLS = 3 * CONV_WIDTH
RWKV_COLS = 3 * RWKV_WIDTH + D_DECAY_LORA + D_AAA_LORA + D_GATE_LORA
EVEN_IN_COLS = A_COLS + RWKV_COLS
EVEN_MIX_WIDTH = CONV_WIDTH + RWKV_WIDTH
N_HEADS = 16
N_KV_HEADS = 2
GROUP = N_HEADS // N_KV_HEADS
HEAD_DIM = 64
WINDOW = 128
WINDOW_CHUNKS = WINDOW // CHUNK
BAND = WINDOW_CHUNKS * CHUNK
QKV_COLS = (N_HEADS + 2 * N_KV_HEADS) * HEAD_DIM
D_FF = 4 * D_MODEL
EPS = 1e-6
LNX_EPS = 64e-5
NEG_INF = -1e30
N_EVEN = (DEPTH + 1) // 2
N_ODD = DEPTH // 2

kernel_name = "hybrid_conv_rwkv7_swa_sink_encoder"

def rms_norm(x, g, eps=EPS):
    xf = x.astype(jnp.float32)
    y = xf * lax.rsqrt(jnp.mean(xf * xf, axis=-1, keepdims=True) + eps)
    return (y * g.astype(jnp.float32)).astype(x.dtype)

def causal_depthwise_conv(u, w):
    c = u.shape[-1]
    return lax.conv_general_dilated(
        u, w.reshape(CONV_K, 1, c).astype(u.dtype),
        window_strides=(1,), padding=[(CONV_K - 1, 0)],
        dimension_numbers=("NWC", "WIO", "NWC"), feature_group_count=c)

def rwkv7_scan(r, w, k, v, a, b):
    bsz, _, nh, n = r.shape
    xs = tuple(jnp.swapaxes(t, 0, 1) for t in (r, w, k, v, a, b))

    def step(state, inp):
        r_t, w_t, k_t, v_t, a_t, b_t = inp
        sa = jnp.einsum("bhvk,bhk->bhv", state, a_t)
        state = (state * w_t[:, :, None, :] + sa[..., None] * b_t[:, :, None, :]
                 + v_t[..., None] * k_t[:, :, None, :])
        return state, jnp.einsum("bhvk,bhk->bhv", state, r_t)

    init = jnp.zeros((bsz, nh, n, n), jnp.float32)
    _, out = lax.scan(step, init, xs)
    return jnp.swapaxes(out, 0, 1)

def conv_rwkv_mixer(h, w_in, conv_w, shift_mu, w0, w_decay2, a0, w_aaa2, w_gate2,
                    k_k, k_a, r_k, lnx_w, lnx_b, w_out):
    bsz, s, _ = h.shape
    proj = h @ w_in
    pa, pb = proj[..., :A_COLS], proj[..., A_COLS:]
    gate_b, gate_c, u = jnp.split(pa, 3, axis=-1)
    y_a = gate_b * causal_depthwise_conv(gate_c * u, conv_w)
    pb = pb.astype(jnp.float32)
    pb_prev = jnp.pad(pb, ((0, 0), (1, 0), (0, 0)))[:, :-1]
    pb = pb + (pb_prev - pb) * shift_mu
    o1 = RWKV_WIDTH
    r, k, v, w_lr, a_lr, g_lr = jnp.split(
        pb, [o1, 2 * o1, 3 * o1, 3 * o1 + D_DECAY_LORA,
             3 * o1 + D_DECAY_LORA + D_AAA_LORA], axis=-1)
    w = -jax.nn.softplus(-(w0 + jnp.tanh(w_lr) @ w_decay2)) - 0.5
    decay = jnp.exp(-jnp.exp(w))
    a = jax.nn.sigmoid(a0 + a_lr @ w_aaa2)
    g = jax.nn.sigmoid(g_lr) @ w_gate2
    hs = lambda t: t.reshape(bsz, s, RWKV_HEADS, RWKV_HEAD)
    kk = hs(k * k_k)
    kk = kk / jnp.maximum(jnp.linalg.norm(kk, axis=-1, keepdims=True), 1e-12)
    k = k * (1.0 + (a - 1.0) * k_a)
    r_h, k_h, v_h, a_h = hs(r), hs(k), hs(v), hs(a)
    out = rwkv7_scan(r_h, hs(decay), k_h, v_h, -kk, kk * a_h)
    mu = jnp.mean(out, axis=-1, keepdims=True)
    var = jnp.mean(jnp.square(out - mu), axis=-1, keepdims=True)
    out = (out - mu) * lax.rsqrt(var + LNX_EPS)
    out = out * lnx_w.reshape(RWKV_HEADS, RWKV_HEAD) + lnx_b.reshape(RWKV_HEADS, RWKV_HEAD)
    out = out + jnp.sum(r_h * k_h * r_k, axis=-1, keepdims=True) * v_h
    y_b = (out.reshape(bsz, s, RWKV_WIDTH) * g).astype(h.dtype)
    return jnp.concatenate([y_a, y_b], axis=-1) @ w_out

def shift_chunks(t, d):
    nc = t.shape[1]
    pad = [(0, 0), (d, 0)] + [(0, 0)] * (t.ndim - 2)
    return jnp.pad(t, pad)[:, :nc]

def swa_sink_mixer(h, w_qkv, q_gain, k_gain, sinks, w_o):
    bsz, s, _ = h.shape
    nc = s // CHUNK
    qkv = h @ w_qkv
    q = qkv[..., :N_HEADS * HEAD_DIM].reshape(bsz, s, N_HEADS, HEAD_DIM)
    k = qkv[..., N_HEADS * HEAD_DIM:(N_HEADS + N_KV_HEADS) * HEAD_DIM].reshape(bsz, s, N_KV_HEADS, HEAD_DIM)
    v = qkv[..., (N_HEADS + N_KV_HEADS) * HEAD_DIM:].reshape(bsz, s, N_KV_HEADS, HEAD_DIM)
    q = rms_norm(q, q_gain).astype(jnp.float32).reshape(bsz, nc, CHUNK, N_KV_HEADS, GROUP, HEAD_DIM)
    k = rms_norm(k, k_gain).astype(jnp.float32).reshape(bsz, nc, CHUNK, N_KV_HEADS, HEAD_DIM)
    v = v.astype(jnp.float32).reshape(bsz, nc, CHUNK, N_KV_HEADS, HEAD_DIM)
    offsets = range(WINDOW_CHUNKS - 1, -1, -1)
    k_band = jnp.concatenate([shift_chunks(k, d) for d in offsets], axis=2)
    v_band = jnp.concatenate([shift_chunks(v, d) for d in offsets], axis=2)
    scores = jnp.einsum("bcqkgd,bcskd->bckgqs", q, k_band) * (HEAD_DIM ** -0.5)
    j = jnp.arange(BAND)
    d_off = WINDOW_CHUNKS - 1 - j // CHUNK
    i = jnp.arange(CHUNK)[:, None]
    dist = jnp.abs(d_off[None, :] * CHUNK + i - (j % CHUNK)[None, :]).astype(jnp.float32)
    slopes = 2.0 ** (-8.0 * jnp.arange(1, N_HEADS + 1, dtype=jnp.float32) / N_HEADS)
    bias = -slopes.reshape(N_KV_HEADS, GROUP)[:, :, None, None] * dist
    valid = jnp.arange(nc)[:, None] >= d_off[None, :]
    scores = jnp.where(valid[None, :, None, None, None, :], scores + bias, NEG_INF)
    sink = sinks.astype(jnp.float32).reshape(N_KV_HEADS, GROUP)[None, None, :, :, None, None]
    m = jnp.maximum(jnp.max(scores, axis=-1, keepdims=True), sink)
    p = jnp.exp(scores - m)
    denom = jnp.sum(p, axis=-1, keepdims=True) + jnp.exp(sink - m)
    o = jnp.einsum("bckgqs,bcskd->bcqkgd", p / denom, v_band)
    return o.reshape(bsz, s, N_HEADS * HEAD_DIM).astype(h.dtype) @ w_o

def squared_relu_mlp(h, w_up, w_down):
    return jnp.square(jax.nn.relu(h @ w_up)) @ w_down

def setup_inputs(seed: int = 0) -> dict:
    key = jax.random.key(seed)
    ks = jax.random.split(key, 32)
    nrm = lambda k, shape, scale: jax.random.normal(k, shape, jnp.float32) * scale
    d = D_MODEL
    return {
        "x": nrm(ks[0], (BATCH, SEQ, d), 1.0),
        "norm_mix": 1.0 + nrm(ks[1], (DEPTH, d), 0.02),
        "norm_mlp": 1.0 + nrm(ks[2], (DEPTH, d), 0.02),
        "mlp_up": nrm(ks[3], (DEPTH, d, D_FF), d ** -0.5),
        "mlp_down": nrm(ks[4], (DEPTH, D_FF, d), D_FF ** -0.5),
        "w_in_ab": nrm(ks[5], (N_EVEN, d, EVEN_IN_COLS), d ** -0.5),
        "conv_w": nrm(ks[6], (N_EVEN, CONV_K, CONV_WIDTH), CONV_K ** -0.5),
        "shift_mu": jax.random.uniform(ks[7], (N_EVEN, RWKV_COLS), jnp.float32),
        "w0": jax.random.uniform(ks[8], (N_EVEN, RWKV_WIDTH), jnp.float32, -3.0, 1.0),
        "w_decay2": nrm(ks[9], (N_EVEN, D_DECAY_LORA, RWKV_WIDTH), 0.5 * D_DECAY_LORA ** -0.5),
        "a0": nrm(ks[10], (N_EVEN, RWKV_WIDTH), 0.1),
        "w_aaa2": nrm(ks[11], (N_EVEN, D_AAA_LORA, RWKV_WIDTH), 0.5 * D_AAA_LORA ** -0.5),
        "w_gate2": nrm(ks[12], (N_EVEN, D_GATE_LORA, RWKV_WIDTH), D_GATE_LORA ** -0.5),
        "k_k": 0.85 + nrm(ks[13], (N_EVEN, RWKV_WIDTH), 0.05),
        "k_a": 1.0 + nrm(ks[14], (N_EVEN, RWKV_WIDTH), 0.05),
        "r_k": nrm(ks[15], (N_EVEN, RWKV_HEADS, RWKV_HEAD), 0.1),
        "lnx_w": 1.0 + nrm(ks[16], (N_EVEN, RWKV_WIDTH), 0.02),
        "lnx_b": nrm(ks[17], (N_EVEN, RWKV_WIDTH), 0.02),
        "w_out_ab": nrm(ks[18], (N_EVEN, EVEN_MIX_WIDTH, d), EVEN_MIX_WIDTH ** -0.5),
        "w_qkv": nrm(ks[19], (N_ODD, d, QKV_COLS), d ** -0.5),
        "q_gain": 1.0 + nrm(ks[20], (N_ODD, HEAD_DIM), 0.02),
        "k_gain": 1.0 + nrm(ks[21], (N_ODD, HEAD_DIM), 0.02),
        "sinks": nrm(ks[22], (N_ODD, N_HEADS), 0.5),
        "w_o": nrm(ks[23], (N_ODD, N_HEADS * HEAD_DIM, d), (N_HEADS * HEAD_DIM) ** -0.5),
    }

def reference(x, norm_mix, norm_mlp, mlp_up, mlp_down, w_in_ab, conv_w, shift_mu, w0,
              w_decay2, a0, w_aaa2, w_gate2, k_k, k_a, r_k, lnx_w, lnx_b, w_out_ab,
              w_qkv, q_gain, k_gain, sinks, w_o):
    for layer in range(DEPTH):
        i = layer // 2
        h = rms_norm(x, norm_mix[layer])
        if layer % 2 == 0:
            y = conv_rwkv_mixer(h, w_in_ab[i], conv_w[i], shift_mu[i], w0[i], w_decay2[i],
                                a0[i], w_aaa2[i], w_gate2[i], k_k[i], k_a[i], r_k[i],
                                lnx_w[i], lnx_b[i], w_out_ab[i])
        else:
            y = swa_sink_mixer(h, w_qkv[i], q_gain[i], k_gain[i], sinks[i], w_o[i])
        x = x + y
        x = x + squared_relu_mlp(rms_norm(x, norm_mlp[layer]), mlp_up[layer], mlp_down[layer])
    return x


_drawn_inputs = setup_inputs


def setup_inputs(seed=0):
    import zlib

    import numpy as np

    out = dict(_drawn_inputs(seed))
    spreads = {}
    factors = {'w_decay2': 3.162,
     'a0': 3.376,
     'k_k': 8.0,
     'k_a': 3.184,
     'lnx_w': 8.0,
     'lnx_b': 8.0,
     'q_gain': 8.0,
     'k_gain': 8.0,
     'sinks': 4.662}
    for name, (base, spread) in spreads.items():
        noise = np.random.default_rng([zlib.crc32(name.encode()), seed]).standard_normal(out[name].shape)
        drawn = base * np.exp(spread * noise) if base else spread * noise
        out[name] = __import__('jax').numpy.asarray(drawn.astype(out[name].dtype))
    for name, factor in factors.items():
        out[name] = (out[name] * factor).astype(out[name].dtype)
    return out
```

```python
from contextlib import ExitStack

import numpy as np

import concourse.bass as bass
from concourse import mybir
from concourse.alu_op_type import AluOpType as ALU

ACT = mybir.ActivationFunctionType
AXX = mybir.AxisListType.X
F32 = mybir.dt.float32
F32R = mybir.dt.float32r

P = 128
D = 1024
S = 1024
KD = D // P
HALF = 512
NT = S // P
RH = 64
NP_ = 4
KAPPA = 0.6065306597126334
EPS = 1e-6
LNX_EPS = 64e-5
LEVELS = 6
NQ, NKV = 16, 2
WIN = 192
GF = 4
NG = 4096 // P // GF

C_ID, C_BLK, C_ONE, C_MU, C_MX, C_M0, C_RST, C_DIST = 0, 128, 256, 384, 640, 1408, 1536, 2048
C_END = C_DIST + 2 * WIN

V_MIX, V_MLP, V_MU, V_W0, V_A0, V_KK, V_KA, V_RK, V_LW, V_LB, V_CW, V_QG, V_KG = (
    0, 16, 32, 46, 50, 54, 58, 62, 66, 70, 74, 86, 87)
V_ROWS = 88
V_QS = 88

STAGE = {"in": (0, 0), "out": (26, 26), "mlp0": (34, 34), "qkv": (98, 130), "wo": (108, 140),
         "mlp1": (116, 148)}
A_END = 148 + 96
N_CONST = 20
H_FILL = {"in": 0, "out": 1, "mlp0": 2, "qkv": 3, "wo": 4, "mlp1": 5}


def shape_constants():
    c = np.zeros((P, C_END), np.float32)
    i = np.arange(P)
    row, col = i[:, None], i[None, :]
    c[:, C_ID:C_ID + P] = row == col
    c[:, C_BLK:C_BLK + P] = row // RH == col // RH
    c[:, C_ONE:C_ONE + P] = 1.0
    c[:, C_MU:C_MU + P] = row < col
    c[:, C_MU + P:C_MU + 2 * P] = row <= col
    for k in range(LEVELS):
        b = 2 << k
        c[:, C_MX + k * P:C_MX + (k + 1) * P] = (
            (row // (2 * b) == col // (2 * b)) & (row % (2 * b) < b) & (col % (2 * b) >= b))
    c[:, C_M0:C_M0 + P] = (row % 2 == 0) & (col == row + 1)
    c[:, C_RST:C_RST + 4 * P] = (np.arange(4 * P) % P != 0)[None, :]
    key = np.arange(WIN)[None, :]
    dist = np.abs(row - key + RH).astype(np.float32)
    seen = (key // RH == row // RH) | (key // RH == row // RH + 1)
    c[:, C_DIST:C_DIST + WIN] = np.where(seen, dist, np.float32(1e34))
    first = seen & (key >= RH)
    c[:, C_DIST + WIN:C_END] = np.where(first, dist, np.float32(1e34))
    return c


def hybrid_trunk(nc, x, norm_mix, norm_mlp, mlp_up, mlp_down, w_in_ab, conv_w, shift_mu, w0,
                 w_decay2, a0, w_aaa2, w_gate2, k_k, k_a, r_k, lnx_w, lnx_b, w_out_ab, w_qkv,
                 q_gain, k_gain, sinks, w_o, consts, out):
    ya_dram = nc.dram_tensor("ya_spill", (4, P, S), F32).ap()
    base = 16512

    def at(name, shape, kb, dt=F32):
        return nc.alloc_sbuf_tensor_at(name, [P] + shape, dt, offset=base + int(kb * 1024))

    X = at("residual", [KD, S], 0)
    Hh = at("h_hi", [KD, S], 32, F32R)
    Hl = at("h_lo", [KD, S], 64, F32R)
    WR = at("w_raw", [2, 1024], 96)
    WH = at("w_hi", [2, 1024], 104, F32R)
    WL = at("w_lo", [2, 1024], 112, F32R)
    ACh = at("mlp_hi", [GF, S], 120, F32R)
    ACl = at("mlp_lo", [GF, S], 136, F32R)
    RKV = at("rkv", [12, S], 120)
    WA = at("decay_aaa_in", [S], 168)
    GL = at("gate_in", [S], 172)
    ST0 = at("stage0", [S + 4], 176)
    ST1 = at("stage1", [S + 4], 180.25)
    ST2 = at("stage2", [S + 4], 184.5)
    CON = at("constants", [C_END], 189)
    LOR = at("lora_w", [2, 4 * P], 198.5)
    VT = at("vectors", [96], 202.5)
    SNK = at("sink_cols", [NQ], 203)
    NSNK = at("minus_sinks", [NQ], 203.0625)
    T6 = at("prep_t6", [4, P], 203.25)
    GS = at("decay_ends", [2, 2, 4], 205.5)
    GSR = at("decay_ends_raw", [2, 4], 205.75)
    XT8 = at("x_tile", [2, 8, P], 32)
    VROW = at("vector_rows", [P], 48)
    AR = at("a_r_dec", [2, 4, 2, P], 32)
    BK = at("b_k_dec", [2, 2, 4, P], 40)
    VC = at("v_chunk", [2, 4, P], 48)
    BON = at("bonus", [2, 4, P], 52)
    G1M = at("decay_in_mask", [2, 4, P], 56)
    TOK = at("token_major", [4, 4 * P], 60)
    MTRB = at("mt_rb", [8, 2, P], 68)
    NTRK = at("nt_rk", [8, 2, P], 76)
    TI = at("tri_inv", [8, P], 84)
    TIT = at("tri_inv_t", [8, P], 88)
    WT = at("w_t", [4, P], 92)
    ZZ = at("z_part", [4 * P], 94)
    YL = at("y_level", [8, P], 176)
    XL = at("x_level", [8, P], 180)
    SS = at("state", [4, P], 184)
    SP_ = at("state_in", [4, P], 186)
    NV = at("nv_part", [4 * P], 104)
    UU = at("u_part", [4 * P], 106)
    T0, T1, T2, T3, T4 = (at(f"prep_t{n}", [4, P], 108 + 2 * n) for n in range(5))
    T5 = at("prep_t5", [4, P], 118)
    WAG = at("lora_chunk", [P], 188)
    Q = at("q_then_o", [KD, S], 120)
    K2 = at("k_zero_padded", [NKV, 2, S + RH], 152)
    VP = at("v_padded", [S + 2 * RH], 169.5)
    SQ = at("squares", [S], 190.5)
    QST = at("q_tile", [2, KD, P], 32)
    VST = at("v_window", [2, 2, P], 43)
    VTOK = at("v_token_major", [9, P], 45)
    PP = at("probs", [2, NQ, WIN], 50)
    PTA = at("probs_t_a", [NQ, P], 74)
    PTB = at("probs_t_b", [NQ, P], 82)
    STA = at("softmax_stats", [2, 6, NQ], 90)

    with ExitStack() as ctx:
        PS = ctx.enter_context(nc.psum_tensor("ps", [P, 8, HALF], F32))

        def sem(name):
            return ctx.enter_context(nc.semaphore(name))

        w_load = [sem("w_load0"), sem("w_load1")]
        w_hi, w_lo = sem("w_hi_done"), sem("w_lo_done")
        acc_done = sem("acc_done")
        acc_free = [sem("acc_free0"), sem("acc_free1")]
        h_tmp, h_hi, h_lo = sem("h_tmp"), sem("h_hi_done"), sem("h_lo_done")
        const_in, x_in = sem("const_in"), [sem("x_in0"), sem("x_in1")]
        vec_t, vec_ok, eps_set = sem("vectors_transposed"), sem("vectors_ready"), sem("eps_set")
        pads_zero, conv_zero, shift_zero = sem("attn_pads_zero"), sem("conv_zero"), sem("shift_zero")
        x_tr, x_ev = sem("x_transposed"), sem("x_evacuated")
        block = ctx.enter_context(nc.Block())

        seq = {"act": sem("act_waited"), "pool": sem("pool_waited"), "dve": sem("dve_waited")}

        def waited(engine, name):
            engine.sem_inc(seq[name], 1)

        ident = CON[:, C_ID:C_ID + P]
        blk = CON[:, C_BLK:C_BLK + P]
        ones = CON[:, C_ONE:C_ONE + P]

        def vb(row, n=4, m=P):
            return VT[:, row:row + n].unsqueeze(2).to_broadcast([P, n, m])

        def over(ap, n):
            return ap.unsqueeze(1).to_broadcast([P, n, ap.shape[1]])

        def acc(a_slot, half=None):
            return (PS[:, 2 * a_slot:2 * a_slot + 2, :] if half is None
                    else PS[:, 2 * a_slot + half, :])

        def acc2(a_slot):
            return acc(a_slot).rearrange("p b n -> p (b n)")

        win = w_in_ab[0].rearrange("(k p) n -> p k n", p=P)
        wout = w_out_ab[0].rearrange("(k p) n -> p k n", p=P)
        wqkv = w_qkv[0].rearrange("(k p) n -> p k n", p=P)
        wo = w_o[0].rearrange("(k p) n -> p k n", p=P)
        wup = [mlp_up[l].rearrange("(k p) n -> p k n", p=P) for l in range(2)]
        wdn = [mlp_down[l].rearrange("(g k p) n -> g p k n", k=GF, p=P) for l in range(2)]

        def load_unit(sp, slot, u, src, k=8):
            sp.wait_ge(w_lo, u + 1)
            sp.dma_start(WR[:, slot].rearrange("p (k n) -> p k n", k=k), src).then_inc(w_load[slot], 16)

        def split_hi(act, slot, n, need):
            act.wait_ge(w_load[slot], 16 * n + 16)
            act.wait_ge(acc_done, need)
            nc.scalar.copy(WH[:, slot], WR[:, slot]).then_inc(w_hi, 1)

        def split_lo(dve, slot, u):
            dve.wait_ge(w_hi, u + 1)
            nc.vector.tensor_tensor(WL[:, slot], WR[:, slot], WH[:, slot].bitcast(F32),
                                    ALU.subtract).then_inc(w_lo, 1)

        def load_stage(sp, name, src, units):
            u0, _ = STAGE[name]
            with sp.Fori(0, units // 2) as i:
                for j in range(2):
                    load_unit(sp, j, u0 + 2 * i + j, src[:, :, bass.ds((2 * i + j) * P, P)])

        def load_mlp(sp, l):
            u0, _ = STAGE[f"mlp{l}"]
            with sp.Fori(0, NG) as g:
                for j in range(4):
                    load_unit(sp, j % 2, u0 + 8 * g + j, wup[l][:, :, bass.ds(g * 512 + j * P, P)])
                for d in range(4):
                    src = wdn[l][bass.ds(g, 1)].rearrange("a p k n -> p (a k) n")
                    load_unit(sp, d % 2, u0 + 8 * g + 4 + d, src[:, :, 256 * d:256 * d + 256], k=4)

        def product(t, slot, a_slot, a_half, u, nk, step, off, xh, xl, ready=None, order=None,
                    new_unit=True):
            if new_unit:
                t.wait_ge(w_lo, u + 3)
            t.wait_ge(acc_free[a_slot], a_half + 1)
            order = order or list(range(nk))
            for n, k in enumerate(order):
                if ready is not None:
                    t.wait_ge(ready[0], ready[1] + n + 1)
                w_h = WH[:, slot, k * step + off:k * step + off + P]
                w_l = WL[:, slot, k * step + off:k * step + off + P]
                for ww, xx in ((w_h, xh), (w_h, xl), (w_l, xh)):
                    first, last = n == 0 and ww is w_h and xx is xh, n == nk - 1 and ww is w_l
                    for half in range(2):
                        m = nc.tensor.matmul(acc(a_slot, half), ww,
                                             xx[:, k, half * HALF:(half + 1) * HALF],
                                             start=first, stop=last)
            m.then_inc(acc_done, 1)

        def dense_pe(t, name, units, order=None, loops=None):
            u0, a0_ = STAGE[name]
            fill = H_FILL[name]
            with t.Fori(0, units // 2) as i:
                for j in range(2):
                    product(t, j, j, a0_ // 2 + i, u0 + 2 * i + j, 8, P, 0, Hh, Hl,
                            ready=(h_lo, 8 * fill) if j == 0 else None, order=order)

        act_lo = sem("mlp_lo_done")

        def mlp_pe(t, l):
            u0, a0_ = STAGE[f"mlp{l}"]
            with t.Fori(0, NG) as g:
                for j in range(4):
                    product(t, j % 2, j % 2, a0_ // 2 + 6 * g + j // 2, u0 + 8 * g + j, 8, P, 0,
                            Hh, Hl, ready=(h_lo, 8 * H_FILL[f"mlp{l}"]) if j == 0 else None)
                for m in range(8):
                    product(t, m // 2 % 2, m % 2, a0_ // 2 + 6 * g + 2 + m // 2, u0 + 8 * g + 4 + m // 2,
                            GF, 256, P * (m % 2), ACh, ACl,
                            ready=(act_lo, 4 * NG * l + 4 * g + 1) if m == 0 else None,
                            new_unit=m % 2 == 0)

        sq_done, ss_add, ss_done = sem("squared"), sem("squares_added"), sem("sum_over_features")
        rms_done, rinv_done = sem("rms_done"), sem("rms_inverted")
        NORMS = {"in": 0, "mlp0": 1, "qkv": 2, "mlp1": 3}

        def residual_done(engine, name):
            if name == "in":
                engine.wait_ge(x_ev, 2 + NT)
            else:
                engine.wait_ge(acc_free[1], (STAGE[name][1] if name in STAGE else A_END) // 2 + 1)

        def norm_act(act, name):
            n, f = NORMS[name], H_FILL[name]
            residual_done(act, name)
            for k in range(KD):
                dst = (ST2, ST0, ST1)[0 if k == 0 else 1 + k % 2]
                if k >= 3:
                    act.wait_ge(ss_add, 7 * n + k - 2)
                nc.scalar.activation(dst[:, 0:S], X[:, k], ACT.Square).then_inc(sq_done, 1)
            act.wait_ge(ss_done, n + 1)
            act.wait_ge(ss_add, 7 * n + 7)
            nc.scalar.activation(ST2[:, 0:S], PS[:, 4:6, :].rearrange("p b n -> p (b n)"), ACT.Sqrt,
                                 bias=VT[:, 90:91], scale=1.0 / D).then_inc(rms_done, 1)
            for k in range(KD):
                act.wait_ge(h_tmp, 8 * n + k + 1)
                nc.scalar.copy(Hh[:, k], (ST0, ST1)[k % 2][:, 0:S]).then_inc(h_hi, 1)

        def norm_dve(dve, name, row):
            n, f = NORMS[name], H_FILL[name]
            for k in range(1, KD):
                dve.wait_ge(sq_done, 8 * n + k + 1)
                if k > 1:
                    dve.wait_ge(ss_add, 7 * n + k - 1)
                nc.vector.tensor_tensor(ST2[:, 0:S], ST2[:, 0:S], (ST0, ST1)[k % 2][:, 0:S],
                                        ALU.add).then_inc(ss_add, 1)
            dve.wait_ge(rms_done, n + 1)
            nc.vector.reciprocal(ST2[:, 0:S], ST2[:, 0:S]).then_inc(rinv_done, 1)
            dve.wait_ge(rinv_done, n + 1)
            for k in range(KD):
                tmp = (ST0, ST1)[k % 2]
                if k >= 2:
                    dve.wait_ge(h_lo, 8 * f + k - 1)
                nc.vector.scalar_tensor_tensor(tmp[:, 0:S], X[:, k], VT[:, row + k:row + k + 1],
                                               ST2[:, 0:S], ALU.mult, ALU.mult).then_inc(h_tmp, 1)
                if k >= 1:
                    h_lo_split(dve, f, k - 1, (ST0, ST1)[(k - 1) % 2][:, 0:S])
            h_lo_split(dve, f, KD - 1, (ST0, ST1)[(KD - 1) % 2][:, 0:S])

        def h_lo_split(dve, f, k, src, pos=None):
            pos = k if pos is None else pos
            dve.wait_ge(h_hi, 8 * f + pos + 1)
            nc.vector.tensor_tensor(Hl[:, k], src, Hh[:, k].bitcast(F32), ALU.subtract).then_inc(h_lo, 1)

        def norm_pe(t, name):
            n = NORMS[name]
            t.wait_ge(ss_add, 7 * n + 7)
            for half in range(2):
                m = nc.tensor.matmul(PS[:, 4 + half], ones, ST2[:, half * HALF:(half + 1) * HALF],
                                     start=True, stop=True)
            m.then_inc(ss_done, 1)

        relu_sq, act_hi = sem("relu_squared"), sem("mlp_hi_done")

        def mlp_act(act, l, g, last=False):
            u0, a0_ = STAGE[f"mlp{l}"]
            ag, n = a0_ + 12 * g, 4 * NG * l + 4 * g
            need = [None, ag + 2, ag + 3, ag + 4, ag + 5, ag + 6, ag + 8, ag + 10, ag + 13]
            for j in range(8):
                if not (last and j == 7):
                    split_hi(act, (j + 1) % 2, u0 // 2 + 4 * g + (j + 1) // 2, need[j + 1])
                if j < 4:
                    act.wait_ge(acc_done, ag + j + 3)
                    act.wait_ge(act_lo, n + j + 1)
                    nc.scalar.activation(ST0[:, 0:S], acc2(j % 2), ACT.Relu).then_inc(acc_free[j % 2], 1)
                    act.wait_ge(relu_sq, n + j + 1)
                    nc.scalar.copy(ACh[:, j], ST1[:, 0:S]).then_inc(act_hi, 1)

        def mlp_dve(dve, l, g, last=False):
            u0, a0_ = STAGE[f"mlp{l}"]
            ag, n = a0_ + 12 * g, 4 * NG * l + 4 * g
            for j in range(8):
                if not (last and j == 7):
                    split_lo(dve, (j + 1) % 2, u0 + 8 * g + j + 1)
                if j < 4:
                    dve.wait_ge(acc_free[j % 2], a0_ // 2 + 6 * g + j // 2 + 2)
                    nc.vector.tensor_tensor(ST1[:, 0:S], ST0[:, 0:S], ST0[:, 0:S], ALU.mult).then_inc(relu_sq, 1)
                    dve.wait_ge(act_hi, n + j + 1)
                    nc.vector.tensor_tensor(ACl[:, j], ST1[:, 0:S], ACh[:, j].bitcast(F32),
                                            ALU.subtract).then_inc(act_lo, 1)
                else:
                    for m in (2 * (j - 4), 2 * (j - 4) + 1):
                        dve.wait_ge(acc_done, ag + 4 + m + 3)
                        nc.vector.tensor_tensor(X[:, m], X[:, m], acc2(m % 2), ALU.add)\
                            .then_inc(acc_free[m % 2], 1)

        def residual_act(act, name, units):
            u0, a0_ = STAGE[name]
            with act.Fori(0, units // 2) as i:
                for j in range(2):
                    split_hi(act, 1 - j, u0 // 2 + i + j, a0_ + 2 * i + j + 2)

        def residual_dve(dve, name, units):
            u0, a0_ = STAGE[name]
            with dve.Fori(0, units // 2) as i:
                for j in range(2):
                    split_lo(dve, 1 - j, u0 + 2 * i + j + 1)
                    dve.wait_ge(acc_done, a0_ + 2 * i + j + 3)
                    xk = X[:, bass.ds(2 * i + j, 1), :]
                    nc.vector.tensor_tensor(xk, xk, acc2(j).unsqueeze(1), ALU.add).then_inc(acc_free[j], 1)

        conv_step, conv_done, ya_out = sem("conv_step"), sem("conv_done"), sem("ya_out")
        gl_free = sem("conv_output_left")
        shift_diff, shift_done = sem("shift_diff"), sem("shift_done")
        lora_act = sem("lora_inputs_activated")

        def in_act(act):
            split_hi(act, 0, 0, 1)
            with act.Fori(0, 2) as i:
                for q in range(2):
                    for r in range(3):
                        j = 3 * q + r
                        split_hi(act, (j + 1) % 2, 3 * i + (j + 1) // 2, 6 * i + j + 2)
                        act.wait_ge(acc_done, 6 * i + j + 3)
                        act.wait_ge(conv_done, 2 * i + q + 1)
                        nc.scalar.copy((ST0[:, 0:S], ST1[:, 0:S], WA[:, 0:S])[r], acc2(j % 2))\
                            .then_inc(acc_free[j % 2], 1)
            with act.Fori(0, 6) as i:
                for j in range(2):
                    split_hi(act, 1 - j, 6 + i + j, 12 + 2 * i + j + 2)
                    shift_copy(act, 2 * i + j, j, 12 + 2 * i + j)
            split_hi(act, 1, 12, 26)
            shift_copy(act, 12, 0, 24)
            shift_copy(act, 13, 1, 25)
            act.wait_ge(shift_done, 2 + 14)
            nc.scalar.activation(WA[0:RH, :], WA[0:RH, :], ACT.Tanh).then_inc(lora_act, 1)
            nc.scalar.activation(GL[:, :], GL[:, :], ACT.Sigmoid).then_inc(lora_act, 1)

        def shift_copy(act, n, slot, a):
            act.wait_ge(acc_done, a + 3)
            act.wait_ge(conv_done, 5)
            act.wait_ge(shift_done, n + 1)
            nc.scalar.copy((ST0, ST1)[slot][:, 1:S + 1], acc2(slot)).then_inc(acc_free[slot], 1)

        def in_dve(dve):
            nc.vector.memset(ST2[:, 0:2], 0.0).then_inc(conv_zero, 1)
            dve.wait_ge(conv_zero, 1)
            split_lo(dve, 0, 0)
            with dve.Fori(0, 2) as i:
                for q in range(2):
                    for r in range(3):
                        split_lo(dve, (3 * q + r + 1) % 2, 6 * i + 3 * q + r + 1)
                    g = 2 * i + q
                    w = VT[:, bass.ds(V_CW + g, 1)], VT[:, bass.ds(V_CW + 4 + g, 1)], \
                        VT[:, bass.ds(V_CW + 8 + g, 1)]
                    dve.wait_ge(acc_free[q], 3 * i + q + 3)
                    cu = ST2
                    nc.vector.tensor_tensor(cu[:, 2:S + 2], ST1[:, 0:S], WA[:, :], ALU.mult).then_inc(conv_step, 1)
                    dve.wait_ge(conv_step, 4 * g + 1)
                    dve.wait_ge(gl_free, g + 1)
                    nc.vector.tensor_scalar(GL[:, :], cu[:, 2:S + 2], w[2], None, ALU.mult).then_inc(conv_step, 1)
                    for n in (1, 0):
                        dve.wait_ge(conv_step, 4 * g + 3 - n)
                        nc.vector.scalar_tensor_tensor(GL[:, :], cu[:, n:S + n], w[n], GL[:, :], ALU.mult,
                                                       ALU.add).then_inc(conv_step, 1)
                    dve.wait_ge(conv_step, 4 * g + 4)
                    nc.vector.tensor_tensor(GL[:, :], GL[:, :], ST0[:, 0:S], ALU.mult).then_inc(conv_done, 1)
            dve.wait_ge(conv_done, 5)
            nc.vector.memset(ST0[:, 0:1], 0.0).then_inc(shift_zero, 1)
            nc.vector.memset(ST1[:, 0:1], 0.0).then_inc(shift_zero, 1)
            dve.wait_ge(shift_zero, 2)
            with dve.Fori(0, 6) as i:
                for j in range(2):
                    split_lo(dve, 1 - j, 12 + 2 * i + j + 1)
                    shift(dve, 2 * i + j, j, 6 + i, RKV[:, bass.ds(2 * i + j, 1), :])
            split_lo(dve, 1, 25)
            dve.wait_ge(gl_free, 5)
            shift(dve, 12, 0, 12, WA[:, :].unsqueeze(1))
            shift(dve, 13, 1, 12, GL[:, :].unsqueeze(1))

        def shift(dve, n, slot, half, dst):
            st = (ST0, ST1)[slot]
            dve.wait_ge(acc_free[slot], half + 2)
            nc.vector.tensor_tensor(dst, st[:, 0:S].unsqueeze(1), st[:, 1:S + 1].unsqueeze(1), ALU.subtract)\
                .then_inc(shift_diff, 1)
            dve.wait_ge(shift_diff, n + 1)
            mu = VT[:, bass.ds(V_MU + n, 1)]
            nc.vector.scalar_tensor_tensor(dst, dst, mu, st[:, 1:S + 1].unsqueeze(1), ALU.mult, ALU.add)\
                .then_inc(shift_done, 1)

        class Track:

            def __init__(self, name, steps):
                self.sem, self.steps, self.next = sem(name), steps, 0

            def done(self, instruction, step):
                assert self.steps[self.next] == step, (self.steps[self.next], step)
                self.next = (self.next + 1) % len(self.steps)
                instruction.then_inc(self.sem, 1)

            def wait(self, engine, chunk, step):
                engine.wait_ge(self.sem, len(self.steps) * chunk + (self.steps.index(step) + 1))

        two = (0, 1)
        prep_pool = Track("prep_pool", ["wag", "vc", "g1m"])
        prep_pe = Track("prep_pe", ["zw", "za", "n2", "bon"])
        prep_act = Track("prep_act", ["sq", "sw", "a", "g", "e1", "e2", "e1x", "nrm"])
        prep_dve = Track("prep_dve", ["zws", "kkr", "zas", "scan", "mid", "end", "d", "dx", "max", "rcp", "kkn",
                                      "a_dec", "b0", "b_dec", "ka", "k2", "k_dec", "r_dec", "rk", "rk2", "bon"])
        solve_pe = Track("solve_pe", ["tok0", "tok1", "tok2", "tok3", "p1_0", "p2_0", "p1_1", "p2_1", "nv",
                                      "t0_0", "t0_1"]
                         + [f"{w}{k}_{b}" for k in range(LEVELS) for w, b in
                            (("y", 0), ("y", 1), ("dt", 0), ("dtt", 0), ("dt", 1), ("dtt", 1))
                            if not (w == "dt" and k == LEVELS - 1)]
                         + ["wt", "z", "u", "s", "o"])
        solve_act = Track("solve_act", ["tok0", "tok1", "tok2", "tok3", "nv", "t0_0", "t0_1"]
                          + [f"y{k}_{b}" for k in range(LEVELS) for b in two] + ["wt", "z", "o"])
        solve_dve = Track("solve_dve", ["m0", "n0", "m1", "n1", "s_in"]
                          + [f"{w}{k}_{b}" for k in range(LEVELS) for b in two for w in ("t", "tt")
                             if not (w == "t" and k == LEVELS - 1)] + ["u", "s1", "s"])
        solve_pool = Track("solve_pool", ["i0", "tt_0", "x0_0", "i1", "tt_1", "x0_1"]
                           + [f"x{k}_{b}" for k in range(1, LEVELS) for b in two])
        out_pe = Track("out_pe", ["mean", "var", "gate"])
        out_act = Track("out_act", ["sq", "sd"])
        out_dve = Track("out_dve", ["d", "rcp", "m1", "m2", "m3", "m4", "yb"])
        state_zero = sem("state_zero")

        def bank(n):
            return PS[:, n, :].rearrange("p (a m) -> p a m", m=P)

        def part(c, first):
            return RKV[:, first:first + 4, bass.ds(c * P, P)]

        def heads(ap, b):
            return ap[:, 4 * b:4 * b + 4]

        def prep_pool_step(pool, e, s, level):
            if level == 0:
                if not (isinstance(e, int) and e == 0):
                    prep_pe.wait(pool, e - 1, "za")
                    waited(pool, "pool")
                prep_pool.done(nc.gpsimd.tensor_copy(WAG[:, :], WA[:, bass.ds(e * P, P)]), "wag")
                prep_pool.done(nc.gpsimd.tensor_copy(VC[:, s], part(e, 8)), "vc")
            if level == 3:
                prep_act.wait(pool, e, "g")
                prep_pool.done(nc.gpsimd.tensor_tensor(
                    G1M[:, s], over(blk, 4), GS[:, s, 0].unsqueeze(2).to_broadcast([P, 4, P]), ALU.mult), "g1m")

        def prep_pe_step(t, e, s, level):
            if level == 0:
                prep_pool.wait(t, e, "wag")
                for p in range(4):
                    m = nc.tensor.matmul(bank(7)[:, p], LOR[0:RH, 0, p * P:(p + 1) * P], WAG[0:RH, :],
                                         start=True, stop=True)
                prep_pe.done(m, "zw")
            if level == 1:
                prep_dve.wait(t, e, "zws")
                for p in range(4):
                    m = nc.tensor.matmul(bank(7)[:, p], LOR[RH:P, 0, p * P:(p + 1) * P], WAG[RH:P, :],
                                         start=True, stop=True)
                prep_pe.done(m, "za")
            if level == 3:
                prep_dve.wait(t, e, "zas")
                prep_act.wait(t, e, "sq")
                prep_pe.done(nc.tensor.matmul(bank(7), blk, T6[:, :], start=True, stop=True), "n2")
            if level == 5:
                prep_act.wait(t, e, "nrm")
                prep_dve.wait(t, e, "rk2")
                prep_pe.done(nc.tensor.matmul(bank(7), blk, T1[:, :], start=True, stop=True), "bon")

        def prep_act_step(act, e, s, level):
            A = nc.scalar.activation
            if level == 0:
                prep_dve.wait(act, e, "kkr")
                prep_act.done(A(T6[:, :], T5[:, :], ACT.Square), "sq")
                prep_act.done(A(T0[:, :], T0[:, :], ACT.Sigmoid), "sw")
            if level == 1:
                prep_dve.wait(act, e, "zas")
                prep_act.done(A(T1[:, :], T1[:, :], ACT.Sigmoid), "a")
            if level == 2:
                prep_dve.wait(act, e, "dx")
                prep_act.done(A(GS[:, s], GSR[:, :], ACT.Exp, scale=-KAPPA), "g")
                prep_act.done(A(T2[:, :], T3[:, :], ACT.Exp, scale=-KAPPA), "e1")
                prep_act.wait(act, e, "e1")
                prep_act.done(A(T3[:, :], T3[:, :], ACT.Exp, scale=KAPPA), "e2")
                prep_act.done(A(T4[:, :], T4[:, :], ACT.Exp, scale=-KAPPA), "e1x")
            if level == 3:
                prep_pe.wait(act, e, "n2")
                prep_act.done(A(T6[:, :], bank(7), ACT.Sqrt), "nrm")

        def prep_dve_step(dve, e, s, level):
            V, TT, STT = prep_dve, nc.vector.tensor_tensor, nc.vector.scalar_tensor_tensor
            k, r = part(e, 4), part(e, 0)
            if level == 0:
                prep_pe.wait(dve, e, "zw")
                V.done(TT(T0[:, :], bank(7), vb(V_W0), ALU.add), "zws")
                V.done(TT(T5[:, :], k, vb(V_KK), ALU.mult), "kkr")
            if level == 1:
                prep_pe.wait(dve, e, "za")
                V.done(TT(T1[:, :], bank(7), vb(V_A0), ALU.add), "zas")
                prep_act.wait(dve, e, "sw")
                flat = lambda ap: ap.rearrange("p a n -> p (a n)")
                V.done(nc.vector.tensor_tensor_scan(flat(T2[:, :]), CON[:, C_RST:C_RST + 4 * P], flat(T0[:, :]),
                                                    0.0, ALU.mult, ALU.add), "scan")
                V.wait(dve, e, "scan")
                V.done(nc.vector.tensor_copy(GSR[:, 0], T2[:, :, 63]), "mid")
                V.wait(dve, e, "mid")
                V.done(TT(GSR[:, 1], T2[:, :, 127], GSR[:, 0], ALU.subtract), "end")
                V.done(TT(T3[:, :], T2[:, :], GSR[:, 0].unsqueeze(2).to_broadcast([P, 4, P]), ALU.subtract), "d")
                V.wait(dve, e, "d")
                V.done(TT(T4[:, :], T3[:, :], T0[:, :], ALU.subtract), "dx")
            if level == 3:
                prep_act.wait(dve, e, "nrm")
                V.done(nc.vector.tensor_scalar(T6[:, :], T6[:, :], 1e-12, None, ALU.max), "max")
                V.wait(dve, e, "max")
                V.done(nc.vector.reciprocal(T6[:, :], T6[:, :]), "rcp")
                V.wait(dve, e, "rcp")
                V.done(TT(T5[:, :], T5[:, :], T6[:, :], ALU.mult), "kkn")
                V.wait(dve, e, "kkn")
                V.done(STT(AR[:, s, :, 0], T5[:, :], -1.0, T4[:, :], ALU.mult, ALU.mult), "a_dec")
            if level == 4:
                V.wait(dve, e, "a_dec")
                V.done(TT(T5[:, :], T5[:, :], T1[:, :], ALU.mult), "b0")
                V.wait(dve, e, "b0")
                V.done(TT(BK[:, s, 0], T5[:, :], T3[:, :], ALU.mult), "b_dec")
                V.done(STT(T1[:, :], T1[:, :], -1.0, vb(V_KA), ALU.add, ALU.mult), "ka")
                V.wait(dve, e, "ka")
                V.done(STT(T1[:, :], T1[:, :], 1.0, k, ALU.add, ALU.mult), "k2")
                V.wait(dve, e, "k2")
                V.done(TT(BK[:, s, 1], T1[:, :], T3[:, :], ALU.mult), "k_dec")
                V.done(TT(AR[:, s, :, 1], r, T2[:, :], ALU.mult), "r_dec")
                V.wait(dve, e, "k_dec")
                V.done(TT(T1[:, :], T1[:, :], r, ALU.mult), "rk")
                V.wait(dve, e, "rk")
                V.done(TT(T1[:, :], T1[:, :], vb(V_RK), ALU.mult), "rk2")
            if level == 5:
                prep_pe.wait(dve, e, "bon")
                prep_pool.wait(dve, e, "vc")
                V.done(TT(BON[:, s], bank(7), VC[:, s], ALU.mult), "bon")

        def out_pe_step(t, o, level):
            if level == 0:
                solve_act.wait(t, o, "o")
                out_pe.done(nc.tensor.matmul(bank(6), blk, part(o, 4), start=True, stop=True), "mean")
            if level == 1:
                out_act.wait(t, o, "sq")
                out_dve.wait(t, o, "d")
                out_pe.done(nc.tensor.matmul(bank(6), blk, part(o, 8), start=True, stop=True), "var")
            if level == 2:
                out_act.wait(t, o, "sd")
                for p in range(4):
                    m = nc.tensor.matmul(bank(6)[:, p], LOR[:, 1, p * P:(p + 1) * P], GL[:, bass.ds(o * P, P)],
                                         start=True, stop=True)
                out_pe.done(m, "gate")

        def out_act_step(act, o, level):
            if level == 0:
                out_dve.wait(act, o, "d")
                waited(act, "act")
                out_act.done(nc.scalar.activation(part(o, 8), part(o, 4), ACT.Square), "sq")
            if level == 1:
                out_pe.wait(act, o, "var")
                waited(act, "act")
                out_act.done(nc.scalar.activation(part(o, 8), bank(6), ACT.Sqrt, bias=VT[:, 91:92],
                                                  scale=1.0 / RH), "sd")

        def out_dve_step(dve, o, s, level):
            O, TT = out_dve, nc.vector.tensor_tensor
            oo, vv = part(o, 4), part(o, 8)
            if level == 0:
                out_pe.wait(dve, o, "mean")
                O.done(nc.vector.scalar_tensor_tensor(oo, bank(6), -1.0 / RH, oo, ALU.mult, ALU.add), "d")
            if level == 2:
                out_act.wait(dve, o, "sd")
                waited(dve, "dve")
                O.done(nc.vector.reciprocal(vv, vv), "rcp")
                for step, a, op in (("m1", vv, ALU.mult), ("m2", vb(V_LW), ALU.mult), ("m3", vb(V_LB), ALU.add),
                                    ("m4", BON[:, s], ALU.add)):
                    O.wait(dve, o, O.steps[O.steps.index(step) - 1])
                    O.done(TT(oo, oo, a, op), step)
                O.wait(dve, o, "m4")
                out_pe.wait(dve, o, "gate")
                O.done(TT(part(o, 0), oo, bank(6), ALU.mult), "yb")

        def chunk_pe(t, c, s, prep, outp):
            T, MM, TR = solve_pe, nc.tensor.matmul, nc.tensor.transpose
            prep_dve.wait(t, c, "bon")
            prep_pool.wait(t, c, "vc")
            for q in range(4):
                for p in range(4):
                    src = (AR[:, s, p, 0], BK[:, s, 0, p], BK[:, s, 1, p], VC[:, s, p])[q]
                    m = TR(bank(q)[:, p], src, ident)
                T.done(m, f"tok{q}")
            for b in two:
                for q in two:
                    if b == 0 and q == 0:
                        if not (isinstance(c, int) and c == 0):
                            solve_dve.wait(t, c - 1, "s1")
                        first = 4
                    elif b == 0:
                        solve_act.wait(t, c, "tok1")
                        first = 0
                    elif q == 0:
                        solve_act.wait(t, c, "tok3")
                        first = 2
                    else:
                        solve_dve.wait(t, c, "m0")
                        first = 4
                    for j in range(4):
                        h = 4 * b + j
                        lo = RH * (h % 2)
                        m = MM(PS[:, first + j % 2, 256 * (j // 2):256 * (j // 2) + 256].rearrange(
                                   "p (a m) -> p a m", m=P),
                               BK[lo:lo + RH, s, q, h // 2], AR[lo:lo + RH, s, h // 2], start=True, stop=True)
                    T.done(m, f"p{q + 1}_{b}")
            solve_dve.wait(t, c, "n1")
            for h in range(8):
                m = MM(PS[:, 2, RH * h:RH * h + RH], NTRK[:, h, 0], TOK[:, 3, RH * h:RH * h + RH],
                       start=True, stop=True)
            T.done(m, "nv")
            for b in two:
                solve_pool.wait(t, c, f"tt_{b}")
                for j in range(4):
                    m = TR(bank(3 * b)[:, j], TIT[:, 4 * b + j], ident)
                T.done(m, f"t0_{b}")
            for k in range(LEVELS):
                if outp:
                    out_pe_step(t, c - 1, k)
                if prep:
                    prep_pe_step(t, c + 1, 1 - s, k)
                for b in two:
                    solve_pool.wait(t, c, f"x{k}_{b}")
                    if k == 0:
                        solve_act.wait(t, c, f"t0_{b}")
                    else:
                        solve_dve.wait(t, c, f"t{k - 1}_{b}")
                    for j in range(4):
                        m = MM(bank(3 * b)[:, j], XL[:, 4 * b + j], TI[:, 4 * b + j], start=True, stop=True)
                    T.done(m, f"y{k}_{b}")
                for b in two:
                    solve_act.wait(t, c, f"y{k}_{b}")
                    if k == 0 and b == 0:
                        solve_act.wait(t, c, "nv")
                    if k > 0:
                        solve_dve.wait(t, c, f"tt{k - 1}_{b}")
                    if k < LEVELS - 1:
                        for j in range(4):
                            m = MM(bank(3 * b + 1)[:, j], TIT[:, 4 * b + j], YL[:, 4 * b + j],
                                   start=True, stop=True)
                        T.done(m, f"dt{k}_{b}")
                    for j in range(4):
                        m = MM(bank(3 * b + 2)[:, j], YL[:, 4 * b + j], TIT[:, 4 * b + j], start=True, stop=True)
                    T.done(m, f"dtt{k}_{b}")
            for b in two:
                solve_dve.wait(t, c, f"tt{LEVELS - 1}_{b}")
            for h in range(8):
                lo = RH * (h % 2)
                m = MM(PS[lo:lo + RH, 0, P * (h // 2):P * (h // 2) + P], TOK[:, 0, RH * h:RH * h + RH], TIT[:, h],
                       start=True, stop=True)
            T.done(m, "wt")
            for h in range(8):
                m = MM(PS[:, 1, RH * h:RH * h + RH], TIT[:, h], NV[:, RH * h:RH * h + RH], start=True, stop=True)
            T.done(m, "z")
            solve_act.wait(t, c, "wt")
            solve_dve.wait(t, c, "s_in")
            for p in range(4):
                m = MM(bank(3)[:, p], WT[:, p], SP_[:, p], start=True, stop=True)
            T.done(m, "u")
            if outp:
                out_dve.wait(t, c - 1, "yb")
            for p in range(4):
                MM(bank(4)[:, p], TOK[:, 2, P * p:P * p + P], TOK[:, 3, P * p:P * p + P], start=(p == 0),
                   stop=False, skip_group_check=True)
            for p in range(4):
                MM(bank(6)[:, p], SP_[:, p], AR[:, s, p, 1], start=(p == 0), stop=False, skip_group_check=True)
            for h in range(8):
                lo = RH * (h % 2)
                MM(PS[lo:lo + RH, 6, P * (h // 2):P * (h // 2) + P], TOK[:, 3, RH * h:RH * h + RH],
                   NTRK[:, h, 1], start=False, stop=False, skip_group_check=True)
            solve_dve.wait(t, c, "u")
            for p in range(4):
                m = MM(bank(4)[:, p], TOK[:, 1, P * p:P * p + P], UU[:, P * p:P * p + P], start=False, stop=True,
                       skip_group_check=True)
            T.done(m, "s")
            for h in range(8):
                lo = RH * (h % 2)
                m = MM(PS[lo:lo + RH, 6, P * (h // 2):P * (h // 2) + P], UU[:, RH * h:RH * h + RH],
                       MTRB[:, h, 1], start=False, stop=True, skip_group_check=True)
            T.done(m, "o")

        def chunk_act(act, c, s, prep, outp):
            T = solve_act
            for q in range(4):
                solve_pe.wait(act, c, f"tok{q}")
                T.done(nc.scalar.copy(TOK[:, q], PS[:, q]), f"tok{q}")
            solve_pe.wait(act, c, "nv")
            T.done(nc.scalar.copy(NV[:, :], PS[:, 2]), "nv")
            for b in two:
                solve_pe.wait(act, c, f"t0_{b}")
                T.done(nc.scalar.copy(heads(TI, b), bank(3 * b)), f"t0_{b}")
            for k in range(LEVELS):
                for b in two:
                    solve_pe.wait(act, c, f"y{k}_{b}")
                    T.done(nc.scalar.copy(heads(YL, b), bank(3 * b)), f"y{k}_{b}")
                if outp:
                    out_act_step(act, c - 1, k)
                if prep:
                    prep_act_step(act, c + 1, 1 - s, k)
            solve_pe.wait(act, c, "wt")
            T.done(nc.scalar.copy(WT[:, :], bank(0)), "wt")
            solve_pe.wait(act, c, "z")
            T.done(nc.scalar.copy(ZZ[:, :], PS[:, 1]), "z")
            solve_pe.wait(act, c, "o")
            waited(act, "act")
            T.done(nc.scalar.copy(part(c, 4), bank(6)), "o")

        def chunk_dve(dve, c, s, prep, outp):
            T, TT = solve_dve, nc.vector.tensor_tensor
            mask = CON[:, C_MU:C_MU + 2 * P].rearrange("p (a m) -> p a m", m=P)
            if not (isinstance(c, int) and c == 0):
                solve_pe.wait(dve, c - 1, "o")
            for b in two:
                for q, dst in ((0, MTRB), (1, NTRK)):
                    solve_pe.wait(dve, c, f"p{q + 1}_{b}")
                    first = {(0, 0): 4, (0, 1): 0, (1, 0): 2, (1, 1): 4}[b, q]
                    for par in two:
                        m = TT(dst[:, 4 * b + par:4 * b + 4:2].rearrange("p h a m -> p h (a m)"),
                               PS[:, first + par].rearrange("p (h m) -> p h m", h=2),
                               over(CON[:, C_MU:C_MU + 2 * P], 2), ALU.mult)
                    T.done(m, f"{'mn'[q]}{b}")
            prep_pool.wait(dve, c, "g1m")
            if isinstance(c, int) and c == 0:
                dve.wait_ge(state_zero, 1)
            else:
                T.wait(dve, c - 1, "s")
            T.done(TT(SP_[:, :], SS[:, :], G1M[:, s], ALU.mult), "s_in")
            for k in range(LEVELS):
                for b in two:
                    if k < LEVELS - 1:
                        solve_pe.wait(dve, c, f"dt{k}_{b}")
                        T.done(TT(heads(TI, b), heads(TI, b), bank(3 * b + 1), ALU.add), f"t{k}_{b}")
                    solve_pe.wait(dve, c, f"dtt{k}_{b}")
                    T.done(TT(heads(TIT, b), heads(TIT, b), bank(3 * b + 2), ALU.add), f"tt{k}_{b}")
                if outp:
                    out_dve_step(dve, c - 1, 1 - s, k)
                if prep:
                    prep_dve_step(dve, c + 1, 1 - s, k)
            solve_pe.wait(dve, c, "u")
            solve_act.wait(dve, c, "z")
            T.done(TT(UU[:, :], PS[:, 3], ZZ[:, :], ALU.add), "u")
            solve_pe.wait(dve, c, "s")
            T.done(TT(SS[:, :], bank(4), SP_[:, :], ALU.add), "s1")
            T.wait(dve, c, "s1")
            T.done(TT(SS[:, :], SS[:, :], GS[:, s, 1].unsqueeze(2).to_broadcast([P, 4, P]), ALU.mult), "s")

        def chunk_pool(pool, c, s, prep, outp):
            T, TT = solve_pool, nc.gpsimd.tensor_tensor
            if not (isinstance(c, int) and c == 0):
                solve_pe.wait(pool, c - 1, "o")
            for b in two:
                solve_dve.wait(pool, c, f"m{b}")
                mt = MTRB[:, 4 * b:4 * b + 4, 0]
                T.done(TT(heads(TIT, b), mt, over(CON[:, C_M0:C_M0 + P], 4), ALU.mult), f"i{b}")
                T.wait(pool, c, f"i{b}")
                T.done(TT(heads(TIT, b), heads(TIT, b), over(ident, 4), ALU.add), f"tt_{b}")
                T.done(TT(heads(XL, b), mt, over(CON[:, C_MX:C_MX + P], 4), ALU.mult), f"x0_{b}")
            for k in range(LEVELS):
                if k > 0:
                    for b in two:
                        solve_pe.wait(pool, c, f"y{k - 1}_{b}")
                        T.done(TT(heads(XL, b), MTRB[:, 4 * b:4 * b + 4, 0],
                                  over(CON[:, C_MX + k * P:C_MX + (k + 1) * P], 4), ALU.mult), f"x{k}_{b}")
                if prep:
                    prep_pool_step(pool, c + 1, 1 - s, k)

        def recurrence(engine, chunk, prep_step, out_step):
            for level in range(LEVELS):
                prep_step(engine, 0, 0, level)
            chunk(engine, 0, 0, True, False)
            with engine.Fori(0, (NT - 2) // 2) as i:
                for j in two:
                    chunk(engine, 2 * i + (1 + j), 1 - j, True, True)
            chunk(engine, NT - 1, 1, False, True)
            for level in range(LEVELS):
                out_step(engine, NT - 1, level)

        OUT_ORDER = [4, 5, 6, 7, 0, 1, 2, 3]
        ya_back = sem("ya_back")

        def mixed_split(eng, act):
            for n, k in enumerate(OUT_ORDER):
                src = RKV[:, k - 4] if k >= 4 else RKV[:, k + 4]
                if n == 4:
                    eng.wait_ge(ya_back, 16)
                if act:
                    if n == 0:
                        out_dve.wait(eng, NT - 1, "yb")
                    nc.scalar.copy(Hh[:, k], src).then_inc(h_hi, 1)
                else:
                    h_lo_split(eng, 1, k, src, pos=n)

        qk_copy, qk_sq, qk_ms, qk_sd, qk_rc, qk_norm = (sem("qk_copied"), sem("qk_squared"), sem("qk_mean_square"),
                                                        sem("qk_sqrt"), sem("qk_reciprocal"), sem("qk_normed"))
        k2_in, v_tr, v_tok = sem("k2_in"), sem("v_transposed"), sem("v_token_major")
        SQB = (SQ[:, 0:S], ST2[:, 0:S])
        STB = (ST0[:, 0:S], ST1[:, 0:S])

        def qkv_pe(t):
            u0, a0_ = STAGE["qkv"]

            def unit(j, slot, half, ready=None):
                product(t, slot, slot, a0_ // 2 + half, u0 + j, 8, P, 0, Hh, Hl, ready=ready)

            def mean_square(j, slot):
                t.wait_ge(qk_sq, j + 1)
                if not (isinstance(j, int) and j == 0):
                    t.wait_ge(qk_sd, j)
                for half in range(2):
                    m = nc.tensor.matmul(PS[:, 4 + half], blk, SQB[slot][:, half * HALF:(half + 1) * HALF],
                                         start=True, stop=True)
                m.then_inc(qk_ms, 1)

            unit(0, 0, 0, ready=(h_lo, 8 * H_FILL["qkv"]))
            unit(1, 1, 0)
            mean_square(0, 0)
            with t.Fori(0, 4) as i:
                unit(2 * i + 2, 0, i + 1)
                mean_square(2 * i + 1, 1)
                unit(2 * i + 3, 1, i + 1)
                mean_square(2 * i + 2, 0)

        def qkv_act(act):
            u0, a0_ = STAGE["qkv"]

            def step(j, slot, i):
                split_hi(act, 1 - slot, u0 // 2 + i + slot, a0_ + j + 2)
                act.wait_ge(acc_done, a0_ + j + 3)
                act.wait_ge(qk_norm, j + 1)
                nc.scalar.copy(STB[slot], acc2(slot)).then_inc(acc_free[slot], 1)
                act.wait_ge(acc_free[slot], a0_ // 2 + i + 2)
                nc.scalar.activation(SQB[slot], STB[slot], ACT.Square).then_inc(qk_sq, 1)

            def root(j, slot):
                act.wait_ge(qk_ms, j + 1)
                nc.scalar.activation(SQB[slot], PS[:, 4:6].rearrange("p b n -> p (b n)"), ACT.Sqrt,
                                     bias=VT[:, 90:91], scale=1.0 / RH).then_inc(qk_sd, 1)

            step(0, 0, 0)
            step(1, 1, 0)
            root(0, 0)
            with act.Fori(0, 3) as i:
                step(2 * i + 2, 0, i + 1)
                root(2 * i + 1, 1)
                step(2 * i + 3, 1, i + 1)
                root(2 * i + 2, 0)
            step(8, 0, 4)
            root(7, 1)
            split_hi(act, 0, u0 // 2 + 5, a0_ + 11)
            act.wait_ge(acc_done, a0_ + 12)
            nc.scalar.copy(VP[:, RH:RH + S], acc2(1)).then_inc(acc_free[1], 1)
            root(8, 0)

        def qkv_dve(dve):
            u0, a0_ = STAGE["qkv"]

            def step(j, slot):
                split_lo(dve, 1 - slot, u0 + j + 1)

            def norm(j, slot, dst, gain):
                dve.wait_ge(qk_sd, j + 1)
                nc.vector.reciprocal(SQB[slot], SQB[slot]).then_inc(qk_rc, 1)
                dve.wait_ge(qk_rc, j + 1)
                nc.vector.scalar_tensor_tensor(dst, STB[slot], VT[:, gain:gain + 1], SQB[slot], ALU.mult,
                                               ALU.mult).then_inc(qk_norm, 1)

            def q(n):
                return Q[:, bass.ds(n, 1), :].rearrange("p a n -> p (a n)")

            step(0, 0)
            step(1, 1)
            norm(0, 0, Q[:, 0], V_QS)
            with dve.Fori(0, 3) as i:
                step(2 * i + 2, 0)
                norm(2 * i + 1, 1, q(2 * i + 1), V_QS)
                step(2 * i + 3, 1)
                norm(2 * i + 2, 0, q(2 * i + 2), V_QS)
            step(8, 0)
            norm(7, 1, Q[:, 7], V_QS)
            step(9, 1)
            dve.wait_ge(qk_sd, 9)
            nc.vector.reciprocal(SQB[0], SQB[0]).then_inc(qk_rc, 1)
            dve.wait_ge(qk_rc, 9)
            dve.wait_ge(pads_zero, 3)
            for kv in two:
                rows = slice(RH * kv, RH * kv + RH)
                m = nc.vector.scalar_tensor_tensor(K2[rows, kv, kv, RH:RH + S], STB[0][rows], VT[rows, V_KG:V_KG + 1],
                                                   SQB[0][rows], ALU.mult, ALU.mult)
            m.then_inc(qk_norm, 1)

        q_pool = Track("q_tile_copied", ["q"])
        v_pool = Track("v_tile_copied", ["v"])
        p_pool = Track("probs_pool", ["p1", "p3"])
        sc_pe = Track("score_pe", [f"sc{g}" for g in range(4)])
        pv_pe = Track("value_pe", [f"t{w}{g}" for g in range(4) for w in "ab"] + ["pv"])
        sc_dve = Track("score_dve", [f"{w}{g}" for g in range(4) for w in ("b", "max", "neg")] + ["sink"])
        pv_dve = Track("value_dve", ["den", "rcp", "p0", "e0", "e1", "p2", "e2", "e3"])
        sc_act = Track("score_act", [f"e{g}" for g in range(4)] + ["sink"])
        pv_act = Track("value_act", [f"e{g}" for g in range(4)] + ["o0", "o1"])
        ptb_zero, nsnk_ok = sem("probs_rest_zero"), sem("minus_sinks_ready")
        slopes = [2.0 ** (-8.0 * (h + 1) / NQ) for h in range(NQ)]

        def at_start(tile, n):
            return isinstance(tile, int) and tile < n

        def score_banks(g):
            return PS[:, 2 * (g % 2):2 * (g % 2) + 2, 0:2 * WIN]

        def q_tile(pool, tile, s):
            if not at_start(tile, 2):
                sc_pe.wait(pool, tile - 2, "sc3")
                waited(pool, "pool")
            q_pool.done(nc.gpsimd.tensor_copy(QST[:, s], Q[:, :, bass.ds(tile * P, P)]), "q")

        def v_tile(pool, tile, s):
            if not at_start(tile, 2):
                pv_pe.wait(pool, tile - 2, "pv")
                waited(pool, "pool")
            v_pool.done(nc.gpsimd.tensor_copy(VST[:, s], VTOK[:, bass.ds(tile, 2), :]), "v")

        def score_products(t, tile, s, g):
            if g == 0:
                q_pool.wait(t, tile, "q")
            if g >= 2:
                sc_dve.wait(t, tile, f"b{g - 2}")
            elif not at_start(tile, 1):
                sc_dve.wait(t, tile - 1, f"b{g + 2}")
            for j in two:
                m = nc.tensor.matmul(score_banks(g)[:, j].rearrange("p (a m) -> p a m", a=2), QST[:, s, 2 * g + j],
                                     K2[:, g // 2, :, bass.ds(tile * P, WIN)], start=True, stop=True)
            sc_pe.done(m, f"sc{g}")

        def probs_transposes(t, tile, s, g):
            if g % 2:
                p_pool.wait(t, tile, f"p{g}")
            else:
                pv_dve.wait(t, tile, f"p{g}")
            if g > 0:
                pv_act.wait(t, tile, f"e{g - 1}")
                pv_dve.wait(t, tile, f"e{g - 1}")
            for j in range(4):
                m = nc.tensor.transpose(bank(4)[:, j], PP[:, s, 4 * g + j, 0:P], ident)
            pv_pe.done(m, f"ta{g}")
            for j in range(4):
                m = nc.tensor.transpose(bank(5)[0:RH, j], PP[:, s, 4 * g + j, P:WIN], ident)
            pv_pe.done(m, f"tb{g}")

        def value_products(t, tile, s):
            pv_act.wait(t, tile, "e3")
            pv_dve.wait(t, tile, "e3")
            v_pool.wait(t, tile, "v")
            if at_start(tile, 1):
                t.wait_ge(ptb_zero, 1)
            else:
                pv_act.wait(t, tile - 1, "o1")
            for kv in range(NKV):
                for n, pt in enumerate((PTA, PTB)):
                    for par in two:
                        o = PS[RH * par:RH * par + RH, 6 + kv].rearrange("p (a m) -> p a m", m=P)
                        m = nc.tensor.matmul(o, VST[:, s, n, RH * kv:RH * kv + RH], pt[:, 8 * kv + par:8 * kv + 8:2],
                                             start=n == 0, stop=n == 1)
            pv_pe.done(m, "pv")

        def round_pe(t, new, old, s):
            for g in range(4):
                if new is not None and g < 3:
                    score_products(t, new, s, g + 1)
                if g == 3 and new is not None and not (isinstance(new, int) and new == NT - 1):
                    score_products(t, new + 1, 1 - s, 0)
                if old is not None:
                    probs_transposes(t, old, 1 - s, g)
            if old is not None:
                value_products(t, old, 1 - s)

        def round_dve(dve, new, old, s):
            o = 1 - s
            first = C_DIST + WIN if at_start(new, 1) else C_DIST
            dist = CON[:, first:first + WIN]
            for g in range(4):
                hs = slice(4 * g, 4 * g + 4)
                if new is not None:
                    sc_pe.wait(dve, new, f"sc{g}")
                    if not at_start(new, 2):
                        pv_pe.wait(dve, new - 2, f"tb{g}")
                    for j in range(4):
                        h = 4 * g + j
                        m = nc.vector.scalar_tensor_tensor(
                            PP[:, s, h], dist, -slopes[h],
                            score_banks(g)[:, j // 2, WIN * (j % 2):WIN * (j % 2) + WIN], ALU.mult, ALU.add)
                    sc_dve.done(m, f"b{g}")
                    sc_dve.wait(dve, new, f"b{g}")
                    sc_dve.done(nc.vector.tensor_reduce(STA[:, s, 0, hs], PP[:, s, hs], AXX, ALU.max), f"max{g}")
                    sc_dve.wait(dve, new, f"max{g}")
                    sc_dve.done(nc.vector.scalar_tensor_tensor(STA[:, s, 2, hs], STA[:, s, 0, hs], -1.0, NSNK[:, hs],
                                                               ALU.mult, ALU.min), f"neg{g}")
                if old is not None:
                    if g == 0:
                        sc_act.wait(dve, old, "sink")
                        pv_dve.done(nc.vector.tensor_tensor(STA[:, o, 4], STA[:, o, 4], STA[:, o, 5], ALU.add), "den")
                        pv_dve.wait(dve, old, "den")
                        pv_dve.done(nc.vector.reciprocal(STA[:, o, 4], STA[:, o, 4]), "rcp")
                        pv_dve.wait(dve, old, "rcp")
                    else:
                        rest_copy(dve, old, g - 1)
                    if g % 2 == 0:
                        pv_dve.done(nc.vector.tensor_tensor(
                            PP[:, o, hs], PP[:, o, hs], STA[:, o, 4, hs].unsqueeze(2).to_broadcast([P, 4, WIN]),
                            ALU.mult), f"p{g}")
            if new is not None:
                sc_dve.wait(dve, new, "neg3")
                sc_dve.done(nc.vector.tensor_tensor(STA[:, s, 3], SNK[:, :], STA[:, s, 2], ALU.add), "sink")
            if old is not None:
                rest_copy(dve, old, 3)

        def rest_copy(dve, tile, g):
            pv_pe.wait(dve, tile, f"tb{g}")
            if g == 0 and not at_start(tile, 1):
                pv_pe.wait(dve, tile - 1, "pv")
            pv_dve.done(nc.vector.tensor_copy(PTB[0:RH, 4 * g:4 * g + 4], bank(5)[0:RH]), f"e{g}")

        def round_act(act, new, old, s):
            for g in range(4):
                if new is not None:
                    sc_dve.wait(act, new, f"neg{g}")
                    for h in range(4 * g, 4 * g + 4):
                        m = nc.scalar.activation(PP[:, s, h], PP[:, s, h], ACT.Exp, bias=STA[:, s, 2, h:h + 1],
                                                 accum_out=STA[:, s, 4, h:h + 1])
                    sc_act.done(m, f"e{g}")
                    if g == 3:
                        sc_dve.wait(act, new, "sink")
                        sc_act.done(nc.scalar.activation(STA[:, s, 5], STA[:, s, 3], ACT.Exp), "sink")
                if old is not None:
                    pv_pe.wait(act, old, f"ta{g}")
                    pv_act.done(nc.scalar.copy(PTA[:, 4 * g:4 * g + 4], bank(4)), f"e{g}")
            if old is not None:
                pv_pe.wait(act, old, "pv")
                waited(act, "act")
                for kv in range(NKV):
                    pv_act.done(nc.scalar.copy(Q[:, 4 * kv:4 * kv + 4, bass.ds(old * P, P)], bank(6 + kv)), f"o{kv}")

        def round_pool(pool, new, old, s):
            o = 1 - s
            if new is not None and not (isinstance(new, int) and new == NT - 1):
                q_tile(pool, new + 1, o)
            if old is not None:
                pv_dve.wait(pool, old, "rcp")
                for g in (1, 3):
                    hs = slice(4 * g, 4 * g + 4)
                    p_pool.done(nc.gpsimd.tensor_tensor(
                        PP[:, o, hs], PP[:, o, hs], STA[:, o, 4, hs].unsqueeze(2).to_broadcast([P, 4, WIN]),
                        ALU.mult), f"p{g}")
            if new is not None:
                v_tile(pool, new, s)

        def attention(engine, one_round):
            one_round(engine, 0, None, 0)
            one_round(engine, 1, 0, 1)
            with engine.Fori(0, (NT - 4) // 2) as i:
                for j in two:
                    one_round(engine, 2 * i + (2 + j), 2 * i + (1 + j), j)
            one_round(engine, NT - 2, NT - 3, 0)
            one_round(engine, NT - 1, NT - 2, 1)
            one_round(engine, None, NT - 1, 0)

        def attn_split(eng, act):
            for k in range(KD):
                if act:
                    if k == 0:
                        pv_act.wait(eng, NT - 1, "o1")
                    nc.scalar.copy(Hh[:, k], Q[:, k]).then_inc(h_hi, 1)
                else:
                    h_lo_split(eng, 4, k, Q[:, k])

        out_tr, out_ev, out_st, out_dma = (sem("out_transposed"), sem("out_evacuated"), sem("out_staged"),
                                           [sem("out_dma0"), sem("out_dma1")])
        OT = at("out_tile", [2, KD, P], 64)

        @block.sync
        def _(sp):
            sp.dma_start(CON[:, :], consts).then_inc(const_in, 16)
            rows = [(V_MIX, norm_mix.rearrange("l (k p) -> (l k) p", p=P)),
                    (V_MLP, norm_mlp.rearrange("l (k p) -> (l k) p", p=P)),
                    (V_MU, shift_mu.rearrange("l (k p) -> (l k) p", p=P)),
                    (V_W0, w0.rearrange("l (k p) -> (l k) p", p=P)),
                    (V_A0, a0.rearrange("l (k p) -> (l k) p", p=P)),
                    (V_KK, k_k.rearrange("l (k p) -> (l k) p", p=P)),
                    (V_KA, k_a.rearrange("l (k p) -> (l k) p", p=P)),
                    (V_RK, r_k.rearrange("l (k h) n -> (l k) (h n)", h=2)),
                    (V_LW, lnx_w.rearrange("l (k p) -> (l k) p", p=P)),
                    (V_LB, lnx_b.rearrange("l (k p) -> (l k) p", p=P)),
                    (V_CW, conv_w.rearrange("l j (k p) -> (l j k) p", p=P))]
            for row, src in rows:
                sp.dma_start(VROW[row:row + src.shape[0], :], src).then_inc(const_in, 16)
            for half in two:
                sp.dma_start(VROW[V_QG:V_QG + 1, RH * half:RH * half + RH], q_gain).then_inc(const_in, 16)
                sp.dma_start(VROW[V_KG:V_KG + 1, RH * half:RH * half + RH], k_gain).then_inc(const_in, 16)
            sp.dma_start(LOR[0:RH, 0], w_decay2[0]).then_inc(const_in, 16)
            sp.dma_start(LOR[RH:P, 0], w_aaa2[0]).then_inc(const_in, 16)
            sp.dma_start(LOR[:, 1], w_gate2[0]).then_inc(const_in, 16)
            sp.dma_start(SNK[:, :], sinks.to_broadcast([P, NQ])).then_inc(const_in, 16)
            with sp.Fori(0, 2) as i:
                for q in range(2):
                    for r in range(3):
                        load_unit(sp, (3 * q + r) % 2, 6 * i + 3 * q + r,
                                  win[:, :, bass.ds(i * 256 + (512 * r + P * q), P)])
            with sp.Fori(0, 7) as i:
                for j in two:
                    load_unit(sp, j, 12 + 2 * i + j, win[:, :, bass.ds(i * 256 + (1536 + P * j), P)])
            load_stage(sp, "out", wout, 8)
            load_mlp(sp, 0)
            load_stage(sp, "qkv", wqkv, 10)
            load_stage(sp, "wo", wo, 8)
            load_mlp(sp, 1)
            oo = out[0].rearrange("(t p) (k n) -> t p k n", p=P, n=P)
            for j in two:
                sp.sem_inc(out_dma[j], 16)
            with sp.Fori(0, NT // 2) as i:
                for j in two:
                    sp.wait_ge(out_ev, 2 * i + j + 3)
                    sp.dma_start(oo[bass.ds(2 * i + j, 1)].rearrange("a p k n -> p (a k) n"), OT[:, j])\
                        .then_inc(out_dma[j], 16)
            for j in two:
                sp.wait_ge(out_dma[j], 16 * (NT // 2 + 1))


        @block.gpsimd
        def _(pool):
            pool.sem_inc(gl_free, 1)
            nc.gpsimd.memset(VT[:, 90:91], EPS).then_inc(eps_set, 1)
            nc.gpsimd.memset(VT[:, 91:92], LNX_EPS).then_inc(eps_set, 1)
            xin = x[0].rearrange("(t p) (k n) -> t p k n", p=P, n=P)
            with pool.Fori(0, NT // 2) as i:
                for j in two:
                    pool.wait_ge(x_tr, 2 * i + j + 1)
                    waited(pool, "pool")
                    pool.dma_start(XT8[:, j], xin[bass.ds(2 * i + j, 1)].rearrange("a p k n -> p (a k) n"))\
                        .then_inc(x_in[j], 16)
            for g in range(4):
                pool.wait_ge(conv_done, g + 2)
                pool.dma_start(ya_dram[g], GL[:, :]).then_inc(ya_out, 16)
                pool.wait_ge(ya_out, 16 * g + 16)
                pool.sem_inc(gl_free, 1)
            pool.wait_ge(lora_act, 2)
            nc.gpsimd.memset(SS[:, :], 0.0).then_inc(state_zero, 1)
            recurrence(pool, chunk_pool, prep_pool_step, lambda *a: None)
            out_dve.wait(pool, NT - 1, "yb")
            pool.dma_start(RKV[:, 4:8], ya_dram.rearrange("g p n -> p g n")).then_inc(ya_back, 16)
            residual_done(pool, "qkv")
            nc.gpsimd.memset(K2[:, :, :, :], 0.0).then_inc(pads_zero, 1)
            nc.gpsimd.memset(VP[:, 0:RH], 0.0).then_inc(pads_zero, 1)
            nc.gpsimd.memset(VP[:, RH + S:], 0.0).then_inc(pads_zero, 1)
            pool.wait_ge(qk_norm, 2 + 9)
            for kv in two:
                here, there = slice(RH * kv, RH * kv + RH), slice(RH * (1 - kv), RH * (1 - kv) + RH)
                pool.dma_start(K2[there, kv, 1 - kv, RH:RH + S], K2[here, kv, kv, RH:RH + S]).then_inc(k2_in, 16)
            pool.wait_ge(v_tok, 3)
            q_tile(pool, 0, 0)
            q_pool.wait(pool, 0, "q")
            nc.gpsimd.memset(PTB[RH:P], 0.0).then_inc(ptb_zero, 1)
            pool.wait_ge(ptb_zero, 1)
            attention(pool, round_pool)

        @block.scalar
        def _(act):
            act.wait_ge(eps_set, 2)
            norm_act(act, "in")
            in_act(act)
            recurrence(act, chunk_act, prep_act_step, lambda e, o, l: out_act_step(e, o, l))
            mixed_split(act, True)
            split_hi(act, 0, 13, 28)
            residual_act(act, "out", 8)
            norm_act(act, "mlp0")
            with act.Fori(0, NG) as g:
                mlp_act(act, 0, g)
            norm_act(act, "qkv")
            qkv_act(act)
            attention(act, round_act)
            attn_split(act, True)
            residual_act(act, "wo", 8)
            norm_act(act, "mlp1")
            with act.Fori(0, NG - 1) as g:
                mlp_act(act, 1, g)
            mlp_act(act, 1, NG - 1, last=True)
            residual_done(act, "end")
            with act.Fori(0, NT // 2) as i:
                for j in two:
                    act.wait_ge(out_tr, 2 * i + j + 1)
                    waited(act, "act")
                    nc.scalar.copy(XT8[:, j], X[:, :, bass.ds(i * 256 + j * P, P)]).then_inc(out_st, 1)

        @block.tensor
        def _(t):
            t.sem_inc(acc_done, 2)
            t.sem_inc(x_tr, 2)
            t.sem_inc(out_tr, 2)
            t.wait_ge(const_in, 16 * N_CONST)
            nc.tensor.transpose(PS[:, 7, 0:V_ROWS], VROW[0:V_ROWS, :], ident[0:V_ROWS, 0:V_ROWS]).then_inc(vec_t, 1)
            with t.Fori(0, NT // 2) as i:
                for j in two:
                    t.wait_ge(x_in[j], 16 * i + 16)
                    t.wait_ge(x_ev, 2 * i + j + 1)
                    for k in range(KD):
                        m = nc.tensor.transpose(bank(2 * j + k // 4)[:, k % 4], XT8[:, j, k], ident)
                    m.then_inc(x_tr, 1)
            norm_pe(t, "in")
            with t.Fori(0, 13) as i:
                for j in two:
                    product(t, j, j, i, 2 * i + j, 8, P, 0, Hh, Hl,
                            ready=(h_lo, 0) if j == 0 else None)
            recurrence(t, chunk_pe, prep_pe_step, lambda e, o, l: out_pe_step(e, o, l))
            dense_pe(t, "out", 8, order=OUT_ORDER)
            norm_pe(t, "mlp0")
            mlp_pe(t, 0)
            norm_pe(t, "qkv")
            qkv_pe(t)
            t.wait_ge(acc_free[1], STAGE["wo"][1] // 2 + 1)
            t.wait_ge(pads_zero, 3)
            for n in range(9):
                if n == 8:
                    t.wait_ge(v_tok, 1)
                m = nc.tensor.transpose(bank(6 + n // 4 % 2)[:, n % 4], VP[:, P * n:P * n + P], ident)
                m.then_inc(v_tr, 1)
            t.wait_ge(k2_in, 32)
            score_products(t, 0, 0, 0)
            attention(t, round_pe)
            dense_pe(t, "wo", 8)
            norm_pe(t, "mlp1")
            mlp_pe(t, 1)
            with t.Fori(0, NT // 2) as i:
                for j in two:
                    t.wait_ge(out_st, 2 * i + j + 1)
                    t.wait_ge(out_ev, 2 * i + j + 1)
                    for k in range(KD):
                        m = nc.tensor.transpose(bank(2 * j + k // 4)[:, k % 4], XT8[:, j, k], ident)
                    m.then_inc(out_tr, 1)

        @block.vector
        def _(dve):
            dve.sem_inc(w_lo, 2)
            for j in two:
                dve.sem_inc(acc_free[j], 1)
            dve.sem_inc(x_ev, 2)
            dve.sem_inc(out_ev, 2)
            dve.sem_inc(conv_done, 1)
            dve.sem_inc(shift_done, 2)
            dve.sem_inc(act_lo, 1)
            dve.sem_inc(qk_norm, 2)
            dve.wait_ge(vec_t, 1)
            nc.vector.tensor_copy(VT[:, 0:V_ROWS], PS[:, 7, 0:V_ROWS]).then_inc(vec_ok, 1)
            dve.wait_ge(vec_ok, 1)
            nc.vector.tensor_scalar(VT[:, V_QS:V_QS + 1], VT[:, V_QG:V_QG + 1], float(RH) ** -0.5, None,
                                    ALU.mult).then_inc(vec_ok, 1)
            dve.wait_ge(vec_ok, 2)
            with dve.Fori(0, NT // 2) as i:
                for j in two:
                    dve.wait_ge(x_tr, 2 * i + j + 3)
                    waited(dve, "dve")
                    for q in two:
                        m = nc.vector.tensor_copy(X[:, 4 * q:4 * q + 4, bass.ds(i * 256 + j * P, P)],
                                                  bank(2 * j + q))
                    m.then_inc(x_ev, 1)
            norm_dve(dve, "in", V_MIX)
            in_dve(dve)
            recurrence(dve, chunk_dve, prep_dve_step, lambda e, o, l: out_dve_step(e, o, 1, l))
            mixed_split(dve, False)
            split_lo(dve, 0, 26)
            residual_dve(dve, "out", 8)
            norm_dve(dve, "mlp0", V_MLP)
            with dve.Fori(0, NG) as g:
                mlp_dve(dve, 0, g)
            norm_dve(dve, "qkv", V_MIX + KD)
            qkv_dve(dve)
            nc.vector.tensor_scalar(NSNK[:, :], SNK[:, :], -1.0, None, ALU.mult).then_inc(nsnk_ok, 1)
            dve.wait_ge(nsnk_ok, 1)
            for n in (0, 1, 2):
                dve.wait_ge(v_tr, (4, 8, 9)[n])
                rows = 4 if n < 2 else 1
                nc.vector.tensor_copy(VTOK[:, 4 * n:4 * n + rows], bank(6 + n % 2)[:, 0:rows]).then_inc(v_tok, 1)
            attention(dve, round_dve)
            attn_split(dve, False)
            residual_dve(dve, "wo", 8)
            norm_dve(dve, "mlp1", V_MLP + KD)
            with dve.Fori(0, NG - 1) as g:
                mlp_dve(dve, 1, g)
            mlp_dve(dve, 1, NG - 1, last=True)
            with dve.Fori(0, NT // 2) as i:
                for j in two:
                    dve.wait_ge(out_tr, 2 * i + j + 3)
                    dve.wait_ge(out_dma[j], 16 * i + 16)
                    for q in two:
                        m = nc.vector.tensor_copy(OT[:, j, 4 * q:4 * q + 4], bank(2 * j + q))
                    m.then_inc(out_ev, 1)


_INS = ["x", "norm_mix", "norm_mlp", "mlp_up", "mlp_down", "w_in_ab", "conv_w", "shift_mu", "w0", "w_decay2",
        "a0", "w_aaa2", "w_gate2", "k_k", "k_a", "r_k", "lnx_w", "lnx_b", "w_out_ab", "w_qkv", "q_gain",
        "k_gain", "sinks", "w_o"]


def kernel(**inputs):
    import concourse.bacc as bacc
    from concourse.bass_utils import run_bass_kernel_spmd

    nc = bacc.Bacc("TRN2", target_bir_lowering=False, num_devices=1)
    arrays, args = {}, {}
    for name in _INS + ["consts"]:
        a = shape_constants() if name == "consts" else np.ascontiguousarray(inputs[name])
        arrays[f"in_{name}"] = a
        args[name] = nc.dram_tensor(f"in_{name}", a.shape, mybir.dt.from_np(a.dtype), kind="ExternalInput").ap()
    args["out"] = nc.dram_tensor("out_0", (1, S, D), F32, kind="ExternalOutput").ap()
    hybrid_trunk(nc, **args)
    r = run_bass_kernel_spmd(nc, [arrays], core_ids=[0])
    return r.results[0]["out_0"]
```

```python
from contextlib import ExitStack

import numpy as np

import concourse.bass as bass
from concourse import mybir
from concourse.alu_op_type import AluOpType as ALU

ACT = mybir.ActivationFunctionType
AXX = mybir.AxisListType.X
F32 = mybir.dt.float32
F32R = mybir.dt.float32r

P = 128
D = 1024
S = 1024
KD = D // P
HALF = 512
NT = S // P
RH = 64
NP_ = 4
KAPPA = 0.6065306597126334
EPS = 1e-6
LNX_EPS = 64e-5
LEVELS = 6
NQ, NKV = 16, 2
WIN = 192
GF = 4
NG = 4096 // P // GF

C_ID, C_BLK, C_ONE, C_MU, C_MX, C_M0, C_RST, C_DIST = 0, 128, 256, 384, 640, 1408, 1536, 2048
C_END = C_DIST + 2 * WIN

V_MIX, V_MLP, V_MU, V_W0, V_A0, V_KK, V_KA, V_RK, V_LW, V_LB, V_CW, V_QG, V_KG = (
    0, 16, 32, 46, 50, 54, 58, 62, 66, 70, 74, 86, 87)
V_ROWS = 88
V_QS = 88

STAGE = {"in": (0, 0), "out": (26, 26), "mlp0": (34, 34), "qkv": (98, 130), "wo": (108, 140),
         "mlp1": (116, 148)}
A_END = 148 + 96
N_EARLY = 16
N_LATE = 5
H_FILL = {"in": 0, "out": 1, "mlp0": 2, "qkv": 3, "wo": 4, "mlp1": 5}


def shape_constants():
    c = np.zeros((P, C_END), np.float32)
    i = np.arange(P)
    row, col = i[:, None], i[None, :]
    c[:, C_ID:C_ID + P] = row == col
    c[:, C_BLK:C_BLK + P] = row // RH == col // RH
    c[:, C_ONE:C_ONE + P] = 1.0
    c[:, C_MU:C_MU + P] = row < col
    c[:, C_MU + P:C_MU + 2 * P] = row <= col
    for k in range(LEVELS):
        b = 2 << k
        c[:, C_MX + k * P:C_MX + (k + 1) * P] = (
            (row // (2 * b) == col // (2 * b)) & (row % (2 * b) < b) & (col % (2 * b) >= b))
    c[:, C_M0:C_M0 + P] = (row % 2 == 0) & (col == row + 1)
    c[:, C_RST:C_RST + 4 * P] = (np.arange(4 * P) % P != 0)[None, :]
    key = np.arange(WIN)[None, :]
    dist = np.abs(row - key + RH).astype(np.float32)
    seen = (key // RH == row // RH) | (key // RH == row // RH + 1)
    c[:, C_DIST:C_DIST + WIN] = np.where(seen, dist, np.float32(1e34))
    first = seen & (key >= RH)
    c[:, C_DIST + WIN:C_END] = np.where(first, dist, np.float32(1e34))
    return c


def hybrid_trunk(nc, x, norm_mix, norm_mlp, mlp_up, mlp_down, w_in_ab, conv_w, shift_mu, w0,
                 w_decay2, a0, w_aaa2, w_gate2, k_k, k_a, r_k, lnx_w, lnx_b, w_out_ab, w_qkv,
                 q_gain, k_gain, sinks, w_o, consts, out):
    ya_dram = nc.dram_tensor("ya_spill", (4, P, S), F32).ap()
    base = 16512

    def at(name, shape, kb, dt=F32):
        return nc.alloc_sbuf_tensor_at(name, [P] + shape, dt, offset=base + int(kb * 1024))

    X = at("residual", [KD, S], 0)
    Hh = at("h_hi", [KD, S], 32, F32R)
    Hl = at("h_lo", [KD, S], 64, F32R)
    WR = at("w_raw", [2, 1024], 96)
    WH = at("w_hi", [2, 1024], 104, F32R)
    WL = at("w_lo", [2, 1024], 112, F32R)
    ACh = at("mlp_hi", [GF, S], 120, F32R)
    ACl = at("mlp_lo", [GF, S], 136, F32R)
    RKV = at("rkv", [12, S], 120)
    WA = at("decay_aaa_in", [S], 168)
    GL = at("gate_in", [S], 172)
    ST0 = at("stage0", [S + 4], 176)
    ST1 = at("stage1", [S + 4], 180.25)
    ST2 = at("stage2", [S + 4], 184.5)
    CON = at("constants", [C_END], 189)
    LOR = at("lora_w", [2, 4 * P], 198.5)
    VT = at("vectors", [96], 202.5)
    SNK = at("sink_cols", [NQ], 203)
    NSNK = at("minus_sinks", [NQ], 203.0625)
    T6 = at("prep_t6", [4, P], 203.25)
    GS = at("decay_ends", [2, 2, 4], 205.25)
    GSR = at("decay_ends_raw", [2, 4], 205.375)
    T7 = at("prep_t7", [4, P], 205.5)
    RI = at("rms_inverse", [S], 203.25)
    SSQ = at("sum_squares", [NT], 188.625)
    RIV = at("rms_inverse_tokens", [2 * NT], 188.6875)
    XIN = at("x_in_tile", [4, KD, P], 120)
    XT8 = at("x_tile", [2, KD, P], 32)
    VROW = at("vector_rows", [P], 136)
    AR = at("a_r_dec", [2, 4, 2, P], 32)
    ARP = at("a_r_zero_padded", [4, 2, 2, P], 96)
    BK = at("b_k_dec", [2, 2, 4, P], 40)
    VC = at("v_chunk", [2, 4, P], 48)
    BON = at("bonus", [2, 4, P], 52)
    G1M = at("decay_in_mask", [2, 4, P], 56)
    TOK = at("token_major", [4, 4 * P], 60)
    MTRB = at("mt_rb", [8, 2, P], 68)
    NTRK = at("nt_rk", [8, 2, P], 76)
    TI = at("tri_inv", [8, P], 84)
    TIT = at("tri_inv_t", [8, P], 88)
    WT = at("w_t", [4, P], 92)
    ZZ = at("z_part", [4 * P], 94)
    YL = at("y_level", [8, P], 176)
    XL = at("x_level", [8, P], 180)
    SS = at("state", [4, P], 184)
    SP_ = at("state_in", [4, P], 186)
    NV = at("nv_part", [4 * P], 104)
    UU = at("u_part", [4 * P], 106)
    T0, T1, T2, T3, T4 = (at(f"prep_t{n}", [4, P], 108 + 2 * n) for n in range(5))
    T5 = at("prep_t5", [4, P], 118)
    WAG = at("lora_chunk", [P], 188)
    Q = at("q_then_o", [KD, S], 120)
    K2 = at("k_zero_padded", [NKV, 2, S + RH], 152)
    VP = at("v_padded", [S + 2 * RH], 169.5)
    QR = at("head_roots", [2 * NT], 188.75)
    SQ = at("squares", [S], 198.5)
    QST = at("q_tile", [2, KD, P], 32)
    VST = at("v_window", [2, 2, P], 43)
    VTOK = at("v_token_major", [9, P], 190.5)
    PP = at("probs", [2, NQ, WIN], 50)
    PTA = at("probs_t_a", [NQ, P], 74)
    PTB = at("probs_t_b", [NQ, P], 82)
    STA = at("softmax_stats", [2, 6, NQ], 90)

    with ExitStack() as ctx:
        PS = ctx.enter_context(nc.psum_tensor("ps", [P, 8, HALF], F32))

        def sem(name):
            return ctx.enter_context(nc.semaphore(name))

        w_load = [sem("w_load0"), sem("w_load1")]
        w_hi, w_lo = sem("w_hi_done"), sem("w_lo_done")
        acc_done = sem("acc_done")
        acc_free = [sem("acc_free0"), sem("acc_free1")]
        h_hi, h_lo = sem("h_hi_done"), sem("h_lo_done")
        const_in, late_in, x_in = sem("const_in"), sem("late_const_in"), [sem(f"x_in{j}") for j in range(4)]
        vec_t, vec_ok, eps_set = sem("vectors_transposed"), sem("vectors_ready"), sem("eps_set")
        pads_zero, conv_zero, shift_zero = sem("attn_pads_zero"), sem("conv_zero"), sem("shift_zero")
        x_tr, x_ev, x_gain = sem("x_transposed"), sem("x_evacuated"), sem("x_gained")
        block = ctx.enter_context(nc.Block())

        seq = {"act": sem("act_waited"), "pool": sem("pool_waited"), "dve": sem("dve_waited")}

        def waited(engine, name):
            engine.sem_inc(seq[name], 1)

        ident = CON[:, C_ID:C_ID + P]
        blk = CON[:, C_BLK:C_BLK + P]
        ones = CON[:, C_ONE:C_ONE + P]

        def vb(row, n=4, m=P):
            return VT[:, row:row + n].unsqueeze(2).to_broadcast([P, n, m])

        def over(ap, n):
            return ap.unsqueeze(1).to_broadcast([P, n, ap.shape[1]])

        def acc(a_slot, half=None):
            return (PS[:, 2 * a_slot:2 * a_slot + 2, :] if half is None
                    else PS[:, 2 * a_slot + half, :])

        def acc2(a_slot):
            return acc(a_slot).rearrange("p b n -> p (b n)")

        win = w_in_ab[0].rearrange("(k p) n -> p k n", p=P)
        wout = w_out_ab[0].rearrange("(k p) n -> p k n", p=P)
        wqkv = w_qkv[0].rearrange("(k p) n -> p k n", p=P)
        wo = w_o[0].rearrange("(k p) n -> p k n", p=P)
        wup = [mlp_up[l].rearrange("(k p) n -> p k n", p=P) for l in range(2)]
        wdn = [mlp_down[l].rearrange("(g k p) n -> g p k n", k=GF, p=P) for l in range(2)]

        def load_unit(sp, slot, u, src, k=8):
            sp.wait_ge(w_lo, u + 1)
            sp.dma_start(WR[:, slot].rearrange("p (k n) -> p k n", k=k), src).then_inc(w_load[slot], 16)

        def split_hi(act, slot, n, need):
            act.wait_ge(w_load[slot], 16 * n + 16)
            act.wait_ge(acc_done, need)
            nc.scalar.copy(WH[:, slot], WR[:, slot]).then_inc(w_hi, 1)

        def split_lo(dve, slot, u):
            dve.wait_ge(w_hi, u + 1)
            nc.vector.tensor_tensor(WL[:, slot], WR[:, slot], WH[:, slot].bitcast(F32),
                                    ALU.subtract).then_inc(w_lo, 1)

        def load_stage(sp, name, src, units):
            u0, _ = STAGE[name]
            with sp.Fori(0, units // 2) as i:
                for j in range(2):
                    load_unit(sp, j, u0 + 2 * i + j, src[:, :, bass.ds((2 * i + j) * P, P)])

        def load_mlp(sp, l):
            u0, _ = STAGE[f"mlp{l}"]
            with sp.Fori(0, NG) as g:
                for j in range(4):
                    load_unit(sp, j % 2, u0 + 8 * g + j, wup[l][:, :, bass.ds(g * 512 + j * P, P)])
                for d in range(4):
                    src = wdn[l][bass.ds(g, 1)].rearrange("a p k n -> p (a k) n")
                    load_unit(sp, d % 2, u0 + 8 * g + 4 + d, src[:, :, 256 * d:256 * d + 256], k=4)

        def product(t, slot, a_slot, a_half, u, nk, step, off, xh, xl, ready=None, order=None,
                    new_unit=True, between=None):
            if new_unit:
                t.wait_ge(w_lo, u + 3)
            t.wait_ge(acc_free[a_slot], a_half + 1)
            order = order or list(range(nk))
            for n, k in enumerate(order):
                if between and n in between:
                    between[n]()
                if ready is not None:
                    t.wait_ge(ready[0], ready[1] + n + 1)
                w_h = WH[:, slot, k * step + off:k * step + off + P]
                w_l = WL[:, slot, k * step + off:k * step + off + P]
                for ww, xx in ((w_h, xh), (w_h, xl), (w_l, xh)):
                    first, last = n == 0 and ww is w_h and xx is xh, n == nk - 1 and ww is w_l
                    for half in range(2):
                        m = nc.tensor.matmul(acc(a_slot, half), ww,
                                             xx[:, k, half * HALF:(half + 1) * HALF],
                                             start=first, stop=last)
            m.then_inc(acc_done, 1)

        def dense_pe(t, name, units, order=None, loops=None):
            u0, a0_ = STAGE[name]
            fill = H_FILL[name]
            with t.Fori(0, units // 2) as i:
                for j in range(2):
                    product(t, j, j, a0_ // 2 + i, u0 + 2 * i + j, 8, P, 0, Hh, Hl,
                            ready=(h_lo, 8 * fill) if j == 0 else None, order=order)

        act_lo = sem("mlp_lo_done")
        acc_banks67 = PS[:, 6:8, :].rearrange("p b n -> p (b n)")

        def mlp_pe(t, l):
            u0, a0_ = STAGE[f"mlp{l}"]

            def group(g, between):
                for j in range(4):
                    product(t, j % 2, j % 2, a0_ // 2 + 6 * g + j // 2, u0 + 8 * g + j, 8, P, 0,
                            Hh, Hl, ready=(h_lo, 8 * H_FILL[f"mlp{l}"]) if j == 0 else None,
                            between=between if j == 0 else None)
                for m in range(8):
                    product(t, m // 2 % 2, m % 2, a0_ // 2 + 6 * g + 2 + m // 2, u0 + 8 * g + 4 + m // 2,
                            GF, 256, P * (m % 2), ACh, ACl,
                            ready=(act_lo, 4 * NG * l + 4 * g + 1) if m == 0 else None,
                            new_unit=m % 2 == 0)

            group(0, norm_between(t, f"mlp{l}"))
            with t.Fori(1, NG) as g:
                group(g, None)

        sq_pool, sq_last, ss_add = sem("squares_pool"), sem("last_square"), sem("squares_added")
        ss_tok, rms_done, rinv_done = sem("sum_squares_tokens"), sem("rms_done"), sem("rms_inverted")
        rinv_tr, ri_done = sem("rms_inverse_transposed"), sem("rms_inverse_ready")
        x_sq = sem("x_squared")
        NORMS = {"in": 0, "mlp0": 1, "qkv": 2, "mlp1": 3}

        def chunk_done(engine, name, k):
            a_next = STAGE[name][1] if name in STAGE else A_END
            engine.wait_ge(acc_free[k % 2], (a_next - 8 + k) // 2 + 2)

        def residual_done(engine, name):
            chunk_done(engine, name, KD - 1)

        def norm_pool(pool, name):
            base = 13 * (NORMS[name] - 1)
            TT = nc.gpsimd.tensor_tensor
            for k in range(KD - 1):
                chunk_done(pool, name, k)
                if k:
                    pool.wait_ge(sq_pool, base + 2 * k - 1)
                TT((ST1 if k else ST2)[:, 0:S], X[:, k], X[:, k], ALU.mult).then_inc(sq_pool, 1)
                if k:
                    pool.wait_ge(sq_pool, base + 2 * k)
                    TT(ST2[:, 0:S], ST2[:, 0:S], ST1[:, 0:S], ALU.add).then_inc(sq_pool, 1)

        def norm_act(act, name, row):
            n, f = NORMS[name], H_FILL[name]
            act.wait_ge(acc_done, STAGE[name][1] + 2)
            for k in range(KD):
                chunk_done(act, name, k)
                nc.scalar.activation(Hh[:, k], X[:, k], ACT.Copy, scale=VT[:, row + k:row + k + 1]).then_inc(h_hi, 1)
                if k == 0:
                    chunk_done(act, name, KD - 1)
                    nc.scalar.activation(ST0[:, 0:S], X[:, KD - 1], ACT.Square).then_inc(sq_last, 1)
                if k == 3:
                    act.wait_ge(ss_tok, n)
                    rms_root(act, PS[:, 4, 0:NT])
            rms_spread(act, n)

        def rms_root(act, sums):
            nc.scalar.activation(RIV[:, 0:NT], sums, ACT.Sqrt, bias=VT[:, 90:91], scale=1.0 / D).then_inc(rms_done, 1)

        def rms_spread(act, n):
            act.wait_ge(rinv_tr, n + 1)
            nc.scalar.copy(RI[:, :], PS[:, 4:6, :].rearrange("p b n -> p (b n)")).then_inc(ri_done, 1)

        def rms_invert(dve, n):
            dve.wait_ge(rms_done, n + 1)
            nc.vector.reciprocal(RIV[:, 0:NT], RIV[:, 0:NT]).then_inc(rinv_done, 1)

        def norm_dve(dve, name, row):
            n, f = NORMS[name], H_FILL[name]
            for k in range(KD):
                dve.wait_ge(h_hi, 8 * f + k + 1)
                nc.vector.scalar_tensor_tensor(Hl[:, k], X[:, k], VT[:, row + k:row + k + 1],
                                               Hh[:, k].bitcast(F32), ALU.mult, ALU.subtract).then_inc(h_lo, 1)
                if k == 0:
                    dve.wait_ge(sq_last, n)
                    dve.wait_ge(sq_pool, 13 * n)
                    nc.vector.tensor_tensor(ST2[:, 0:S], ST2[:, 0:S], ST0[:, 0:S], ALU.add).then_inc(ss_add, 1)
                if k == 4:
                    rms_invert(dve, n)
            dve.wait_ge(ri_done, n + 1)

        def norm_between(t, name):
            n = NORMS[name]

            def sums():
                t.wait_ge(ss_add, n)
                for tile in range(NT):
                    m = nc.tensor.matmul(PS[:, 4, tile:tile + 1], ST2[:, tile * P:tile * P + P], ones[:, 0:1],
                                         start=True, stop=True)
                m.then_inc(ss_tok, 1)

            def spread():
                t.wait_ge(rinv_done, n + 1)
                for tile in range(NT):
                    m = nc.tensor.transpose(bank(4 + tile // 4)[:, tile % 4],
                                            RIV[:, tile:tile + 1].to_broadcast([P, P]), ident)
                m.then_inc(rinv_tr, 1)

            return {5: spread} if name == "in" else {2: sums, 5: spread}

        def bank(n):
            return PS[:, n, :].rearrange("p (a m) -> p a m", m=P)

        def scale_out(dve, dst, slot):
            nc.vector.tensor_tensor(dst, acc2(slot), RI[:, :], ALU.mult).then_inc(acc_free[slot], 1)

        def h_lo_split(dve, f, k, src, pos=None):
            pos = k if pos is None else pos
            dve.wait_ge(h_hi, 8 * f + pos + 1)
            nc.vector.tensor_tensor(Hl[:, k], src, Hh[:, k].bitcast(F32), ALU.subtract).then_inc(h_lo, 1)

        relu_sq, act_hi = sem("relu_squared"), sem("mlp_hi_done")

        def mlp_act(act, l, g, last=False):
            u0, a0_ = STAGE[f"mlp{l}"]
            ag, n = a0_ + 12 * g, 4 * NG * l + 4 * g
            need = [None, ag + 2, ag + 3, ag + 4, ag + 5, ag + 6, ag + 8, ag + 10, ag + 13]
            for j in range(8):
                if not (last and j == 7):
                    split_hi(act, (j + 1) % 2, u0 // 2 + 4 * g + (j + 1) // 2, need[j + 1])
                if j < 4:
                    act.wait_ge(acc_free[j % 2], a0_ // 2 + 6 * g + j // 2 + 2)
                    nc.scalar.activation(ST1[:, 0:S], ST0[:, 0:S], ACT.Square).then_inc(relu_sq, 1)
                    act.wait_ge(relu_sq, n + j + 1)
                    nc.scalar.copy(ACh[:, j], ST1[:, 0:S]).then_inc(act_hi, 1)

        def mlp_dve(dve, l, g, last=False):
            u0, a0_ = STAGE[f"mlp{l}"]
            ag, n = a0_ + 12 * g, 4 * NG * l + 4 * g
            for j in range(8):
                if not (last and j == 7):
                    split_lo(dve, (j + 1) % 2, u0 + 8 * g + j + 1)
                if j < 4:
                    dve.wait_ge(acc_done, ag + j + 3)
                    nc.vector.scalar_tensor_tensor(ST0[:, 0:S], acc2(j % 2), 0.0, RI[:, :], ALU.max, ALU.mult)\
                        .then_inc(acc_free[j % 2], 1)
                    dve.wait_ge(act_hi, n + j + 1)
                    nc.vector.tensor_tensor(ACl[:, j], ST1[:, 0:S], ACh[:, j].bitcast(F32),
                                            ALU.subtract).then_inc(act_lo, 1)
                else:
                    for m in (2 * (j - 4), 2 * (j - 4) + 1):
                        dve.wait_ge(acc_done, ag + 4 + m + 3)
                        nc.vector.tensor_tensor(X[:, m], X[:, m], acc2(m % 2), ALU.add)\
                            .then_inc(acc_free[m % 2], 1)

        def residual_act(act, name, units):
            u0, a0_ = STAGE[name]
            with act.Fori(0, units // 2) as i:
                for j in range(2):
                    split_hi(act, 1 - j, u0 // 2 + i + j, a0_ + 2 * i + j + 2)

        def residual_dve(dve, name, units):
            u0, a0_ = STAGE[name]
            with dve.Fori(0, units // 2) as i:
                for j in range(2):
                    split_lo(dve, 1 - j, u0 + 2 * i + j + 1)
                    dve.wait_ge(acc_done, a0_ + 2 * i + j + 3)
                    xk = X[:, bass.ds(2 * i + j, 1), :]
                    nc.vector.tensor_tensor(xk, xk, acc2(j).unsqueeze(1), ALU.add).then_inc(acc_free[j], 1)

        conv_step, conv_done, ya_out = sem("conv_step"), sem("conv_done"), sem("ya_out")
        gl_free = sem("conv_output_left")
        shift_diff, shift_done = sem("shift_diff"), sem("shift_done")
        lora_act = sem("lora_inputs_activated")

        def in_act(act):
            with act.Fori(0, 12) as i:
                for j in range(2):
                    split_hi(act, 1 - j, i + j, 2 * i + j + 2)
            split_hi(act, 1, 12, 26)
            act.wait_ge(shift_done, 2 + 14)
            nc.scalar.activation(WA[0:RH, :], WA[0:RH, :], ACT.Tanh).then_inc(lora_act, 1)
            nc.scalar.activation(GL[:, :], GL[:, :], ACT.Sigmoid).then_inc(lora_act, 1)

        def in_dve(dve):
            dve.wait_ge(h_lo, NT)
            nc.vector.memset(ST2[:, 0:2], 0.0).then_inc(conv_zero, 1)
            dve.wait_ge(conv_zero, 1)
            dve.wait_ge(ri_done, 1)
            with dve.Fori(0, 2) as i:
                for q in range(2):
                    for r in range(3):
                        j = 3 * q + r
                        split_lo(dve, (j + 1) % 2, 6 * i + j + 1)
                        dve.wait_ge(acc_done, 6 * i + j + 3)
                        dve.wait_ge(conv_done, 2 * i + q + 1)
                        scale_out(dve, (ST0[:, 0:S], ST1[:, 0:S], WA[:, 0:S])[r], j % 2)
                    g = 2 * i + q
                    w = VT[:, bass.ds(V_CW + g, 1)], VT[:, bass.ds(V_CW + 4 + g, 1)], \
                        VT[:, bass.ds(V_CW + 8 + g, 1)]
                    dve.wait_ge(acc_free[q], 3 * i + q + 3)
                    cu = ST2
                    nc.vector.tensor_tensor(cu[:, 2:S + 2], ST1[:, 0:S], WA[:, :], ALU.mult).then_inc(conv_step, 1)
                    dve.wait_ge(conv_step, 4 * g + 1)
                    dve.wait_ge(gl_free, g + 1)
                    nc.vector.tensor_scalar(GL[:, :], cu[:, 2:S + 2], w[2], None, ALU.mult).then_inc(conv_step, 1)
                    for n in (1, 0):
                        dve.wait_ge(conv_step, 4 * g + 3 - n)
                        nc.vector.scalar_tensor_tensor(GL[:, :], cu[:, n:S + n], w[n], GL[:, :], ALU.mult,
                                                       ALU.add).then_inc(conv_step, 1)
                    dve.wait_ge(conv_step, 4 * g + 4)
                    nc.vector.tensor_tensor(GL[:, :], GL[:, :], ST0[:, 0:S], ALU.mult).then_inc(conv_done, 1)
            dve.wait_ge(conv_done, 5)
            nc.vector.memset(ST0[:, 0:1], 0.0).then_inc(shift_zero, 1)
            nc.vector.memset(ST1[:, 0:1], 0.0).then_inc(shift_zero, 1)
            dve.wait_ge(shift_zero, 2)
            with dve.Fori(0, 6) as i:
                for j in range(2):
                    split_lo(dve, 1 - j, 12 + 2 * i + j + 1)
                    shift(dve, 2 * i + j, j, 6 + i, RKV[:, bass.ds(2 * i + j, 1), :])
            split_lo(dve, 1, 25)
            dve.wait_ge(gl_free, 5)
            shift(dve, 12, 0, 12, WA[:, :].unsqueeze(1))
            shift(dve, 13, 1, 12, GL[:, :].unsqueeze(1))

        def shift(dve, n, slot, half, dst):
            st = (ST0, ST1)[slot]
            dve.wait_ge(acc_done, 2 * half + slot + 3)
            dve.wait_ge(shift_done, n + 1)
            scale_out(dve, st[:, 1:S + 1], slot)
            dve.wait_ge(acc_free[slot], half + 2)
            nc.vector.tensor_tensor(dst, st[:, 0:S].unsqueeze(1), st[:, 1:S + 1].unsqueeze(1), ALU.subtract)\
                .then_inc(shift_diff, 1)
            dve.wait_ge(shift_diff, n + 1)
            mu = VT[:, bass.ds(V_MU + n, 1)]
            nc.vector.scalar_tensor_tensor(dst, dst, mu, st[:, 1:S + 1].unsqueeze(1), ALU.mult, ALU.add)\
                .then_inc(shift_done, 1)

        class Track:

            def __init__(self, name, steps):
                self.sem, self.steps, self.next = sem(name), steps, 0

            def done(self, instruction, step):
                assert self.steps[self.next] == step, (self.steps[self.next], step)
                self.next = (self.next + 1) % len(self.steps)
                instruction.then_inc(self.sem, 1)

            def wait(self, engine, chunk, step):
                engine.wait_ge(self.sem, len(self.steps) * chunk + (self.steps.index(step) + 1))

        two = (0, 1)
        prep_pool = Track("prep_pool", ["wag", "vc", "g1m", "r_dec", "rk", "rk2"])
        prep_pe = Track("prep_pe", ["zw", "za", "n2", "bon"])
        prep_act = Track("prep_act", ["sq", "sw", "a", "g", "e1", "e2", "e1x", "nrm", "pad0", "pad1"])
        prep_dve = Track("prep_dve", ["kkr", "zws", "zas", "scan", "mid", "end", "d", "dx", "ka", "k2", "max", "rcp",
                                      "kkn", "a_dec", "b0", "b_dec", "k_dec", "bon"])
        solve_pe = Track("solve_pe", ["tok0", "tok1", "tok2", "tok3", "p1_0", "p1_1", "p2_0", "p2_1", "t0_0", "nv",
                                      "t0_1"]
                         + [f"{w}{k}_{b}" for k in range(LEVELS) for w, b in
                            (("y", 0), ("y", 1), ("dt", 0), ("dtt", 0), ("dt", 1), ("dtt", 1))
                            if not (w == "dt" and k == LEVELS - 1)]
                         + ["wt", "z", "u", "s", "o"])
        solve_act = Track("solve_act", ["tok0", "tok1", "tok2", "tok3", "t0_0", "nv", "t0_1"]
                          + [f"y{k}_{b}" for k in range(LEVELS) for b in two] + ["wt", "z", "o"])
        solve_dve = Track("solve_dve", ["m0", "m1", "n0", "n1", "s_in"]
                          + [f"{w}{k}_{b}" for k in range(LEVELS) for b in two for w in ("t", "tt")
                             if not (w == "t" and k == LEVELS - 1)] + ["u", "s1", "s"])
        solve_pool = Track("solve_pool", ["i0", "tt_0", "i1", "tt_1", "x0_0", "x0_1"]
                           + [f"x{k}_{b}" for k in range(1, LEVELS) for b in two])
        out_pe = Track("out_pe", ["mean", "var", "gate"])
        out_act = Track("out_act", ["sq", "sd"])
        out_dve = Track("out_dve", ["d", "rcp", "m1", "m4", "yb"])
        out_pool = Track("out_pool", ["m2", "m3"])
        state_zero, ar_zero = sem("state_zero"), sem("a_r_pads_zero")

        def part(c, first):
            return RKV[:, first:first + 4, bass.ds(c * P, P)]

        def heads(ap, b):
            return ap[:, 4 * b:4 * b + 4]

        HEAD = ("before the masks", "between the masks", "after the masks")
        PLACES = HEAD + tuple(range(LEVELS))

        def at_start(tile, n):
            return isinstance(tile, int) and tile < n

        def is_first(c):
            return at_start(c, 1)

        def prep_pool_step(pool, e, s, place):
            TT = nc.gpsimd.tensor_tensor
            if place == HEAD[0]:
                if not is_first(e):
                    prep_pe.wait(pool, e - 1, "za")
                    waited(pool, "pool")
                prep_pool.done(nc.gpsimd.tensor_copy(WAG[:, :], WA[:, bass.ds(e * P, P)]), "wag")
            if place == 0:
                prep_pool.done(nc.gpsimd.tensor_copy(VC[:, s], part(e, 8)), "vc")
            if place == 1:
                prep_act.wait(pool, e, "e1")
                prep_pool.done(TT(G1M[:, s], over(blk, 4), GS[:, s, 0].unsqueeze(2).to_broadcast([P, 4, P]),
                                  ALU.mult), "g1m")
                prep_pool.done(TT(AR[:, s, :, 1], T2[:, :], part(e, 0), ALU.mult), "r_dec")
            if place == 2:
                prep_dve.wait(pool, e, "k2")
                waited(pool, "pool")
                prep_pool.done(TT(T7[:, :], T0[:, :], part(e, 0), ALU.mult), "rk")
                prep_pool.wait(pool, e, "rk")
                prep_pool.done(TT(T7[:, :], T7[:, :], vb(V_RK), ALU.mult), "rk2")

        def prep_pe_step(t, e, s, place):
            if place == HEAD[0]:
                prep_pool.wait(t, e, "wag")
                for p in range(4):
                    m = nc.tensor.matmul(bank(7)[:, p], LOR[0:RH, 0, p * P:(p + 1) * P], WAG[0:RH, :],
                                         start=True, stop=True)
                prep_pe.done(m, "zw")
            if place == HEAD[1]:
                prep_dve.wait(t, e, "zws")
                for p in range(4):
                    m = nc.tensor.matmul(bank(7)[:, p], LOR[RH:P, 0, p * P:(p + 1) * P], WAG[RH:P, :],
                                         start=True, stop=True)
                prep_pe.done(m, "za")
            if place == 0:
                prep_dve.wait(t, e, "zas")
                if not is_first(e):
                    solve_act.wait(t, e - 1, "nv")
                prep_act.wait(t, e, "sq")
                prep_pe.done(nc.tensor.matmul(bank(7), blk, T6[:, :], start=True, stop=True), "n2")
            if place == 4:
                prep_act.wait(t, e, "nrm")
                prep_pool.wait(t, e, "rk2")
                prep_pe.done(nc.tensor.matmul(bank(7), blk, T7[:, :], start=True, stop=True), "bon")

        def prep_act_step(act, e, s, place):
            A = nc.scalar.activation
            if place == HEAD[0]:
                prep_dve.wait(act, e, "kkr")
                prep_act.done(A(T6[:, :], T5[:, :], ACT.Square), "sq")
                prep_dve.wait(act, e, "zws")
                prep_act.done(A(T0[:, :], T0[:, :], ACT.Sigmoid), "sw")
            if place == HEAD[1]:
                prep_dve.wait(act, e, "zas")
                prep_act.done(A(T1[:, :], T1[:, :], ACT.Sigmoid), "a")
            if place == 0:
                prep_dve.wait(act, e, "dx")
                prep_act.done(A(GS[:, s], GSR[:, :], ACT.Exp, scale=-KAPPA), "g")
                prep_act.done(A(T2[:, :], T3[:, :], ACT.Exp, scale=-KAPPA), "e1")
                prep_act.wait(act, e, "e1")
                prep_act.done(A(T3[:, :], T3[:, :], ACT.Exp, scale=KAPPA), "e2")
                prep_act.done(A(T4[:, :], T4[:, :], ACT.Exp, scale=-KAPPA), "e1x")
            if place == 1:
                prep_pe.wait(act, e, "n2")
                prep_act.done(A(T6[:, :], bank(7), ACT.Sqrt), "nrm")
            if place == 5:
                prep_dve.wait(act, e, "a_dec")
                prep_pool.wait(act, e, "r_dec")
                if not is_first(e):
                    solve_pe.wait(act, e - 1, "p2_1")
                for par in two:
                    rows = slice(RH * par, RH * par + RH)
                    prep_act.done(nc.scalar.copy(ARP[rows, :, par], AR[rows, s]), f"pad{par}")

        def prep_dve_step(dve, e, s, place):
            V, TT, STT = prep_dve, nc.vector.tensor_tensor, nc.vector.scalar_tensor_tensor
            k = part(e, 4)
            if place == HEAD[0]:
                if not is_first(e):
                    V.wait(dve, e - 1, "bon")
                V.done(TT(T5[:, :], k, vb(V_KK), ALU.mult), "kkr")
                prep_pe.wait(dve, e, "zw")
                V.done(TT(T0[:, :], bank(7), vb(V_W0), ALU.add), "zws")
            if place == HEAD[1]:
                prep_pe.wait(dve, e, "za")
                V.done(TT(T1[:, :], bank(7), vb(V_A0), ALU.add), "zas")
            if place == HEAD[2]:
                prep_act.wait(dve, e, "sw")
                flat = lambda ap: ap.rearrange("p a n -> p (a n)")
                V.done(nc.vector.tensor_tensor_scan(flat(T2[:, :]), CON[:, C_RST:C_RST + 4 * P], flat(T0[:, :]),
                                                    0.0, ALU.mult, ALU.add), "scan")
                V.wait(dve, e, "scan")
                V.done(nc.vector.tensor_copy(GSR[:, 0], T2[:, :, 63]), "mid")
                V.wait(dve, e, "mid")
                V.done(TT(GSR[:, 1], T2[:, :, 127], GSR[:, 0], ALU.subtract), "end")
                V.done(TT(T3[:, :], T2[:, :], GSR[:, 0].unsqueeze(2).to_broadcast([P, 4, P]), ALU.subtract), "d")
                V.wait(dve, e, "d")
                V.done(TT(T4[:, :], T3[:, :], T0[:, :], ALU.subtract), "dx")
            if place == 0:
                prep_act.wait(dve, e, "a")
                V.wait(dve, e, "dx")
                V.done(STT(T0[:, :], T1[:, :], -1.0, vb(V_KA), ALU.add, ALU.mult), "ka")
                V.wait(dve, e, "ka")
                V.done(STT(T0[:, :], T0[:, :], 1.0, k, ALU.add, ALU.mult), "k2")
            if place == 1:
                prep_act.wait(dve, e, "nrm")
                V.done(nc.vector.tensor_scalar(T6[:, :], T6[:, :], 1e-12, None, ALU.max), "max")
                V.wait(dve, e, "max")
                V.done(nc.vector.reciprocal(T6[:, :], T6[:, :]), "rcp")
            if place == 3:
                V.wait(dve, e, "rcp")
                V.done(TT(T5[:, :], T5[:, :], T6[:, :], ALU.mult), "kkn")
                V.wait(dve, e, "kkn")
                V.done(STT(AR[:, s, :, 0], T5[:, :], -1.0, T4[:, :], ALU.mult, ALU.mult), "a_dec")
                V.wait(dve, e, "a_dec")
                V.done(TT(T5[:, :], T5[:, :], T1[:, :], ALU.mult), "b0")
            if place == 4:
                V.wait(dve, e, "b0")
                V.done(TT(BK[:, s, 0], T5[:, :], T3[:, :], ALU.mult), "b_dec")
                V.done(TT(BK[:, s, 1], T0[:, :], T3[:, :], ALU.mult), "k_dec")
            if place == 5:
                prep_pe.wait(dve, e, "bon")
                prep_pool.wait(dve, e, "vc")
                V.done(TT(BON[:, s], bank(7), VC[:, s], ALU.mult), "bon")

        def out_pe_step(t, o, place):
            if place == 0:
                solve_act.wait(t, o, "o")
                out_pe.done(nc.tensor.matmul(bank(6), blk, part(o, 4), start=True, stop=True), "mean")
            if place == 1:
                out_act.wait(t, o, "sq")
                out_dve.wait(t, o, "d")
                out_pe.done(nc.tensor.matmul(bank(6), blk, part(o, 8), start=True, stop=True), "var")
            if place == 2:
                out_act.wait(t, o, "sd")
                for p in range(4):
                    m = nc.tensor.matmul(bank(6)[:, p], LOR[:, 1, p * P:(p + 1) * P], GL[:, bass.ds(o * P, P)],
                                         start=True, stop=True)
                out_pe.done(m, "gate")

        def out_act_step(act, o, place):
            if place == 0:
                out_dve.wait(act, o, "d")
                waited(act, "act")
                out_act.done(nc.scalar.activation(part(o, 8), part(o, 4), ACT.Square), "sq")
            if place == 1:
                out_pe.wait(act, o, "var")
                waited(act, "act")
                out_act.done(nc.scalar.activation(part(o, 8), bank(6), ACT.Sqrt, bias=VT[:, 91:92],
                                                  scale=1.0 / RH), "sd")

        def out_pool_step(pool, o, place):
            oo, TT = part(o, 4), nc.gpsimd.tensor_tensor
            if place == 3:
                out_dve.wait(pool, o, "m1")
                waited(pool, "pool")
                out_pool.done(TT(oo, oo, vb(V_LW), ALU.mult), "m2")
            if place == 4:
                out_pool.wait(pool, o, "m2")
                waited(pool, "pool")
                out_pool.done(TT(oo, oo, vb(V_LB), ALU.add), "m3")

        def out_dve_step(dve, o, s, place):
            O, TT = out_dve, nc.vector.tensor_tensor
            oo, vv = part(o, 4), part(o, 8)
            if place == 0:
                out_pe.wait(dve, o, "mean")
                O.done(nc.vector.scalar_tensor_tensor(oo, bank(6), -1.0 / RH, oo, ALU.mult, ALU.add), "d")
            if place == 2:
                out_act.wait(dve, o, "sd")
                waited(dve, "dve")
                O.done(nc.vector.reciprocal(vv, vv), "rcp")
            if place == 3:
                O.wait(dve, o, "rcp")
                O.done(TT(oo, oo, vv, ALU.mult), "m1")
            if place == 5:
                out_pool.wait(dve, o, "m3")
                O.done(TT(oo, oo, BON[:, s], ALU.add), "m4")
                O.wait(dve, o, "m4")
                out_pe.wait(dve, o, "gate")
                O.done(TT(part(o, 0), oo, bank(6), ALU.mult), "yb")

        def chunk_pe(t, c, s, prep, outp):
            T, MM, TR = solve_pe, nc.tensor.matmul, nc.tensor.transpose
            prep_dve.wait(t, c, "bon")
            prep_pool.wait(t, c, "rk2")
            for q in range(4):
                for p in range(4):
                    src = (AR[:, s, p, 0], BK[:, s, 0, p], BK[:, s, 1, p], VC[:, s, p])[q]
                    m = TR(bank(q)[:, p], src, ident)
                T.done(m, f"tok{q}")
            if prep:
                prep_pe_step(t, c + 1, 1 - s, HEAD[0])
            prep_act.wait(t, c, "pad1")
            for q in two:
                for b in two:
                    if q == 0 and b == 0:
                        if not is_first(c):
                            solve_dve.wait(t, c - 1, "s1")
                    elif q == 0:
                        solve_act.wait(t, c, "tok3")
                    elif b == 0:
                        solve_act.wait(t, c, "tok1")
                    else:
                        solve_dve.wait(t, c, "m0")
                    for j in two:
                        m = MM(PS[:, PRODUCT_BANK[q, b] + j].rearrange("p (g a m) -> p g a m", g=2, m=P),
                               BK[:, s, q, 2 * b + j], ARP[:, 2 * b + j], start=True, stop=True)
                    T.done(m, f"p{q + 1}_{b}")
                if q == 0 and prep:
                    prep_pe_step(t, c + 1, 1 - s, HEAD[1])
            for b in two:
                solve_pool.wait(t, c, f"tt_{b}")
                solve_dve.wait(t, c, f"n{b}")
                for j in range(4):
                    m = TR(bank(3 * b)[:, j], TIT[:, 4 * b + j], ident)
                T.done(m, f"t0_{b}")
                if b == 0:
                    solve_dve.wait(t, c, "n1")
                    if prep:
                        prep_dve.wait(t, c + 1, "zas")
                    for h in range(8):
                        m = MM(PS[:, 7, RH * h:RH * h + RH], NTRK[:, h, 0], TOK[:, 3, RH * h:RH * h + RH],
                               start=True, stop=True)
                    T.done(m, "nv")
            for k in range(LEVELS):
                if outp:
                    out_pe_step(t, c - 1, k)
                if prep:
                    prep_pe_step(t, c + 1, 1 - s, k)
                for b in two:
                    solve_pool.wait(t, c, f"x{k}_{b}")
                    if k == 0:
                        solve_act.wait(t, c, f"t0_{b}")
                    else:
                        solve_dve.wait(t, c, f"t{k - 1}_{b}")
                    for j in range(4):
                        m = MM(bank(3 * b)[:, j], XL[:, 4 * b + j], TI[:, 4 * b + j], start=True, stop=True)
                    T.done(m, f"y{k}_{b}")
                for b in two:
                    solve_act.wait(t, c, f"y{k}_{b}")
                    if k > 0:
                        solve_dve.wait(t, c, f"tt{k - 1}_{b}")
                    if k < LEVELS - 1:
                        for j in range(4):
                            m = MM(bank(3 * b + 1)[:, j], TIT[:, 4 * b + j], YL[:, 4 * b + j],
                                   start=True, stop=True)
                        T.done(m, f"dt{k}_{b}")
                    for j in range(4):
                        m = MM(bank(3 * b + 2)[:, j], YL[:, 4 * b + j], TIT[:, 4 * b + j], start=True, stop=True)
                    T.done(m, f"dtt{k}_{b}")
            for b in two:
                solve_dve.wait(t, c, f"tt{LEVELS - 1}_{b}")
                for h in range(4 * b, 4 * b + 4):
                    lo = RH * (h % 2)
                    m = MM(PS[lo:lo + RH, 0, P * (h // 2):P * (h // 2) + P], TOK[:, 0, RH * h:RH * h + RH],
                           TIT[:, h], start=True, stop=True)
            T.done(m, "wt")
            for h in range(8):
                m = MM(PS[:, 1, RH * h:RH * h + RH], TIT[:, h], NV[:, RH * h:RH * h + RH], start=True, stop=True)
            T.done(m, "z")
            for p in range(4):
                MM(bank(4)[:, p], TOK[:, 2, P * p:P * p + P], TOK[:, 3, P * p:P * p + P], start=(p == 0),
                   stop=False, skip_group_check=True)
            solve_act.wait(t, c, "wt")
            solve_dve.wait(t, c, "s_in")
            for p in range(4):
                m = MM(bank(3)[:, p], WT[:, p], SP_[:, p], start=True, stop=True)
            T.done(m, "u")
            if outp:
                out_dve.wait(t, c - 1, "yb")
            for p in range(4):
                MM(bank(6)[:, p], SP_[:, p], AR[:, s, p, 1], start=(p == 0), stop=False, skip_group_check=True)
            for h in range(8):
                lo = RH * (h % 2)
                MM(PS[lo:lo + RH, 6, P * (h // 2):P * (h // 2) + P], TOK[:, 3, RH * h:RH * h + RH],
                   NTRK[:, h, 1], start=False, stop=False, skip_group_check=True)
            solve_dve.wait(t, c, "u")
            for p in range(4):
                m = MM(bank(4)[:, p], TOK[:, 1, P * p:P * p + P], UU[:, P * p:P * p + P], start=False, stop=True,
                       skip_group_check=True)
            T.done(m, "s")
            for h in range(8):
                lo = RH * (h % 2)
                m = MM(PS[lo:lo + RH, 6, P * (h // 2):P * (h // 2) + P], UU[:, RH * h:RH * h + RH],
                       MTRB[:, h, 1], start=False, stop=True, skip_group_check=True)
            T.done(m, "o")

        def chunk_act(act, c, s, prep, outp):
            T = solve_act
            for q in range(4):
                solve_pe.wait(act, c, f"tok{q}")
                T.done(nc.scalar.copy(TOK[:, q], PS[:, q]), f"tok{q}")
            if prep:
                for place in HEAD:
                    prep_act_step(act, c + 1, 1 - s, place)
            solve_pe.wait(act, c, "t0_0")
            T.done(nc.scalar.copy(heads(TI, 0), bank(0)), "t0_0")
            solve_pe.wait(act, c, "nv")
            T.done(nc.scalar.copy(NV[:, :], PS[:, 7]), "nv")
            solve_pe.wait(act, c, "t0_1")
            T.done(nc.scalar.copy(heads(TI, 1), bank(3)), "t0_1")
            for k in range(LEVELS):
                for b in two:
                    solve_pe.wait(act, c, f"y{k}_{b}")
                    T.done(nc.scalar.copy(heads(YL, b), bank(3 * b)), f"y{k}_{b}")
                if outp:
                    out_act_step(act, c - 1, k)
                if prep:
                    prep_act_step(act, c + 1, 1 - s, k)
            solve_pe.wait(act, c, "wt")
            T.done(nc.scalar.copy(WT[:, :], bank(0)), "wt")
            solve_pe.wait(act, c, "z")
            T.done(nc.scalar.copy(ZZ[:, :], PS[:, 1]), "z")
            solve_pe.wait(act, c, "o")
            waited(act, "act")
            T.done(nc.scalar.copy(part(c, 4), bank(6)), "o")

        PRODUCT_BANK = {(0, 0): 4, (0, 1): 2, (1, 0): 0, (1, 1): 4}

        def chunk_dve(dve, c, s, prep, outp):
            T, TT = solve_dve, nc.vector.tensor_tensor
            if prep:
                prep_dve_step(dve, c + 1, 1 - s, HEAD[0])
            if not is_first(c):
                solve_pe.wait(dve, c - 1, "o")
            for q, dst in ((0, MTRB), (1, NTRK)):
                for b in two:
                    solve_pe.wait(dve, c, f"p{q + 1}_{b}")
                    T.done(TT(dst[:, 4 * b:4 * b + 4].rearrange("p h a m -> p h (a m)"),
                              PS[:, PRODUCT_BANK[q, b]:PRODUCT_BANK[q, b] + 2].rearrange(
                                  "p j (g m) -> p (j g) m", g=2),
                              over(CON[:, C_MU:C_MU + 2 * P], 4), ALU.mult), f"{'mn'[q]}{b}")
                if q == 0 and prep:
                    prep_dve_step(dve, c + 1, 1 - s, HEAD[1])
            if prep:
                prep_dve_step(dve, c + 1, 1 - s, HEAD[2])
            prep_pool.wait(dve, c, "g1m")
            if is_first(c):
                dve.wait_ge(state_zero, 1)
            else:
                T.wait(dve, c - 1, "s")
            T.done(TT(SP_[:, :], SS[:, :], G1M[:, s], ALU.mult), "s_in")
            for k in range(LEVELS):
                for b in two:
                    if k < LEVELS - 1:
                        solve_pe.wait(dve, c, f"dt{k}_{b}")
                        T.done(TT(heads(TI, b), heads(TI, b), bank(3 * b + 1), ALU.add), f"t{k}_{b}")
                    solve_pe.wait(dve, c, f"dtt{k}_{b}")
                    T.done(TT(heads(TIT, b), heads(TIT, b), bank(3 * b + 2), ALU.add), f"tt{k}_{b}")
                if outp:
                    out_dve_step(dve, c - 1, 1 - s, k)
                if prep:
                    prep_dve_step(dve, c + 1, 1 - s, k)
            solve_pe.wait(dve, c, "u")
            solve_act.wait(dve, c, "z")
            T.done(TT(UU[:, :], PS[:, 3], ZZ[:, :], ALU.add), "u")
            solve_pe.wait(dve, c, "s")
            T.done(TT(SS[:, :], bank(4), SP_[:, :], ALU.add), "s1")
            T.wait(dve, c, "s1")
            T.done(TT(SS[:, :], SS[:, :], GS[:, s, 1].unsqueeze(2).to_broadcast([P, 4, P]), ALU.mult), "s")

        def chunk_pool(pool, c, s, prep, outp):
            T, TT = solve_pool, nc.gpsimd.tensor_tensor
            if prep:
                prep_pool_step(pool, c + 1, 1 - s, HEAD[0])
            if not is_first(c):
                solve_pe.wait(pool, c - 1, "o")
            for b in two:
                solve_dve.wait(pool, c, f"m{b}")
                T.done(TT(heads(TIT, b), MTRB[:, 4 * b:4 * b + 4, 0], over(CON[:, C_M0:C_M0 + P], 4), ALU.mult),
                       f"i{b}")
                T.wait(pool, c, f"i{b}")
                T.done(TT(heads(TIT, b), heads(TIT, b), over(ident, 4), ALU.add), f"tt_{b}")
            for k in range(LEVELS):
                for b in two:
                    if k > 0:
                        solve_pe.wait(pool, c, f"y{k - 1}_{b}")
                    T.done(TT(heads(XL, b), MTRB[:, 4 * b:4 * b + 4, 0],
                              over(CON[:, C_MX + k * P:C_MX + (k + 1) * P], 4), ALU.mult), f"x{k}_{b}")
                if outp:
                    out_pool_step(pool, c - 1, k)
                if prep:
                    prep_pool_step(pool, c + 1, 1 - s, k)

        def recurrence(engine, chunk, prep_step, out_step):
            for place in PLACES:
                prep_step(engine, 0, 0, place)
            chunk(engine, 0, 0, True, False)
            with engine.Fori(0, (NT - 2) // 2) as i:
                for j in two:
                    chunk(engine, 2 * i + (1 + j), 1 - j, True, True)
            chunk(engine, NT - 1, 1, False, True)
            for place in PLACES:
                out_step(engine, NT - 1, place)

        OUT_ORDER = [4, 5, 6, 7, 0, 1, 2, 3]
        ya_back = sem("ya_back")

        def mixed_split(eng, act):
            for n, k in enumerate(OUT_ORDER):
                src = RKV[:, k - 4] if k >= 4 else RKV[:, k + 4]
                if n == 4:
                    eng.wait_ge(ya_back, 16)
                if act:
                    if n == 0:
                        out_dve.wait(eng, NT - 1, "yb")
                    nc.scalar.copy(Hh[:, k], src).then_inc(h_hi, 1)
                else:
                    h_lo_split(eng, 1, k, src, pos=n)

        qk_sq, qk_ms, qk_sd, qk_rc, qk_ex, qk_tr, qk_norm = (
            sem("qk_squared"), sem("qk_mean_square"), sem("qk_root"), sem("qk_inverted"), sem("qk_expanded"),
            sem("qk_inverse_transposed"), sem("qk_normed"))
        k2_in, v_tr, v_tok = sem("k2_in"), sem("v_transposed"), sem("v_token_major")
        SQB = (SQ[:, 0:S], ST2[:, 0:S])
        STB = (ST0[:, 0:S], ST1[:, 0:S])

        def qkv_pe(t):
            u0, a0_ = STAGE["qkv"]

            def unit(j, slot, half, between, ready=None):
                product(t, slot, slot, a0_ // 2 + half, u0 + j, 8, P, 0, Hh, Hl, ready=ready, between=between)

            def mean_square(n, slot):
                t.wait_ge(qk_sq, n + 1)
                for tile in range(NT):
                    m = nc.tensor.matmul(PS[:, 4, 2 * tile:2 * tile + 2], SQB[slot][:, tile * P:tile * P + P],
                                         blk[:, 0:P:RH], start=True, stop=True)
                m.then_inc(qk_ms, 1)

            def spread(n, slot):
                t.wait_ge(qk_ex, n + 1)
                t.wait_ge(qk_norm, n + 2)
                for tile in range(NT):
                    m = nc.tensor.transpose(bank(6 + tile // 4)[:, tile % 4], SQB[slot][:, tile * P:tile * P + P], ident)
                m.then_inc(qk_tr, 1)

            def norm_steps(n, slot):
                return {3: lambda: mean_square(n, slot), 6: lambda: spread(n, slot)}

            def v_transposes():
                t.wait_ge(acc_free[1], a0_ // 2 + 2)
                t.wait_ge(pads_zero, 3)
                t.wait_ge(qk_norm, 3)
                for n in range(9):
                    m = nc.tensor.transpose(bank((6, 7, 5)[n // 4])[:, n % 4], VP[:, P * n:P * n + P], ident)
                m.then_inc(v_tr, 1)

            unit(0, 0, 0, norm_between(t, "qkv"), ready=(h_lo, 8 * H_FILL["qkv"]))
            unit(1, 1, 0, norm_steps(0, 0))
            unit(2, 0, 1, {4: v_transposes})
            t.wait_ge(v_tok, 3)
            unit(3, 1, 1, norm_steps(1, 0))
            with t.Fori(0, 3) as i:
                unit(2 * i + 4, 0, i + 2, norm_steps(2 * i + 2, 1))
                unit(2 * i + 5, 1, i + 2, norm_steps(2 * i + 3, 0))
            mean_square(8, 1)
            spread(8, 1)

        def qkv_act(act):
            u0, a0_ = STAGE["qkv"]

            def inverse_root(n, slot):
                act.wait_ge(qk_norm, 3 if at_start(n, 2) and n == 1 else n + 1)
                nc.scalar.activation(SQB[slot], STB[slot], ACT.Square).then_inc(qk_sq, 1)
                act.wait_ge(qk_ms, n + 1)
                nc.scalar.activation(QR[:, :], PS[:, 4, 0:2 * NT], ACT.Sqrt, bias=VT[:, 90:91], scale=1.0 / RH)\
                    .then_inc(qk_sd, 1)
                act.wait_ge(qk_rc, n + 1)
                nc.scalar.copy(SQB[slot].rearrange("p (a m) -> p a m", m=RH), QR[:, :].unsqueeze(2).to_broadcast(
                    [P, 2 * NT, RH])).then_inc(qk_ex, 1)

            def step(j, slot, i, n):
                split_hi(act, slot, u0 // 2 + i + 1, a0_ + j + 3)
                if n is not None:
                    act.wait_ge(acc_free[slot], a0_ // 2 + i + 2)
                    inverse_root(n, slot)

            split_hi(act, 1, u0 // 2, a0_ + 2)
            step(0, 0, 0, 0)
            step(1, 1, 0, None)
            step(2, 0, 1, 1)
            with act.Fori(0, 3) as i:
                step(2 * i + 3, 1, i + 1, 2 * i + 2)
                step(2 * i + 4, 0, i + 2, 2 * i + 3)
            act.wait_ge(acc_free[1], a0_ // 2 + 6)
            inverse_root(8, 1)

        def qkv_dve(dve):
            u0, a0_ = STAGE["qkv"]

            def stage(j, slot, n, dst):
                dve.wait_ge(acc_done, a0_ + j + 3)
                if n is not None:
                    dve.wait_ge(qk_norm, 3 if at_start(n, 2) and n == 1 else n + 1)
                scale_out(dve, dst, slot)

            def invert(n):
                dve.wait_ge(qk_sd, n + 1)
                nc.vector.reciprocal(QR[:, :], QR[:, :]).then_inc(qk_rc, 1)
                dve.wait_ge(qk_tr, n + 1)

            def norm(n, slot, dst):
                invert(n)
                nc.vector.scalar_tensor_tensor(dst, STB[slot], VT[:, V_QS:V_QS + 1], acc_banks67, ALU.mult,
                                               ALU.mult).then_inc(qk_norm, 1)

            def q(n):
                return Q[:, bass.ds(n, 1), :].rearrange("p a n -> p (a n)")

            split_lo(dve, 1, u0 + 1)
            stage(0, 0, 0, STB[0])
            split_lo(dve, 0, u0 + 2)
            invert(0)
            dve.wait_ge(pads_zero, 3)
            for kv in two:
                rows = slice(RH * kv, RH * kv + RH)
                m = nc.vector.scalar_tensor_tensor(K2[rows, kv, kv, RH:RH + S], STB[0][rows], VT[rows, V_KG:V_KG + 1],
                                                   acc_banks67[rows], ALU.mult, ALU.mult)
            m.then_inc(qk_norm, 1)
            stage(1, 1, None, VP[:, RH:RH + S])
            split_lo(dve, 1, u0 + 3)
            dve.wait_ge(v_tr, 1)
            for n in (0, 1, 2):
                rows = 4 if n < 2 else 1
                nc.vector.tensor_copy(VTOK[:, 4 * n:4 * n + rows], bank((6, 7, 5)[n])[:, 0:rows]).then_inc(v_tok, 1)
            stage(2, 0, 1, STB[0])
            split_lo(dve, 0, u0 + 4)
            norm(1, 0, Q[:, 0])
            with dve.Fori(0, 3) as i:
                stage(2 * i + 3, 1, 2 * i + 2, STB[1])
                split_lo(dve, 1, u0 + 2 * i + 5)
                norm(2 * i + 2, 1, q(2 * i + 1))
                stage(2 * i + 4, 0, 2 * i + 3, STB[0])
                split_lo(dve, 0, u0 + 2 * i + 6)
                norm(2 * i + 3, 0, q(2 * i + 2))
            stage(9, 1, 8, STB[1])
            norm(8, 1, Q[:, 7])

        q_pool = Track("q_tile_copied", ["q"])
        v_pool = Track("v_tile_copied", ["v"])
        p_pool = Track("probs_pool", ["p1", "p3"])
        sc_pe = Track("score_pe", [f"sc{g}" for g in range(4)])
        pv_pe = Track("value_pe", [f"t{w}{g}" for g in range(4) for w in "ab"] + ["pv"])
        sc_dve = Track("score_dve", [f"{w}{g}" for g in range(4) for w in ("b", "max", "neg")] + ["sink"])
        pv_dve = Track("value_dve", ["den", "rcp", "p0", "e0", "e1", "p2", "e2", "e3"])
        sc_act = Track("score_act", [f"e{g}" for g in range(4)] + ["sink"])
        pv_act = Track("value_act", [f"e{g}" for g in range(4)] + ["o0", "o1"])
        ptb_zero, nsnk_ok = sem("probs_rest_zero"), sem("minus_sinks_ready")
        slopes = [2.0 ** (-8.0 * (h + 1) / NQ) for h in range(NQ)]

        def score_banks(g):
            return PS[:, 2 * (g % 2):2 * (g % 2) + 2, 0:2 * WIN]

        def q_tile(pool, tile, s):
            if not at_start(tile, 2):
                sc_pe.wait(pool, tile - 2, "sc3")
                waited(pool, "pool")
            q_pool.done(nc.gpsimd.tensor_copy(QST[:, s], Q[:, :, bass.ds(tile * P, P)]), "q")

        def v_tile(pool, tile, s):
            if not at_start(tile, 2):
                pv_pe.wait(pool, tile - 2, "pv")
                waited(pool, "pool")
            v_pool.done(nc.gpsimd.tensor_copy(VST[:, s], VTOK[:, bass.ds(tile, 2), :]), "v")

        def score_products(t, tile, s, g):
            if g == 0:
                q_pool.wait(t, tile, "q")
            if g >= 2:
                sc_dve.wait(t, tile, f"b{g - 2}")
            elif not at_start(tile, 1):
                sc_dve.wait(t, tile - 1, f"b{g + 2}")
            for j in two:
                m = nc.tensor.matmul(score_banks(g)[:, j].rearrange("p (a m) -> p a m", a=2), QST[:, s, 2 * g + j],
                                     K2[:, g // 2, :, bass.ds(tile * P, WIN)], start=True, stop=True)
            sc_pe.done(m, f"sc{g}")

        def probs_transposes(t, tile, s, g):
            if g % 2:
                p_pool.wait(t, tile, f"p{g}")
            else:
                pv_dve.wait(t, tile, f"p{g}")
            if g > 0:
                pv_act.wait(t, tile, f"e{g - 1}")
                pv_dve.wait(t, tile, f"e{g - 1}")
            for j in range(4):
                m = nc.tensor.transpose(bank(4)[:, j], PP[:, s, 4 * g + j, 0:P], ident)
            pv_pe.done(m, f"ta{g}")
            for j in range(4):
                m = nc.tensor.transpose(bank(5)[0:RH, j], PP[:, s, 4 * g + j, P:WIN], ident)
            pv_pe.done(m, f"tb{g}")

        def value_products(t, tile, s):
            pv_act.wait(t, tile, "e3")
            pv_dve.wait(t, tile, "e3")
            v_pool.wait(t, tile, "v")
            if at_start(tile, 1):
                t.wait_ge(ptb_zero, 1)
            else:
                pv_act.wait(t, tile - 1, "o1")
            for kv in range(NKV):
                for n, pt in enumerate((PTA, PTB)):
                    for par in two:
                        o = PS[RH * par:RH * par + RH, 6 + kv].rearrange("p (a m) -> p a m", m=P)
                        m = nc.tensor.matmul(o, VST[:, s, n, RH * kv:RH * kv + RH], pt[:, 8 * kv + par:8 * kv + 8:2],
                                             start=n == 0, stop=n == 1)
            pv_pe.done(m, "pv")

        def round_pe(t, new, old, s):
            for g in range(4):
                if new is not None and g < 3:
                    score_products(t, new, s, g + 1)
                if g == 3 and new is not None and not (isinstance(new, int) and new == NT - 1):
                    score_products(t, new + 1, 1 - s, 0)
                if old is not None:
                    probs_transposes(t, old, 1 - s, g)
            if old is not None:
                value_products(t, old, 1 - s)

        def round_dve(dve, new, old, s):
            o = 1 - s
            first = C_DIST + WIN if at_start(new, 1) else C_DIST
            dist = CON[:, first:first + WIN]
            for g in range(4):
                hs = slice(4 * g, 4 * g + 4)
                if new is not None:
                    sc_pe.wait(dve, new, f"sc{g}")
                    if not at_start(new, 2):
                        pv_pe.wait(dve, new - 2, f"tb{g}")
                    for j in range(4):
                        h = 4 * g + j
                        m = nc.vector.scalar_tensor_tensor(
                            PP[:, s, h], dist, -slopes[h],
                            score_banks(g)[:, j // 2, WIN * (j % 2):WIN * (j % 2) + WIN], ALU.mult, ALU.add)
                    sc_dve.done(m, f"b{g}")
                    sc_dve.wait(dve, new, f"b{g}")
                    sc_dve.done(nc.vector.tensor_reduce(STA[:, s, 0, hs], PP[:, s, hs], AXX, ALU.max), f"max{g}")
                    sc_dve.wait(dve, new, f"max{g}")
                    sc_dve.done(nc.vector.scalar_tensor_tensor(STA[:, s, 2, hs], STA[:, s, 0, hs], -1.0, NSNK[:, hs],
                                                               ALU.mult, ALU.min), f"neg{g}")
                if old is not None:
                    if g == 0:
                        sc_act.wait(dve, old, "sink")
                        pv_dve.done(nc.vector.tensor_tensor(STA[:, o, 4], STA[:, o, 4], STA[:, o, 5], ALU.add), "den")
                        pv_dve.wait(dve, old, "den")
                        pv_dve.done(nc.vector.reciprocal(STA[:, o, 4], STA[:, o, 4]), "rcp")
                        pv_dve.wait(dve, old, "rcp")
                    else:
                        rest_copy(dve, old, g - 1)
                    if g % 2 == 0:
                        pv_dve.done(nc.vector.tensor_tensor(
                            PP[:, o, hs], PP[:, o, hs], STA[:, o, 4, hs].unsqueeze(2).to_broadcast([P, 4, WIN]),
                            ALU.mult), f"p{g}")
            if new is not None:
                sc_dve.wait(dve, new, "neg3")
                sc_dve.done(nc.vector.tensor_tensor(STA[:, s, 3], SNK[:, :], STA[:, s, 2], ALU.add), "sink")
            if old is not None:
                rest_copy(dve, old, 3)

        def rest_copy(dve, tile, g):
            pv_pe.wait(dve, tile, f"tb{g}")
            if g == 0 and not at_start(tile, 1):
                pv_pe.wait(dve, tile - 1, "pv")
            pv_dve.done(nc.vector.tensor_copy(PTB[0:RH, 4 * g:4 * g + 4], bank(5)[0:RH]), f"e{g}")

        def round_act(act, new, old, s):
            for g in range(4):
                if new is not None:
                    sc_dve.wait(act, new, f"neg{g}")
                    for h in range(4 * g, 4 * g + 4):
                        m = nc.scalar.activation(PP[:, s, h], PP[:, s, h], ACT.Exp, bias=STA[:, s, 2, h:h + 1],
                                                 accum_out=STA[:, s, 4, h:h + 1])
                    sc_act.done(m, f"e{g}")
                    if g == 3:
                        sc_dve.wait(act, new, "sink")
                        sc_act.done(nc.scalar.activation(STA[:, s, 5], STA[:, s, 3], ACT.Exp), "sink")
                if old is not None:
                    pv_pe.wait(act, old, f"ta{g}")
                    pv_act.done(nc.scalar.copy(PTA[:, 4 * g:4 * g + 4], bank(4)), f"e{g}")
            if old is not None:
                pv_pe.wait(act, old, "pv")
                waited(act, "act")
                for kv in range(NKV):
                    pv_act.done(nc.scalar.copy(Q[:, 4 * kv:4 * kv + 4, bass.ds(old * P, P)], bank(6 + kv)), f"o{kv}")

        def round_pool(pool, new, old, s):
            o = 1 - s
            if new is not None and not (isinstance(new, int) and new == NT - 1):
                q_tile(pool, new + 1, o)
            if old is not None:
                pv_dve.wait(pool, old, "rcp")
                for g in (1, 3):
                    hs = slice(4 * g, 4 * g + 4)
                    p_pool.done(nc.gpsimd.tensor_tensor(
                        PP[:, o, hs], PP[:, o, hs], STA[:, o, 4, hs].unsqueeze(2).to_broadcast([P, 4, WIN]),
                        ALU.mult), f"p{g}")
            if new is not None:
                v_tile(pool, new, s)

        def attention(engine, one_round):
            one_round(engine, 0, None, 0)
            one_round(engine, 1, 0, 1)
            with engine.Fori(0, (NT - 4) // 2) as i:
                for j in two:
                    one_round(engine, 2 * i + (2 + j), 2 * i + (1 + j), j)
            one_round(engine, NT - 2, NT - 3, 0)
            one_round(engine, NT - 1, NT - 2, 1)
            one_round(engine, None, NT - 1, 0)

        def attn_split(eng, act):
            for k in range(KD):
                if act:
                    if k == 0:
                        pv_act.wait(eng, NT - 1, "o1")
                    nc.scalar.copy(Hh[:, k], Q[:, k]).then_inc(h_hi, 1)
                else:
                    h_lo_split(eng, 4, k, Q[:, k])

        out_tr, out_ev, out_st, out_dma = (sem("out_transposed"), sem("out_evacuated"), sem("out_staged"),
                                           [sem("out_dma0"), sem("out_dma1")])
        OT = at("out_tile", [2, KD, P], 64)

        GX = [b[:, 0:S].rearrange("p (k n) -> p k n", k=KD) for b in (ST1, ST2)]

        def x_banks(tile):
            return PS[:, 2 * (tile % 2):2 * (tile % 2) + 2, :].rearrange("p b (k n) -> p (b k) n", n=P)

        @block.sync
        def _(sp):
            sp.dma_start(CON[:, 0:C_MU], consts[:, 0:C_MU]).then_inc(const_in, 16)
            rows = [(V_MIX, norm_mix.rearrange("l (k p) -> (l k) p", p=P)),
                    (V_MLP, norm_mlp.rearrange("l (k p) -> (l k) p", p=P)),
                    (V_MU, shift_mu.rearrange("l (k p) -> (l k) p", p=P)),
                    (V_W0, w0.rearrange("l (k p) -> (l k) p", p=P)),
                    (V_A0, a0.rearrange("l (k p) -> (l k) p", p=P)),
                    (V_KK, k_k.rearrange("l (k p) -> (l k) p", p=P)),
                    (V_KA, k_a.rearrange("l (k p) -> (l k) p", p=P)),
                    (V_RK, r_k.rearrange("l (k h) n -> (l k) (h n)", h=2)),
                    (V_LW, lnx_w.rearrange("l (k p) -> (l k) p", p=P)),
                    (V_LB, lnx_b.rearrange("l (k p) -> (l k) p", p=P)),
                    (V_CW, conv_w.rearrange("l j (k p) -> (l j k) p", p=P))]
            for row, src in rows:
                sp.dma_start(VROW[row:row + src.shape[0], :], src).then_inc(const_in, 16)
            for half in two:
                sp.dma_start(VROW[V_QG:V_QG + 1, RH * half:RH * half + RH], q_gain).then_inc(const_in, 16)
                sp.dma_start(VROW[V_KG:V_KG + 1, RH * half:RH * half + RH], k_gain).then_inc(const_in, 16)
            with sp.Fori(0, 2) as i:
                for q in range(2):
                    for r in range(3):
                        load_unit(sp, (3 * q + r) % 2, 6 * i + 3 * q + r,
                                  win[:, :, bass.ds(i * 256 + (512 * r + P * q), P)])
            sp.dma_start(CON[:, C_MU:], consts[:, C_MU:]).then_inc(late_in, 16)
            sp.dma_start(LOR[0:RH, 0], w_decay2[0]).then_inc(late_in, 16)
            sp.dma_start(LOR[RH:P, 0], w_aaa2[0]).then_inc(late_in, 16)
            sp.dma_start(LOR[:, 1], w_gate2[0]).then_inc(late_in, 16)
            sp.dma_start(SNK[:, :], sinks.to_broadcast([P, NQ])).then_inc(late_in, 16)
            with sp.Fori(0, 7) as i:
                for j in two:
                    load_unit(sp, j, 12 + 2 * i + j, win[:, :, bass.ds(i * 256 + (1536 + P * j), P)])
            solve_pe.wait(sp, NT - 1, "p2_1")
            load_stage(sp, "out", wout, 8)
            load_mlp(sp, 0)
            u0 = STAGE["qkv"][0]
            for j in two:
                load_unit(sp, j, u0 + j, wqkv[:, :, S + P * j:S + P * j + P])
            with sp.Fori(0, 4) as i:
                for j in two:
                    load_unit(sp, j, u0 + 2 + 2 * i + j, wqkv[:, :, bass.ds((2 * i + j) * P, P)])
            load_stage(sp, "wo", wo, 8)
            load_mlp(sp, 1)
            oo = out[0].rearrange("(t p) (k n) -> t p k n", p=P, n=P)
            for j in two:
                sp.sem_inc(out_dma[j], 16)
            with sp.Fori(0, NT // 2) as i:
                for j in two:
                    sp.wait_ge(out_ev, 2 * i + j + 3)
                    sp.dma_start(oo[bass.ds(2 * i + j, 1)].rearrange("a p k n -> p (a k) n"), OT[:, j])\
                        .then_inc(out_dma[j], 16)
            for j in two:
                sp.wait_ge(out_dma[j], 16 * (NT // 2 + 1))


        @block.gpsimd
        def _(pool):
            pool.sem_inc(gl_free, 1)
            nc.gpsimd.memset(VT[:, 90:91], EPS).then_inc(eps_set, 1)
            nc.gpsimd.memset(VT[:, 91:92], LNX_EPS).then_inc(eps_set, 1)
            xin = x[0].rearrange("(t p) (k n) -> t p k n", p=P, n=P)
            for tile in range(NT):
                if tile >= 4:
                    pool.wait_ge(x_tr, 2 + tile - 3)
                    pool.wait_ge(x_sq, tile - 3)
                pool.dma_start(XIN[:, tile % 4], xin[tile]).then_inc(x_in[tile % 4], 16)
            for g in range(4):
                pool.wait_ge(conv_done, g + 2)
                pool.dma_start(ya_dram[g], GL[:, :]).then_inc(ya_out, 16)
                pool.wait_ge(ya_out, 16 * g + 16)
                pool.sem_inc(gl_free, 1)
            pool.wait_ge(lora_act, 2)
            pool.wait_ge(late_in, 16 * N_LATE)
            nc.gpsimd.memset(SS[:, :], 0.0).then_inc(state_zero, 1)
            nc.gpsimd.memset(ARP[:, :, :, :], 0.0).then_inc(ar_zero, 1)
            pool.wait_ge(ar_zero, 1)
            recurrence(pool, chunk_pool, prep_pool_step, out_pool_step)
            out_dve.wait(pool, NT - 1, "yb")
            pool.dma_start(RKV[:, 4:8], ya_dram.rearrange("g p n -> p g n")).then_inc(ya_back, 16)
            norm_pool(pool, "mlp0")
            residual_done(pool, "mlp0")
            nc.gpsimd.memset(K2[:, :, :, :], 0.0).then_inc(pads_zero, 1)
            nc.gpsimd.memset(VP[:, 0:RH], 0.0).then_inc(pads_zero, 1)
            nc.gpsimd.memset(VP[:, RH + S:], 0.0).then_inc(pads_zero, 1)
            norm_pool(pool, "qkv")
            pool.wait_ge(qk_norm, 3)
            for kv in two:
                here, there = slice(RH * kv, RH * kv + RH), slice(RH * (1 - kv), RH * (1 - kv) + RH)
                pool.dma_start(K2[there, kv, 1 - kv, RH:RH + S], K2[here, kv, kv, RH:RH + S]).then_inc(k2_in, 16)
            pool.wait_ge(qk_norm, 2 + 9)
            q_tile(pool, 0, 0)
            q_pool.wait(pool, 0, "q")
            nc.gpsimd.memset(PTB[RH:P], 0.0).then_inc(ptb_zero, 1)
            pool.wait_ge(ptb_zero, 1)
            attention(pool, round_pool)
            norm_pool(pool, "mlp1")

        @block.scalar
        def _(act):
            for tile in range(NT):
                act.wait_ge(x_in[tile % 4], 16 * (tile // 4) + 16)
                if tile:
                    act.wait_ge(x_sq, tile)
                nc.scalar.activation(ST0[:, 0:S], XIN[:, tile % 4], ACT.Square, accum_out=SSQ[:, tile:tile + 1])\
                    .then_inc(x_sq, 1)
                cols = slice(tile * P, tile * P + P)
                act.wait_ge(x_tr, tile + 3)
                nc.scalar.copy(X[:, :, cols], x_banks(tile)).then_inc(x_ev, 1)
                act.wait_ge(x_gain, tile + 1)
                nc.scalar.copy(Hh[:, :, cols], GX[tile % 2]).then_inc(h_hi, 1)
                if tile == NT - 2:
                    split_hi(act, 0, 0, 1)
            act.wait_ge(eps_set, 2)
            act.wait_ge(x_sq, NT)
            rms_root(act, SSQ[:, :])
            rms_spread(act, 0)
            in_act(act)
            recurrence(act, chunk_act, prep_act_step, lambda e, o, l: out_act_step(e, o, l))
            mixed_split(act, True)
            split_hi(act, 0, 13, 28)
            residual_act(act, "out", 8)
            norm_act(act, "mlp0", V_MLP)
            with act.Fori(0, NG) as g:
                mlp_act(act, 0, g)
            norm_act(act, "qkv", V_MIX + KD)
            qkv_act(act)
            attention(act, round_act)
            attn_split(act, True)
            residual_act(act, "wo", 8)
            norm_act(act, "mlp1", V_MLP + KD)
            with act.Fori(0, NG - 1) as g:
                mlp_act(act, 1, g)
            mlp_act(act, 1, NG - 1, last=True)
            residual_done(act, "end")
            with act.Fori(0, NT // 2) as i:
                for j in two:
                    act.wait_ge(out_tr, 2 * i + j + 1)
                    waited(act, "act")
                    nc.scalar.copy(XT8[:, j], X[:, :, bass.ds(i * 256 + j * P, P)]).then_inc(out_st, 1)

        @block.tensor
        def _(t):
            t.sem_inc(acc_done, 2)
            t.sem_inc(x_tr, 2)
            t.sem_inc(out_tr, 2)
            t.wait_ge(const_in, 16 * N_EARLY)
            nc.tensor.transpose(PS[:, 7, 0:V_ROWS], VROW[0:V_ROWS, :], ident[0:V_ROWS, 0:V_ROWS]).then_inc(vec_t, 1)
            for tile in range(NT):
                t.wait_ge(x_in[tile % 4], 16 * (tile // 4) + 16)
                t.wait_ge(x_ev, tile + 1)
                for k in range(KD):
                    m = nc.tensor.transpose(x_banks(tile)[:, k], XIN[:, tile % 4, k], ident)
                m.then_inc(x_tr, 1)
            t.wait_ge(h_lo, NT)
            product(t, 0, 0, 0, 0, 8, P, 0, Hh, Hl, between=norm_between(t, "in"))
            product(t, 1, 1, 0, 1, 8, P, 0, Hh, Hl)
            with t.Fori(1, 13) as i:
                for j in two:
                    product(t, j, j, i, 2 * i + j, 8, P, 0, Hh, Hl)
            t.wait_ge(late_in, 16 * N_LATE)
            recurrence(t, chunk_pe, prep_pe_step, lambda e, o, l: out_pe_step(e, o, l))
            dense_pe(t, "out", 8, order=OUT_ORDER)
            mlp_pe(t, 0)
            qkv_pe(t)
            t.wait_ge(k2_in, 32)
            score_products(t, 0, 0, 0)
            attention(t, round_pe)
            dense_pe(t, "wo", 8)
            mlp_pe(t, 1)
            with t.Fori(0, NT // 2) as i:
                for j in two:
                    t.wait_ge(out_st, 2 * i + j + 1)
                    t.wait_ge(out_ev, 2 * i + j + 1)
                    for k in range(KD):
                        m = nc.tensor.transpose(bank(2 * j + k // 4)[:, k % 4], XT8[:, j, k], ident)
                    m.then_inc(out_tr, 1)

        @block.vector
        def _(dve):
            dve.sem_inc(w_lo, 2)
            for j in two:
                dve.sem_inc(acc_free[j], 1)
            dve.sem_inc(x_ev, 2)
            dve.sem_inc(out_ev, 2)
            dve.sem_inc(conv_done, 1)
            dve.sem_inc(shift_done, 2)
            dve.sem_inc(act_lo, 1)
            dve.sem_inc(qk_norm, 2)
            dve.wait_ge(vec_t, 1)
            nc.vector.tensor_copy(VT[:, 0:V_ROWS], PS[:, 7, 0:V_ROWS]).then_inc(vec_ok, 1)
            dve.wait_ge(vec_ok, 1)
            nc.vector.tensor_scalar(VT[:, V_QS:V_QS + 1], VT[:, V_QG:V_QG + 1], float(RH) ** -0.5, None,
                                    ALU.mult).then_inc(vec_ok, 1)
            dve.wait_ge(vec_ok, 2)
            for tile in range(NT + 1):
                if tile < NT:
                    dve.wait_ge(x_ev, tile + 3)
                    if tile >= 2:
                        dve.wait_ge(h_lo, tile - 1)
                    nc.vector.tensor_tensor(GX[tile % 2], X[:, :, tile * P:tile * P + P], vb(V_MIX, KD), ALU.mult).then_inc(x_gain, 1)
                if tile == NT:
                    split_lo(dve, 0, 0)
                if tile:
                    dve.wait_ge(h_hi, tile)
                    cols = slice((tile - 1) * P, tile * P)
                    nc.vector.tensor_tensor(Hl[:, :, cols], GX[(tile - 1) % 2], Hh[:, :, cols].bitcast(F32),
                                            ALU.subtract).then_inc(h_lo, 1)
            rms_invert(dve, 0)
            in_dve(dve)
            dve.wait_ge(late_in, 16 * N_LATE)
            recurrence(dve, chunk_dve, prep_dve_step, lambda e, o, l: out_dve_step(e, o, 1, l))
            mixed_split(dve, False)
            split_lo(dve, 0, 26)
            residual_dve(dve, "out", 8)
            norm_dve(dve, "mlp0", V_MLP)
            with dve.Fori(0, NG) as g:
                mlp_dve(dve, 0, g)
            norm_dve(dve, "qkv", V_MIX + KD)
            qkv_dve(dve)
            nc.vector.tensor_scalar(NSNK[:, :], SNK[:, :], -1.0, None, ALU.mult).then_inc(nsnk_ok, 1)
            dve.wait_ge(nsnk_ok, 1)
            attention(dve, round_dve)
            attn_split(dve, False)
            residual_dve(dve, "wo", 8)
            norm_dve(dve, "mlp1", V_MLP + KD)
            with dve.Fori(0, NG - 1) as g:
                mlp_dve(dve, 1, g)
            mlp_dve(dve, 1, NG - 1, last=True)
            with dve.Fori(0, NT // 2) as i:
                for j in two:
                    dve.wait_ge(out_tr, 2 * i + j + 3)
                    dve.wait_ge(out_dma[j], 16 * i + 16)
                    for q in two:
                        m = nc.vector.tensor_copy(OT[:, j, 4 * q:4 * q + 4], bank(2 * j + q))
                    m.then_inc(out_ev, 1)


_INS = ["x", "norm_mix", "norm_mlp", "mlp_up", "mlp_down", "w_in_ab", "conv_w", "shift_mu", "w0", "w_decay2",
        "a0", "w_aaa2", "w_gate2", "k_k", "k_a", "r_k", "lnx_w", "lnx_b", "w_out_ab", "w_qkv", "q_gain",
        "k_gain", "sinks", "w_o"]


def kernel(**inputs):
    import concourse.bacc as bacc
    from concourse.bass_utils import run_bass_kernel_spmd

    nc = bacc.Bacc("TRN2", target_bir_lowering=False, num_devices=1)
    arrays, args = {}, {}
    for name in _INS + ["consts"]:
        a = shape_constants() if name == "consts" else np.ascontiguousarray(inputs[name])
        arrays[f"in_{name}"] = a
        args[name] = nc.dram_tensor(f"in_{name}", a.shape, mybir.dt.from_np(a.dtype), kind="ExternalInput").ap()
    args["out"] = nc.dram_tensor("out_0", (1, S, D), F32, kind="ExternalOutput").ap()
    hybrid_trunk(nc, **args)
    r = run_bass_kernel_spmd(nc, [arrays], core_ids=[0])
    return r.results[0]["out_0"]
```

```python
from contextlib import ExitStack

import numpy as np

import concourse.bass as bass
from concourse import mybir
from concourse.alu_op_type import AluOpType as ALU

ACT = mybir.ActivationFunctionType
AXX = mybir.AxisListType.X
F32 = mybir.dt.float32
F32R = mybir.dt.float32r

P = 128
D = 1024
S = 1024
KD = D // P
HALF = 512
NT = S // P
RH = 64
NP_ = 4
KAPPA = 0.6065306597126334
EPS = 1e-6
LNX_EPS = 64e-5
LEVELS = 6
NQ, NKV = 16, 2
WIN = 192
GF = 4
NG = 4096 // P // GF

C_ID, C_BLK, C_ONE, C_MU, C_MX, C_M0, C_RST, C_DIST = 0, 128, 256, 384, 640, 1408, 1536, 2048
C_END = C_DIST + 2 * WIN

V_MIX, V_MLP, V_MU, V_W0, V_A0, V_KK, V_KA, V_RK, V_LW, V_LB, V_CW, V_QG, V_KG = (
    0, 16, 32, 46, 50, 54, 58, 62, 66, 70, 74, 86, 87)
V_ROWS = 88
V_QS = 88

STAGE = {"in": (0, 0), "out": (26, 26), "mlp0": (34, 34), "qkv": (98, 130), "wo": (108, 140),
         "mlp1": (116, 148)}
A_END = 148 + 96
N_EARLY = 15
N_LATE = 5
H_FILL = {"in": 0, "out": 1, "mlp0": 2, "qkv": 3, "wo": 4, "mlp1": 5}


def shape_constants():
    c = np.zeros((P, C_END), np.float32)
    i = np.arange(P)
    row, col = i[:, None], i[None, :]
    c[:, C_ID:C_ID + P] = row == col
    c[:, C_BLK:C_BLK + P] = row // RH == col // RH
    c[:, C_ONE:C_ONE + P] = 1.0
    c[:, C_MU:C_MU + P] = row < col
    c[:, C_MU + P:C_MU + 2 * P] = row <= col
    for k in range(LEVELS):
        b = 2 << k
        c[:, C_MX + k * P:C_MX + (k + 1) * P] = (
            (row // (2 * b) == col // (2 * b)) & (row % (2 * b) < b) & (col % (2 * b) >= b))
    c[:, C_M0:C_M0 + P] = (row % 2 == 0) & (col == row + 1)
    c[:, C_RST:C_RST + 4 * P] = (np.arange(4 * P) % P != 0)[None, :]
    key = np.arange(WIN)[None, :]
    dist = np.abs(row - key + RH).astype(np.float32)
    seen = (key // RH == row // RH) | (key // RH == row // RH + 1)
    c[:, C_DIST:C_DIST + WIN] = np.where(seen, dist, np.float32(1e34))
    first = seen & (key >= RH)
    c[:, C_DIST + WIN:C_END] = np.where(first, dist, np.float32(1e34))
    return c


def hybrid_trunk(nc, x, norm_mix, norm_mlp, mlp_up, mlp_down, w_in_ab, conv_w, shift_mu, w0,
                 w_decay2, a0, w_aaa2, w_gate2, k_k, k_a, r_k, lnx_w, lnx_b, w_out_ab, w_qkv,
                 q_gain, k_gain, sinks, w_o, consts, out):
    ya_dram = nc.dram_tensor("ya_spill", (4, P, S), F32).ap()
    base = 16512

    def at(name, shape, kb, dt=F32):
        return nc.alloc_sbuf_tensor_at(name, [P] + shape, dt, offset=base + int(kb * 1024))

    X = at("residual", [KD, S], 0)
    Hh = at("h_hi", [KD, S], 32, F32R)
    Hl = at("h_lo", [KD, S], 64, F32R)
    WR = at("w_raw", [2, 1024], 96)
    WH = at("w_hi", [2, 1024], 104, F32R)
    WL = at("w_lo", [2, 1024], 112, F32R)
    ACh = at("mlp_hi", [GF, S], 120, F32R)
    ACl = at("mlp_lo", [GF, S], 136, F32R)
    RKV = at("rkv", [12, S], 120)
    WA = at("decay_aaa_in", [S], 168)
    GL = at("gate_in", [S], 172)
    ST0 = at("stage0", [S + 4], 176)
    ST1 = at("stage1", [S + 4], 180.25)
    ST2 = at("stage2", [S + 4], 184.5)
    CON = at("constants", [C_END], 189)
    LOR = at("lora_w", [3, 4 * P], 197)
    VT = at("vectors", [96], 203)
    SNK = at("sink_cols", [NQ], 203.375)
    NSNK = at("minus_sinks", [NQ], 203.4375)
    T6 = at("prep_t6", [4, P], 203.5)
    GS = at("decay_ends", [2, 2, 4], 205.5)
    GSR = at("decay_ends_raw", [2, 4], 205.625)
    T7 = at("prep_t7", [4, P], 205.75)
    NR = at("key_norms", [2 * NP_], 188.84375)
    VR = at("group_norms", [2 * NP_], 188.875)
    RI = at("rms_inverse", [S], 203.5)
    SSQ = at("sum_squares", [NT], 188.625)
    RIV = at("rms_inverse_tokens", [2 * NT], 188.6875)
    XIN = at("x_in_tile", [4, KD, P], 120)
    VROW = at("vector_rows", [P], 136)
    AR = at("a_r_dec", [2, 4, 2, P], 32)
    ARP = at("a_r_zero_padded", [4, 2, 2, P], 96)
    BK = at("b_k_dec", [2, 2, 4, P], 40)
    VC = at("v_chunk", [2, 4, P], 48)
    BON = at("bonus", [2, 4, P], 52)
    G1M = at("decay_in_mask", [2, 4, P], 56)
    TOK = at("token_major", [4, 4 * P], 60)
    MTRB = at("mt_rb", [8, 2, P], 68)
    NTRK = at("nt_rk", [8, 2, P], 76)
    TI = at("tri_inv", [8, P], 84)
    TIT = at("tri_inv_t", [8, P], 88)
    WT = at("w_t", [4, P], 92)
    ZZ = at("z_part", [4 * P], 94)
    YL = at("y_level", [8, P], 176)
    XL = at("x_level", [8, P], 180)
    SS = at("state", [4, P], 184)
    SP_ = at("state_in", [4, P], 186)
    NV = at("nv_part", [4 * P], 104)
    UU = at("u_part", [4 * P], 106)
    T0, T1, T2, T3, T4 = (at(f"prep_t{n}", [4, P], 108 + 2 * n) for n in range(5))
    T5 = at("prep_t5", [4, P], 118)
    WAG = at("lora_chunk", [P], 188)
    Q = at("q_then_o", [KD, S], 120)
    K2 = at("k_zero_padded", [NKV, 2, S + RH], 152)
    VP = at("v_padded", [S + 2 * RH], 169.5)
    QR = at("head_roots", [2 * NT], 188.75)
    SQ = at("squares", [S], 198.5)
    QST = at("q_tile", [2, KD, P], 32)
    VST = at("v_window", [2, 2, P], 43)
    VTOK = at("v_token_major", [9, P], 190.5)
    PP = at("probs", [2, NQ, WIN], 50)
    PTA = at("probs_t_a", [NQ, P], 74)
    PTB = at("probs_t_b", [NQ, P], 82)
    STA = at("softmax_stats", [2, 6, NQ], 90)

    with ExitStack() as ctx:
        PS = ctx.enter_context(nc.psum_tensor("ps", [P, 8, HALF], F32))

        def sem(name):
            return ctx.enter_context(nc.semaphore(name))

        w_load = [sem("w_load0"), sem("w_load1")]
        w_hi, w_lo = sem("w_hi_done"), sem("w_lo_done")
        acc_done = sem("acc_done")
        acc_free = [sem("acc_free0"), sem("acc_free1")]
        h_hi, h_lo = sem("h_hi_done"), sem("h_lo_done")
        ident_in, const_in, late_in = sem("ident_in"), sem("const_in"), sem("late_const_in")
        x_in = [sem(f"x_in{j}") for j in range(4)]
        lora_zero, dist_in = sem("lora_pads_zero"), sem("distances_in")
        vec_t, vec_ok, eps_set = sem("vectors_transposed"), sem("vectors_ready"), sem("eps_set")
        pads_zero, conv_zero, shift_zero = sem("attn_pads_zero"), sem("conv_zero"), sem("shift_zero")
        x_tr, x_ev, x_gain = sem("x_transposed"), sem("x_evacuated"), sem("x_gained")
        block = ctx.enter_context(nc.Block())

        seq = {"act": sem("act_waited"), "pool": sem("pool_waited"), "dve": sem("dve_waited")}

        def waited(engine, name):
            engine.sem_inc(seq[name], 1)

        ident = CON[:, C_ID:C_ID + P]
        blk = CON[:, C_BLK:C_BLK + P]
        ones = CON[:, C_ONE:C_ONE + P]

        def vb(row, n=4, m=P):
            return VT[:, row:row + n].unsqueeze(2).to_broadcast([P, n, m])

        def over(ap, n):
            return ap.unsqueeze(1).to_broadcast([P, n, ap.shape[1]])

        def acc(a_slot, half=None):
            return (PS[:, 2 * a_slot:2 * a_slot + 2, :] if half is None
                    else PS[:, 2 * a_slot + half, :])

        def acc2(a_slot):
            return acc(a_slot).rearrange("p b n -> p (b n)")

        win = w_in_ab[0].rearrange("(k p) n -> p k n", p=P)
        wout = w_out_ab[0].rearrange("(k p) n -> p k n", p=P)
        wqkv = w_qkv[0].rearrange("(k p) n -> p k n", p=P)
        wo = w_o[0].rearrange("(k p) n -> p k n", p=P)
        wup = [mlp_up[l].rearrange("(k p) n -> p k n", p=P) for l in range(2)]
        wdn = [mlp_down[l].rearrange("(g k p) n -> g p k n", k=GF, p=P) for l in range(2)]

        def load_unit(sp, slot, u, src, k=8):
            sp.wait_ge(w_lo, u + 1)
            sp.dma_start(WR[:, slot].rearrange("p (k n) -> p k n", k=k), src).then_inc(w_load[slot], 16)

        def split_hi(act, slot, n, need):
            act.wait_ge(w_load[slot], 16 * n + 16)
            act.wait_ge(acc_done, need)
            nc.scalar.copy(WH[:, slot], WR[:, slot]).then_inc(w_hi, 1)

        def split_lo(dve, slot, u):
            dve.wait_ge(w_hi, u + 1)
            nc.vector.tensor_tensor(WL[:, slot], WR[:, slot], WH[:, slot].bitcast(F32),
                                    ALU.subtract).then_inc(w_lo, 1)

        def load_stage(sp, name, src, units):
            u0, _ = STAGE[name]
            with sp.Fori(0, units // 2) as i:
                for j in range(2):
                    load_unit(sp, j, u0 + 2 * i + j, src[:, :, bass.ds((2 * i + j) * P, P)])

        def load_mlp(sp, l):
            u0, _ = STAGE[f"mlp{l}"]
            with sp.Fori(0, NG) as g:
                for j in range(4):
                    load_unit(sp, j % 2, u0 + 8 * g + j, wup[l][:, :, bass.ds(g * 512 + j * P, P)])
                for d in range(4):
                    src = wdn[l][bass.ds(g, 1)].rearrange("a p k n -> p (a k) n")
                    load_unit(sp, d % 2, u0 + 8 * g + 4 + d, src[:, :, 256 * d:256 * d + 256], k=4)

        def product(t, slot, a_slot, a_half, u, nk, step, off, xh, xl, ready=None, new_unit=True, between=None):
            if new_unit:
                t.wait_ge(w_lo, u + 3)
            t.wait_ge(acc_free[a_slot], a_half + 1)
            for k in range(nk):
                if between and k in between:
                    between[k]()
                if ready is not None:
                    t.wait_ge(ready[0], ready[1] + k + 1)
                w_h = WH[:, slot, k * step + off:k * step + off + P]
                w_l = WL[:, slot, k * step + off:k * step + off + P]
                for ww, xx in ((w_h, xh), (w_h, xl), (w_l, xh)):
                    first, last = k == 0 and ww is w_h and xx is xh, k == nk - 1 and ww is w_l
                    for half in range(2):
                        m = nc.tensor.matmul(acc(a_slot, half), ww,
                                             xx[:, k, half * HALF:(half + 1) * HALF],
                                             start=first, stop=last)
            m.then_inc(acc_done, 1)

        def dense_pe(t, name, units):
            u0, a0_ = STAGE[name]
            fill = H_FILL[name]
            with t.Fori(0, units // 2) as i:
                for j in range(2):
                    product(t, j, j, a0_ // 2 + i, u0 + 2 * i + j, 8, P, 0, Hh, Hl,
                            ready=(h_lo, 8 * fill) if j == 0 else None)

        act_lo = sem("mlp_lo_done")
        out_tr, out_st, out_dma = sem("out_transposed"), sem("out_staged"), [sem("out_dma0"), sem("out_dma1")]

        def out_transposes(t, k):
            chunk_done(t, "end", k)
            t.wait_ge(out_st, k + 1)
            for tile in range(NT):
                m = nc.tensor.transpose(bank(4 + 2 * (k % 2) + tile // 4)[:, tile % 4],
                                        X[:, k, tile * P:tile * P + P], ident)
            m.then_inc(out_tr, 1)

        acc_banks67 = PS[:, 6:8, :].rearrange("p b n -> p (b n)")

        def mlp_pe(t, l):
            u0, a0_ = STAGE[f"mlp{l}"]

            def group(g, between, after=None):
                for j in range(4):
                    product(t, j % 2, j % 2, a0_ // 2 + 6 * g + j // 2, u0 + 8 * g + j, 8, P, 0,
                            Hh, Hl, ready=(h_lo, 8 * H_FILL[f"mlp{l}"]) if j == 0 else None,
                            between=between if j == 0 else None)
                for m in range(8):
                    product(t, m // 2 % 2, m % 2, a0_ // 2 + 6 * g + 2 + m // 2, u0 + 8 * g + 4 + m // 2,
                            GF, 256, P * (m % 2), ACh, ACl,
                            ready=(act_lo, 4 * NG * l + 4 * g + 1) if m == 0 else None,
                            new_unit=m % 2 == 0,
                            between={2: lambda m=m: after(t, m - 1)} if after and m else None)

            group(0, norm_between(t, f"mlp{l}"))
            with t.Fori(1, NG - l) as g:
                group(g, None)
            if l == 1:
                group(NG - 1, None, out_transposes)
                out_transposes(t, KD - 1)

        sq_pool, sq_last, ss_add = sem("squares_pool"), sem("last_square"), sem("squares_added")
        ss_tok, rms_done, rinv_done = sem("sum_squares_tokens"), sem("rms_done"), sem("rms_inverted")
        rinv_tr, ri_done = sem("rms_inverse_transposed"), sem("rms_inverse_ready")
        x_sq = sem("x_squared")
        NORMS = {"in": 0, "mlp0": 1, "qkv": 2, "mlp1": 3}

        def chunk_done(engine, name, k):
            a_next = STAGE[name][1] if name in STAGE else A_END
            engine.wait_ge(acc_free[k % 2], (a_next - 8 + k) // 2 + 2)

        def residual_done(engine, name):
            chunk_done(engine, name, KD - 1)

        def norm_pool(pool, name):
            base = 13 * (NORMS[name] - 1)
            TT = nc.gpsimd.tensor_tensor
            for k in range(KD - 1):
                chunk_done(pool, name, k)
                if k:
                    pool.wait_ge(sq_pool, base + 2 * k - 1)
                TT((ST1 if k else ST2)[:, 0:S], X[:, k], X[:, k], ALU.mult).then_inc(sq_pool, 1)
                if k:
                    pool.wait_ge(sq_pool, base + 2 * k)
                    TT(ST2[:, 0:S], ST2[:, 0:S], ST1[:, 0:S], ALU.add).then_inc(sq_pool, 1)

        def norm_act(act, name, row):
            n, f = NORMS[name], H_FILL[name]
            act.wait_ge(acc_done, STAGE[name][1] + 2)
            for k in range(KD):
                chunk_done(act, name, k)
                nc.scalar.activation(Hh[:, k], X[:, k], ACT.Copy, scale=VT[:, row + k:row + k + 1]).then_inc(h_hi, 1)
                if k == 0:
                    chunk_done(act, name, KD - 1)
                    nc.scalar.activation(ST0[:, 0:S], X[:, KD - 1], ACT.Square).then_inc(sq_last, 1)
                if k == 3:
                    act.wait_ge(ss_tok, n)
                    rms_root(act, PS[:, 4, 0:NT])
            rms_spread(act, n)

        def rms_root(act, sums):
            nc.scalar.activation(RIV[:, 0:NT], sums, ACT.Sqrt, bias=VT[:, 90:91], scale=1.0 / D).then_inc(rms_done, 1)

        def rms_spread(act, n):
            act.wait_ge(rinv_tr, n + 1)
            nc.scalar.copy(RI[:, :], PS[:, 4:6, :].rearrange("p b n -> p (b n)")).then_inc(ri_done, 1)

        def rms_invert(dve, n):
            dve.wait_ge(rms_done, n + 1)
            nc.vector.reciprocal(RIV[:, 0:NT], RIV[:, 0:NT]).then_inc(rinv_done, 1)

        def norm_dve(dve, name, row):
            n, f = NORMS[name], H_FILL[name]
            for k in range(KD):
                dve.wait_ge(h_hi, 8 * f + k + 1)
                nc.vector.scalar_tensor_tensor(Hl[:, k], X[:, k], VT[:, row + k:row + k + 1],
                                               Hh[:, k].bitcast(F32), ALU.mult, ALU.subtract).then_inc(h_lo, 1)
                if k == 0:
                    dve.wait_ge(sq_last, n)
                    dve.wait_ge(sq_pool, 13 * n)
                    nc.vector.tensor_tensor(ST2[:, 0:S], ST2[:, 0:S], ST0[:, 0:S], ALU.add).then_inc(ss_add, 1)
                if k == 4:
                    rms_invert(dve, n)
            dve.wait_ge(ri_done, n + 1)

        def norm_between(t, name):
            n = NORMS[name]

            def sums():
                t.wait_ge(ss_add, n)
                for tile in range(NT):
                    m = nc.tensor.matmul(PS[:, 4, tile:tile + 1], ST2[:, tile * P:tile * P + P], ones[:, 0:1],
                                         start=True, stop=True)
                m.then_inc(ss_tok, 1)

            def spread():
                t.wait_ge(rinv_done, n + 1)
                for tile in range(NT):
                    m = nc.tensor.transpose(bank(4 + tile // 4)[:, tile % 4],
                                            RIV[:, tile:tile + 1].to_broadcast([P, P]), ident)
                m.then_inc(rinv_tr, 1)

            return {5: spread} if name == "in" else {2: sums, 5: spread}

        def bank(n):
            return PS[:, n, :].rearrange("p (a m) -> p a m", m=P)

        def scale_out(dve, dst, slot):
            nc.vector.tensor_tensor(dst, acc2(slot), RI[:, :], ALU.mult).then_inc(acc_free[slot], 1)

        def h_lo_split(dve, f, k, src, pos=None):
            pos = k if pos is None else pos
            dve.wait_ge(h_hi, 8 * f + pos + 1)
            nc.vector.tensor_tensor(Hl[:, k], src, Hh[:, k].bitcast(F32), ALU.subtract).then_inc(h_lo, 1)

        relu_sq, act_hi = sem("relu_squared"), sem("mlp_hi_done")

        def mlp_act(act, l, g, last=False):
            u0, a0_ = STAGE[f"mlp{l}"]
            ag, n = a0_ + 12 * g, 4 * NG * l + 4 * g
            need = [None, ag + 2, ag + 3, ag + 4, ag + 5, ag + 6, ag + 8, ag + 10, ag + 13]
            for j in range(8):
                if not (last and j == 7):
                    split_hi(act, (j + 1) % 2, u0 // 2 + 4 * g + (j + 1) // 2, need[j + 1])
                if j < 4:
                    act.wait_ge(acc_free[j % 2], a0_ // 2 + 6 * g + j // 2 + 2)
                    nc.scalar.activation(ST1[:, 0:S], ST0[:, 0:S], ACT.Square).then_inc(relu_sq, 1)
                    act.wait_ge(relu_sq, n + j + 1)
                    nc.scalar.copy(ACh[:, j], ST1[:, 0:S]).then_inc(act_hi, 1)

                if last and j == 5:
                    out_copy(act, 0)
                    out_copy(act, 1)

        def out_copy(act, k):
            j = k % 2
            act.wait_ge(out_tr, k + 1)
            act.wait_ge(out_dma[j], 16 * (k // 2) + 16)
            nc.scalar.copy(OT[:, j].rearrange("p t n -> p (t n)"),
                           PS[:, 4 + 2 * j:6 + 2 * j, :].rearrange("p b n -> p (b n)")).then_inc(out_st, 1)

        def mlp_dve(dve, l, g, last=False):
            u0, a0_ = STAGE[f"mlp{l}"]
            ag, n = a0_ + 12 * g, 4 * NG * l + 4 * g
            for j in range(8):
                if not (last and j == 7):
                    split_lo(dve, (j + 1) % 2, u0 + 8 * g + j + 1)
                if j < 4:
                    dve.wait_ge(acc_done, ag + j + 3)
                    nc.vector.scalar_tensor_tensor(ST0[:, 0:S], acc2(j % 2), 0.0, RI[:, :], ALU.max, ALU.mult)\
                        .then_inc(acc_free[j % 2], 1)
                    dve.wait_ge(act_hi, n + j + 1)
                    nc.vector.tensor_tensor(ACl[:, j], ST1[:, 0:S], ACh[:, j].bitcast(F32),
                                            ALU.subtract).then_inc(act_lo, 1)
                else:
                    for m in (2 * (j - 4), 2 * (j - 4) + 1):
                        dve.wait_ge(acc_done, ag + 4 + m + 3)
                        nc.vector.tensor_tensor(X[:, m], X[:, m], acc2(m % 2), ALU.add)\
                            .then_inc(acc_free[m % 2], 1)

        def residual_act(act, name, units):
            u0, a0_ = STAGE[name]
            with act.Fori(0, units // 2) as i:
                for j in range(2):
                    split_hi(act, 1 - j, u0 // 2 + i + j, a0_ + 2 * i + j + 2)

        def residual_dve(dve, name, units):
            u0, a0_ = STAGE[name]
            with dve.Fori(0, units // 2) as i:
                for j in range(2):
                    split_lo(dve, 1 - j, u0 + 2 * i + j + 1)
                    dve.wait_ge(acc_done, a0_ + 2 * i + j + 3)
                    xk = X[:, bass.ds(2 * i + j, 1), :]
                    nc.vector.tensor_tensor(xk, xk, acc2(j).unsqueeze(1), ALU.add).then_inc(acc_free[j], 1)

        conv_step, conv_done, ya_out = sem("conv_step"), sem("conv_done"), sem("ya_out")
        gl_free = sem("conv_output_left")
        shift_diff, shift_done = sem("shift_diff"), sem("shift_done")
        lora_act = sem("lora_inputs_activated")

        def in_act(act):
            def splits(first, end):
                with act.Fori(first, end) as i:
                    for j in range(2):
                        split_hi(act, 1 - j, i + j, 2 * i + j + 2)

            splits(0, 7)
            act.wait_ge(shift_done, 2 + 2)
            nc.scalar.activation(WA[0:RH, :], WA[0:RH, :], ACT.Tanh).then_inc(lora_act, 1)
            nc.scalar.activation(GL[:, :], GL[:, :], ACT.Sigmoid).then_inc(lora_act, 1)
            splits(7, 12)
            split_hi(act, 1, 12, 26)

        def in_dve(dve):
            dve.wait_ge(h_lo, NT)
            nc.vector.memset(ST2[:, 0:2], 0.0).then_inc(conv_zero, 1)
            dve.wait_ge(conv_zero, 1)
            dve.wait_ge(ri_done, 1)
            with dve.Fori(0, 2) as i:
                for q in range(2):
                    for r in range(3):
                        j = 3 * q + r
                        split_lo(dve, (j + 1) % 2, 6 * i + j + 1)
                        dve.wait_ge(acc_done, 6 * i + j + 3)
                        dve.wait_ge(conv_done, 2 * i + q + 1)
                        scale_out(dve, (ST0[:, 0:S], ST1[:, 0:S], WA[:, 0:S])[r], j % 2)
                    g = 2 * i + q
                    w = VT[:, bass.ds(V_CW + g, 1)], VT[:, bass.ds(V_CW + 4 + g, 1)], \
                        VT[:, bass.ds(V_CW + 8 + g, 1)]
                    dve.wait_ge(acc_free[q], 3 * i + q + 3)
                    cu = ST2
                    nc.vector.tensor_tensor(cu[:, 2:S + 2], ST1[:, 0:S], WA[:, :], ALU.mult).then_inc(conv_step, 1)
                    dve.wait_ge(conv_step, 4 * g + 1)
                    dve.wait_ge(gl_free, g + 1)
                    nc.vector.tensor_scalar(GL[:, :], cu[:, 2:S + 2], w[2], None, ALU.mult).then_inc(conv_step, 1)
                    for n in (1, 0):
                        dve.wait_ge(conv_step, 4 * g + 3 - n)
                        nc.vector.scalar_tensor_tensor(GL[:, :], cu[:, n:S + n], w[n], GL[:, :], ALU.mult,
                                                       ALU.add).then_inc(conv_step, 1)
                    dve.wait_ge(conv_step, 4 * g + 4)
                    nc.vector.tensor_tensor(GL[:, :], GL[:, :], ST0[:, 0:S], ALU.mult).then_inc(conv_done, 1)
            dve.wait_ge(conv_done, 5)
            nc.vector.memset(ST0[:, 0:1], 0.0).then_inc(shift_zero, 1)
            nc.vector.memset(ST1[:, 0:1], 0.0).then_inc(shift_zero, 1)
            dve.wait_ge(shift_zero, 2)
            split_lo(dve, 1, 13)
            dve.wait_ge(gl_free, 5)
            shift(dve, 0, 12, 0, 6, WA[:, :].unsqueeze(1))
            split_lo(dve, 0, 14)
            shift(dve, 1, 13, 1, 6, GL[:, :].unsqueeze(1))

            def rkv_shift(i, j):
                shift(dve, 2 * i + (2 + j), 2 * i + j, j, i + 7, RKV[:, bass.ds(2 * i + j, 1), :])

            with dve.Fori(0, 5) as i:
                for j in range(2):
                    split_lo(dve, 1 - j, 2 * i + (15 + j))
                    rkv_shift(i, j)
            split_lo(dve, 1, 25)
            for j in range(2):
                rkv_shift(5, j)

        def shift(dve, n, m, slot, half, dst):
            st = (ST0, ST1)[slot]
            dve.wait_ge(acc_done, 2 * half + (slot + 3))
            dve.wait_ge(shift_done, n + 1)
            scale_out(dve, st[:, 1:S + 1], slot)
            dve.wait_ge(acc_free[slot], half + 2)
            nc.vector.tensor_tensor(dst, st[:, 0:S].unsqueeze(1), st[:, 1:S + 1].unsqueeze(1), ALU.subtract)\
                .then_inc(shift_diff, 1)
            dve.wait_ge(shift_diff, n + 1)
            mu = VT[:, bass.ds(V_MU + m, 1)]
            nc.vector.scalar_tensor_tensor(dst, dst, mu, st[:, 1:S + 1].unsqueeze(1), ALU.mult, ALU.add)\
                .then_inc(shift_done, 1)

        class Track:

            def __init__(self, name, steps):
                self.sem, self.steps, self.next = sem(name), steps, 0

            def done(self, instruction, step):
                assert self.steps[self.next] == step, (self.steps[self.next], step)
                self.next = (self.next + 1) % len(self.steps)
                instruction.then_inc(self.sem, 1)

            def wait(self, engine, chunk, step):
                engine.wait_ge(self.sem, len(self.steps) * chunk + (self.steps.index(step) + 1))

        two = (0, 1)
        prep_pool = Track("prep_pool", ["wag", "vc", "g1m", "rk", "rk2", "lb"])
        prep_pe = Track("prep_pe", ["zw", "za", "n2", "nt", "bon"])
        prep_act = Track("prep_act", ["sq", "sw", "a", "g", "e1", "e2", "e1x", "nrm", "spread", "pad0", "pad1"])
        prep_dve = Track("prep_dve", ["kkr", "zws", "zas", "scan", "mid", "end", "d", "dx", "ka", "k2", "max", "rcp",
                                      "r_dec", "kkn", "a_dec", "b0", "b_dec", "k_dec", "bon"])
        solve_pe = Track("solve_pe", ["tok0", "tok1", "tok2", "tok3", "p1_0", "p1_1", "p2_0", "p2_1", "t0_0", "nv",
                                      "t0_1"]
                         + [f"{w}{k}_{b}" for k in range(LEVELS) for w, b in
                            (("y", 0), ("y", 1), ("dt", 0), ("dtt", 0), ("dt", 1), ("dtt", 1))
                            if not (w == "dt" and k == LEVELS - 1)]
                         + ["wt", "z", "u", "s", "o"])
        solve_act = Track("solve_act", ["tok0", "tok1", "tok2", "tok3", "t0_0", "nv", "t0_1"]
                          + [f"y{k}_{b}" for k in range(LEVELS) for b in two] + ["wt", "z", "o"])
        solve_dve = Track("solve_dve", ["m0", "m1", "n0", "n1", "x0_0", "x0_1", "s_in"]
                          + [f"{w}{k}_{b}" for k in range(LEVELS) for b in two for w in ("t", "tt")
                             if not (w == "t" and k == LEVELS - 1)] + ["u", "s1", "s"])
        solve_pool = Track("solve_pool", ["i0", "tt_0", "i1", "tt_1"]
                           + [f"x{k}_{b}" for k in range(1, LEVELS) for b in two])
        out_pe = Track("out_pe", ["mean", "var", "vt", "gate"])
        out_act = Track("out_act", ["sq", "sd", "spread"])
        out_dve = Track("out_dve", ["d", "rcp", "m1", "m4", "yb"])
        out_pool = Track("out_pool", ["m2"])
        state_zero, ar_zero = sem("state_zero"), sem("a_r_pads_zero")

        def part(c, first):
            return RKV[:, first:first + 4, bass.ds(c * P, P)]

        def heads(ap, b):
            return ap[:, 4 * b:4 * b + 4]

        HEAD = ("before the masks", "between the masks", "after the masks")
        LEVEL = tuple((k, b) for k in range(LEVELS) for b in two)
        PLACES = HEAD + LEVEL[0:2] + (0,) + LEVEL[2:4] + (1, "root") + sum(
            ((k,) + LEVEL[2 * k:2 * k + 2] if k != 4 else LEVEL[8:10] + (4,) for k in (2, 3, 4, 5)), ()) + ("end",)
        SQO = ZZ.rearrange("p (a m) -> p a m", m=P)

        def at_start(tile, n):
            return isinstance(tile, int) and tile < n

        def is_first(c):
            return at_start(c, 1)

        def head_sums(ps, src):
            for p in range(NP_):
                m = nc.tensor.matmul(ps[:, 2 * p:2 * p + 2], src[:, p], blk[:, 0:P:RH], start=True, stop=True)
            return m

        def spread_back(ps, src):
            for p in range(NP_):
                m = nc.tensor.transpose(ps[:, p], src[:, p], ident)
            return m

        def by_head(ap, cols):
            return (ap.rearrange("p a (g m) -> p (a g) m", m=RH), cols.unsqueeze(2).to_broadcast([P, 2 * NP_, RH]))

        def prep_pool_step(pool, e, s, place):
            TT = nc.gpsimd.tensor_tensor
            if place == HEAD[0]:
                if not is_first(e):
                    prep_pe.wait(pool, e - 1, "za")
                    waited(pool, "pool")
                prep_pool.done(nc.gpsimd.tensor_copy(WAG[:, :], WA[:, bass.ds(e * P, P)]), "wag")
            if place == 0:
                if is_first(e):
                    pool.wait_ge(shift_done, 2 + 14)
                    nc.gpsimd.memset(SS[:, :], 0.0).then_inc(state_zero, 1)
                    nc.gpsimd.memset(ARP[:, :, :, :], 0.0).then_inc(ar_zero, 1)
                    pool.wait_ge(ar_zero, 1)
                prep_pool.done(nc.gpsimd.tensor_copy(VC[:, s], part(e, 8)), "vc")
            if place == 1:
                prep_act.wait(pool, e, "e1")
                prep_pool.done(TT(G1M[:, s], over(blk, 4), GS[:, s, 0].unsqueeze(2).to_broadcast([P, 4, P]),
                                  ALU.mult), "g1m")
            if place == 2:
                prep_dve.wait(pool, e, "k2")
                waited(pool, "pool")
                prep_pool.done(TT(T7[:, :], T0[:, :], part(e, 0), ALU.mult), "rk")
            if place == 3:
                prep_pool.wait(pool, e, "rk")
                prep_pool.done(TT(T7[:, :], T7[:, :], vb(V_RK), ALU.mult), "rk2")
            if place == "end":
                prep_dve.wait(pool, e, "bon")
                prep_pool.done(TT(BON[:, s], BON[:, s], vb(V_LB), ALU.add), "lb")

        def prep_pe_step(t, e, s, place):
            if place == HEAD[0]:
                prep_pool.wait(t, e, "wag")
                for p in range(4):
                    m = nc.tensor.matmul(bank(7)[:, p], LOR[:, 0, p * P:(p + 1) * P], WAG[:, :],
                                         start=True, stop=True)
                prep_pe.done(m, "zw")
            if place == HEAD[1]:
                prep_dve.wait(t, e, "zws")
                for p in range(4):
                    m = nc.tensor.matmul(bank(7)[:, p], LOR[:, 1, p * P:(p + 1) * P], WAG[:, :],
                                         start=True, stop=True)
                prep_pe.done(m, "za")
            if place == 0:
                prep_dve.wait(t, e, "zas")
                if not is_first(e):
                    solve_act.wait(t, e - 1, "nv")
                prep_act.wait(t, e, "sq")
                prep_pe.done(head_sums(PS[:, 7], T6), "n2")
            if place == 2:
                prep_act.wait(t, e, "spread")
                prep_pe.done(spread_back(bank(7), T6), "nt")
            if place == 4:
                prep_dve.wait(t, e, "kkn")
                prep_pool.wait(t, e, "rk2")
                prep_pe.done(nc.tensor.matmul(bank(7), blk, T7[:, :], start=True, stop=True), "bon")

        def prep_act_step(act, e, s, place):
            A = nc.scalar.activation
            if place == HEAD[0]:
                prep_dve.wait(act, e, "kkr")
                prep_act.done(A(T6[:, :], T5[:, :], ACT.Square), "sq")
                prep_dve.wait(act, e, "zws")
                prep_act.done(A(T0[:, :], T0[:, :], ACT.Sigmoid), "sw")
            if place == HEAD[1]:
                prep_dve.wait(act, e, "zas")
                prep_act.done(A(T1[:, :], T1[:, :], ACT.Sigmoid), "a")
            if place == 0:
                prep_dve.wait(act, e, "dx")
                prep_act.done(A(GS[:, s], GSR[:, :], ACT.Exp, scale=-KAPPA), "g")
                prep_act.done(A(T2[:, :], T3[:, :], ACT.Exp, scale=-KAPPA), "e1")
                prep_act.wait(act, e, "e1")
                prep_act.done(A(T3[:, :], T3[:, :], ACT.Exp, scale=KAPPA), "e2")
            if place == 1:
                prep_act.done(A(T4[:, :], T4[:, :], ACT.Exp, scale=-KAPPA), "e1x")
                prep_pe.wait(act, e, "n2")
                prep_act.done(A(NR[:, :], PS[:, 7, 0:2 * NP_], ACT.Sqrt), "nrm")
            if place == "root":
                prep_dve.wait(act, e, "rcp")
                dst, src = by_head(T6[:, :], NR[:, :])
                prep_act.done(nc.scalar.copy(dst, src), "spread")
            if place == 5:
                prep_dve.wait(act, e, "a_dec")
                if is_first(e):
                    act.wait_ge(ar_zero, 1)
                else:
                    solve_pe.wait(act, e - 1, "p2_1")
                for par in two:
                    rows = slice(RH * par, RH * par + RH)
                    prep_act.done(nc.scalar.copy(ARP[rows, :, par], AR[rows, s]), f"pad{par}")

        def prep_dve_step(dve, e, s, place):
            V, TT, STT = prep_dve, nc.vector.tensor_tensor, nc.vector.scalar_tensor_tensor
            k = part(e, 4)
            if place == HEAD[0]:
                if not is_first(e):
                    V.wait(dve, e - 1, "bon")
                V.done(TT(T5[:, :], k, vb(V_KK), ALU.mult), "kkr")
                prep_pe.wait(dve, e, "zw")
                V.done(TT(T0[:, :], bank(7), vb(V_W0), ALU.add), "zws")
            if place == HEAD[1]:
                prep_pe.wait(dve, e, "za")
                V.done(TT(T1[:, :], bank(7), vb(V_A0), ALU.add), "zas")
            if place == HEAD[2]:
                prep_act.wait(dve, e, "sw")
                flat = lambda ap: ap.rearrange("p a n -> p (a n)")
                V.done(nc.vector.tensor_tensor_scan(flat(T2[:, :]), CON[:, C_RST:C_RST + 4 * P], flat(T0[:, :]),
                                                    0.0, ALU.mult, ALU.add), "scan")
                V.wait(dve, e, "scan")
                V.done(nc.vector.tensor_copy(GSR[:, 0], T2[:, :, 63]), "mid")
                V.wait(dve, e, "mid")
                V.done(TT(GSR[:, 1], T2[:, :, 127], GSR[:, 0], ALU.subtract), "end")
                V.done(TT(T3[:, :], T2[:, :], GSR[:, 0].unsqueeze(2).to_broadcast([P, 4, P]), ALU.subtract), "d")
                V.wait(dve, e, "d")
                V.done(TT(T4[:, :], T3[:, :], T0[:, :], ALU.subtract), "dx")
            if place == (0, 1):
                prep_act.wait(dve, e, "a")
                V.wait(dve, e, "dx")
                V.done(STT(T0[:, :], T1[:, :], -1.0, vb(V_KA), ALU.add, ALU.mult), "ka")
            if place == (1, 0):
                V.wait(dve, e, "ka")
                V.done(STT(T0[:, :], T0[:, :], 1.0, k, ALU.add, ALU.mult), "k2")
            if place == (1, 1):
                prep_act.wait(dve, e, "nrm")
                V.done(nc.vector.tensor_scalar(NR[:, :], NR[:, :], 1e-12, None, ALU.max), "max")
                V.wait(dve, e, "max")
                V.done(nc.vector.reciprocal(NR[:, :], NR[:, :]), "rcp")
            if place == (2, 0):
                V.done(TT(AR[:, s, :, 1], part(e, 0), T2[:, :], ALU.mult), "r_dec")
            if place == (3, 0):
                prep_pe.wait(dve, e, "nt")
                V.done(TT(T5[:, :], T5[:, :], bank(7), ALU.mult), "kkn")
            if place == (3, 1):
                V.wait(dve, e, "kkn")
                V.done(STT(AR[:, s, :, 0], T5[:, :], -1.0, T4[:, :], ALU.mult, ALU.mult), "a_dec")
            if place == (4, 0):
                V.wait(dve, e, "a_dec")
                V.done(TT(T5[:, :], T5[:, :], T1[:, :], ALU.mult), "b0")
            if place == (4, 1):
                V.wait(dve, e, "b0")
                V.done(TT(BK[:, s, 0], T5[:, :], T3[:, :], ALU.mult), "b_dec")
            if place == (5, 0):
                V.done(TT(BK[:, s, 1], T0[:, :], T3[:, :], ALU.mult), "k_dec")
            if place == (5, 1):
                prep_pe.wait(dve, e, "bon")
                prep_pool.wait(dve, e, "vc")
                V.done(TT(BON[:, s], bank(7), VC[:, s], ALU.mult), "bon")

        def out_pe_step(t, o, place):
            if place == 0:
                solve_act.wait(t, o, "o")
                out_pe.done(nc.tensor.matmul(bank(6), blk, part(o, 4), start=True, stop=True), "mean")
            if place == 1:
                out_act.wait(t, o, "sq")
                out_dve.wait(t, o, "d")
                out_pe.done(head_sums(PS[:, 6], SQO), "var")
            if place == 2:
                out_act.wait(t, o, "spread")
                out_pe.done(spread_back(bank(6), SQO), "vt")
            if place == 4:
                out_dve.wait(t, o, "m1")
                for p in range(4):
                    m = nc.tensor.matmul(bank(6)[:, p], LOR[:, 2, p * P:(p + 1) * P], GL[:, bass.ds(o * P, P)],
                                         start=True, stop=True)
                out_pe.done(m, "gate")

        def out_act_step(act, o, place):
            if place == 0:
                out_dve.wait(act, o, "d")
                waited(act, "act")
                out_act.done(nc.scalar.activation(SQO, part(o, 4), ACT.Square), "sq")
            if place == 1:
                out_pe.wait(act, o, "var")
                out_act.done(nc.scalar.activation(VR[:, :], PS[:, 6, 0:2 * NP_], ACT.Sqrt, bias=VT[:, 91:92],
                                                  scale=1.0 / RH), "sd")
            if place == "root":
                out_dve.wait(act, o, "rcp")
                dst, src = by_head(SQO, VR[:, :])
                out_act.done(nc.scalar.copy(dst, src), "spread")

        def out_pool_step(pool, o, place):
            oo = part(o, 4)
            if place == 4:
                out_dve.wait(pool, o, "m1")
                waited(pool, "pool")
                out_pool.done(nc.gpsimd.tensor_tensor(oo, oo, vb(V_LW), ALU.mult), "m2")

        def out_dve_step(dve, o, s, place):
            O, TT = out_dve, nc.vector.tensor_tensor
            oo = part(o, 4)
            if place == (0, 0):
                out_pe.wait(dve, o, "mean")
                O.done(nc.vector.scalar_tensor_tensor(oo, bank(6), -1.0 / RH, oo, ALU.mult, ALU.add), "d")
            if place == (1, 1):
                out_act.wait(dve, o, "sd")
                O.done(nc.vector.reciprocal(VR[:, :], VR[:, :]), "rcp")
            if place == (3, 0):
                out_pe.wait(dve, o, "vt")
                O.done(TT(oo, oo, bank(6), ALU.mult), "m1")
            if place == (4, 1):
                out_pool.wait(dve, o, "m2")
                prep_pool.wait(dve, o, "lb")
                waited(dve, "dve")
                O.done(TT(oo, oo, BON[:, s], ALU.add), "m4")
            if place == (5, 0):
                O.wait(dve, o, "m4")
                out_pe.wait(dve, o, "gate")
                waited(dve, "dve")
                O.done(TT(part(o, 0), oo, bank(6), ALU.mult), "yb")

        def chunk_pe(t, c, s, prep, outp):
            T, MM, TR = solve_pe, nc.tensor.matmul, nc.tensor.transpose
            prep_dve.wait(t, c, "bon")
            prep_pool.wait(t, c, "rk2")
            for q in range(4):
                for p in range(4):
                    src = (AR[:, s, p, 0], BK[:, s, 0, p], BK[:, s, 1, p], VC[:, s, p])[q]
                    m = TR(bank(q)[:, p], src, ident)
                T.done(m, f"tok{q}")
            if prep:
                prep_pe_step(t, c + 1, 1 - s, HEAD[0])
            prep_act.wait(t, c, "pad1")
            for q in two:
                for b in two:
                    if q == 0 and b == 0:
                        if not is_first(c):
                            solve_dve.wait(t, c - 1, "s1")
                    elif q == 0:
                        solve_act.wait(t, c, "tok3")
                    elif b == 0:
                        solve_act.wait(t, c, "tok1")
                    else:
                        solve_dve.wait(t, c, "m0")
                    for j in two:
                        m = MM(PS[:, PRODUCT_BANK[q, b] + j].rearrange("p (g a m) -> p g a m", g=2, m=P),
                               BK[:, s, q, 2 * b + j], ARP[:, 2 * b + j], start=True, stop=True)
                    T.done(m, f"p{q + 1}_{b}")
                if q == 0 and prep:
                    prep_pe_step(t, c + 1, 1 - s, HEAD[1])
            for b in two:
                solve_pool.wait(t, c, f"tt_{b}")
                solve_dve.wait(t, c, f"n{b}")
                for j in range(4):
                    m = TR(bank(3 * b)[:, j], TIT[:, 4 * b + j], ident)
                T.done(m, f"t0_{b}")
                if b == 0:
                    solve_dve.wait(t, c, "n1")
                    if prep:
                        prep_dve.wait(t, c + 1, "zas")
                    for h in range(8):
                        m = MM(PS[:, 7, RH * h:RH * h + RH], NTRK[:, h, 0], TOK[:, 3, RH * h:RH * h + RH],
                               start=True, stop=True)
                    T.done(m, "nv")
            for k in range(LEVELS):
                for b in two:
                    (solve_pool if k else solve_dve).wait(t, c, f"x{k}_{b}")
                    if k == 0:
                        solve_act.wait(t, c, f"t0_{b}")
                    else:
                        solve_dve.wait(t, c, f"t{k - 1}_{b}")
                    for j in range(4):
                        m = MM(bank(3 * b)[:, j], XL[:, 4 * b + j], TI[:, 4 * b + j], start=True, stop=True)
                    T.done(m, f"y{k}_{b}")
                if outp:
                    out_pe_step(t, c - 1, k)
                if prep:
                    prep_pe_step(t, c + 1, 1 - s, k)
                for b in two:
                    solve_act.wait(t, c, f"y{k}_{b}")
                    if k > 0:
                        solve_dve.wait(t, c, f"tt{k - 1}_{b}")
                    if k < LEVELS - 1:
                        for j in range(4):
                            m = MM(bank(3 * b + 1)[:, j], TIT[:, 4 * b + j], YL[:, 4 * b + j],
                                   start=True, stop=True)
                        T.done(m, f"dt{k}_{b}")
                    for j in range(4):
                        m = MM(bank(3 * b + 2)[:, j], YL[:, 4 * b + j], TIT[:, 4 * b + j], start=True, stop=True)
                    T.done(m, f"dtt{k}_{b}")
            for p in range(4):
                MM(bank(4)[:, p], TOK[:, 2, P * p:P * p + P], TOK[:, 3, P * p:P * p + P], start=(p == 0),
                   stop=False, skip_group_check=True)
            for b in two:
                solve_dve.wait(t, c, f"tt{LEVELS - 1}_{b}")
                for h in range(4 * b, 4 * b + 4):
                    lo = RH * (h % 2)
                    m = MM(PS[lo:lo + RH, 0, P * (h // 2):P * (h // 2) + P], TOK[:, 0, RH * h:RH * h + RH],
                           TIT[:, h], start=True, stop=True)
            T.done(m, "wt")
            for h in range(8):
                m = MM(PS[:, 1, RH * h:RH * h + RH], TIT[:, h], NV[:, RH * h:RH * h + RH], start=True, stop=True)
            T.done(m, "z")
            if outp:
                out_dve.wait(t, c - 1, "yb")
            for h in range(8):
                lo = RH * (h % 2)
                MM(PS[lo:lo + RH, 6, P * (h // 2):P * (h // 2) + P], TOK[:, 3, RH * h:RH * h + RH],
                   NTRK[:, h, 1], start=(h < 2), stop=False, skip_group_check=True)
            solve_act.wait(t, c, "wt")
            solve_dve.wait(t, c, "s_in")
            for p in range(4):
                m = MM(bank(3)[:, p], WT[:, p], SP_[:, p], start=True, stop=True)
            T.done(m, "u")
            for p in range(4):
                MM(bank(6)[:, p], SP_[:, p], AR[:, s, p, 1], start=False, stop=False, skip_group_check=True)
            solve_dve.wait(t, c, "u")
            for p in range(4):
                m = MM(bank(4)[:, p], TOK[:, 1, P * p:P * p + P], UU[:, P * p:P * p + P], start=False, stop=True,
                       skip_group_check=True)
            T.done(m, "s")
            for h in range(8):
                lo = RH * (h % 2)
                m = MM(PS[lo:lo + RH, 6, P * (h // 2):P * (h // 2) + P], UU[:, RH * h:RH * h + RH],
                       MTRB[:, h, 1], start=False, stop=True, skip_group_check=True)
            T.done(m, "o")

        def chunk_act(act, c, s, prep, outp):
            T = solve_act
            for q in range(4):
                solve_pe.wait(act, c, f"tok{q}")
                T.done(nc.scalar.copy(TOK[:, q], PS[:, q]), f"tok{q}")
            if prep:
                for place in HEAD:
                    prep_act_step(act, c + 1, 1 - s, place)
            solve_pe.wait(act, c, "t0_0")
            T.done(nc.scalar.copy(heads(TI, 0), bank(0)), "t0_0")
            solve_pe.wait(act, c, "nv")
            T.done(nc.scalar.copy(NV[:, :], PS[:, 7]), "nv")
            solve_pe.wait(act, c, "t0_1")
            T.done(nc.scalar.copy(heads(TI, 1), bank(3)), "t0_1")
            for k in range(LEVELS):
                for b in two:
                    solve_pe.wait(act, c, f"y{k}_{b}")
                    T.done(nc.scalar.copy(heads(YL, b), bank(3 * b)), f"y{k}_{b}")
                for place in (k, "root") if k == 1 else (k,):
                    if outp:
                        out_act_step(act, c - 1, place)
                    if prep:
                        prep_act_step(act, c + 1, 1 - s, place)
            solve_pe.wait(act, c, "wt")
            T.done(nc.scalar.copy(WT[:, :], bank(0)), "wt")
            solve_pe.wait(act, c, "z")
            T.done(nc.scalar.copy(ZZ[:, :], PS[:, 1]), "z")
            solve_pe.wait(act, c, "o")
            waited(act, "act")
            T.done(nc.scalar.copy(part(c, 4), bank(6)), "o")

        PRODUCT_BANK = {(0, 0): 4, (0, 1): 2, (1, 0): 0, (1, 1): 4}

        def chunk_dve(dve, c, s, prep, outp):
            T, TT = solve_dve, nc.vector.tensor_tensor
            if prep:
                prep_dve_step(dve, c + 1, 1 - s, HEAD[0])
            if not is_first(c):
                solve_pe.wait(dve, c - 1, "o")
            for q, dst in ((0, MTRB), (1, NTRK)):
                for b in two:
                    solve_pe.wait(dve, c, f"p{q + 1}_{b}")
                    T.done(TT(dst[:, 4 * b:4 * b + 4].rearrange("p h a m -> p h (a m)"),
                              PS[:, PRODUCT_BANK[q, b]:PRODUCT_BANK[q, b] + 2].rearrange(
                                  "p j (g m) -> p (j g) m", g=2),
                              over(CON[:, C_MU:C_MU + 2 * P], 4), ALU.mult), f"{'mn'[q]}{b}")
                if q == 0 and prep:
                    prep_dve_step(dve, c + 1, 1 - s, HEAD[1])
            T.wait(dve, c, "m1")
            for b in two:
                T.done(TT(heads(XL, b), MTRB[:, 4 * b:4 * b + 4, 0], over(CON[:, C_MX:C_MX + P], 4), ALU.mult),
                       f"x0_{b}")
            if prep:
                prep_dve_step(dve, c + 1, 1 - s, HEAD[2])
            prep_pool.wait(dve, c, "g1m")
            if is_first(c):
                dve.wait_ge(state_zero, 1)
            else:
                T.wait(dve, c - 1, "s")
            T.done(TT(SP_[:, :], SS[:, :], G1M[:, s], ALU.mult), "s_in")
            for k in range(LEVELS):
                for b in two:
                    if k < LEVELS - 1:
                        solve_pe.wait(dve, c, f"dt{k}_{b}")
                        T.done(TT(heads(TI, b), heads(TI, b), bank(3 * b + 1), ALU.add), f"t{k}_{b}")
                    solve_pe.wait(dve, c, f"dtt{k}_{b}")
                    T.done(TT(heads(TIT, b), heads(TIT, b), bank(3 * b + 2), ALU.add), f"tt{k}_{b}")
                    if outp:
                        out_dve_step(dve, c - 1, 1 - s, (k, b))
                    if prep:
                        prep_dve_step(dve, c + 1, 1 - s, (k, b))
            solve_pe.wait(dve, c, "u")
            solve_act.wait(dve, c, "z")
            T.done(TT(UU[:, :], PS[:, 3], ZZ[:, :], ALU.add), "u")
            solve_pe.wait(dve, c, "s")
            T.done(TT(SS[:, :], bank(4), SP_[:, :], ALU.add), "s1")
            T.wait(dve, c, "s1")
            T.done(TT(SS[:, :], SS[:, :], GS[:, s, 1].unsqueeze(2).to_broadcast([P, 4, P]), ALU.mult), "s")

        def chunk_pool(pool, c, s, prep, outp):
            T, TT = solve_pool, nc.gpsimd.tensor_tensor
            if prep:
                prep_pool_step(pool, c + 1, 1 - s, HEAD[0])
            if not is_first(c):
                solve_pe.wait(pool, c - 1, "o")
            for b in two:
                solve_dve.wait(pool, c, f"m{b}")
                T.done(TT(heads(TIT, b), MTRB[:, 4 * b:4 * b + 4, 0], over(CON[:, C_M0:C_M0 + P], 4), ALU.mult),
                       f"i{b}")
                T.wait(pool, c, f"i{b}")
                T.done(TT(heads(TIT, b), heads(TIT, b), over(ident, 4), ALU.add), f"tt_{b}")
            for k in range(LEVELS):
                for b in two if k else ():
                    solve_pe.wait(pool, c, f"y{k - 1}_{b}")
                    T.done(TT(heads(XL, b), MTRB[:, 4 * b:4 * b + 4, 0],
                              over(CON[:, C_MX + k * P:C_MX + (k + 1) * P], 4), ALU.mult), f"x{k}_{b}")
                if outp:
                    out_pool_step(pool, c - 1, k)
                if prep:
                    prep_pool_step(pool, c + 1, 1 - s, k)
            if prep:
                prep_pool_step(pool, c + 1, 1 - s, "end")

        def recurrence(engine, chunk, prep_step, out_step, before_last=None, beside_last=None):
            for place in PLACES:
                prep_step(engine, 0, 0, place)
            chunk(engine, 0, 0, True, False)
            with engine.Fori(0, (NT - 2) // 2) as i:
                for j in two:
                    chunk(engine, 2 * i + (1 + j), 1 - j, True, True)
            if before_last:
                before_last()
            chunk(engine, NT - 1, 1, False, True)
            for place in PLACES:
                out_step(engine, NT - 1, place)
                if beside_last:
                    beside_last(place)

        ya_back = sem("ya_back")
        SPLIT_AT = {0: (0, 1), "root": (2,), 3: (3,)}

        def mixed_source(k):
            return RKV[:, k + 8] if k < 4 else RKV[:, k - 4]

        def mixed_act(act, k):
            if k == 0:
                act.wait_ge(ya_back, 16)
            if k == 4:
                out_dve.wait(act, NT - 1, "yb")
            nc.scalar.copy(Hh[:, k], mixed_source(k)).then_inc(h_hi, 1)
            if k == 0:
                split_hi(act, 0, 13, 28)

        def mixed_dve(dve, k):
            h_lo_split(dve, 1, k, mixed_source(k))
            if k == 0:
                split_lo(dve, 0, 26)

        def beside(step):
            return lambda place: [step(k) for k in SPLIT_AT.get(place, ())]

        qk_sq, qk_ms, qk_sd, qk_rc, qk_ex, qk_tr, qk_norm = (
            sem("qk_squared"), sem("qk_mean_square"), sem("qk_root"), sem("qk_inverted"), sem("qk_expanded"),
            sem("qk_inverse_transposed"), sem("qk_normed"))
        k2_in, v_tr, v_tok = sem("k2_in"), sem("v_transposed"), sem("v_token_major")
        SQB = (SQ[:, 0:S], ST2[:, 0:S])
        STB = (ST0[:, 0:S], ST1[:, 0:S])

        def qkv_pe(t):
            u0, a0_ = STAGE["qkv"]

            def unit(j, slot, half, between, ready=None):
                product(t, slot, slot, a0_ // 2 + half, u0 + j, 8, P, 0, Hh, Hl, ready=ready, between=between)

            def mean_square(n, slot):
                t.wait_ge(qk_sq, n + 1)
                for tile in range(NT):
                    m = nc.tensor.matmul(PS[:, 4, 2 * tile:2 * tile + 2], SQB[slot][:, tile * P:tile * P + P],
                                         blk[:, 0:P:RH], start=True, stop=True)
                m.then_inc(qk_ms, 1)

            def spread(n, slot):
                t.wait_ge(qk_ex, n + 1)
                t.wait_ge(qk_norm, n + 2)
                for tile in range(NT):
                    m = nc.tensor.transpose(bank(6 + tile // 4)[:, tile % 4],
                                            SQB[slot][:, tile * P:tile * P + P], ident)
                m.then_inc(qk_tr, 1)

            def norm_steps(n, slot):
                return {3: lambda: mean_square(n, slot), 6: lambda: spread(n, slot)}

            def v_transposes():
                t.wait_ge(acc_free[1], a0_ // 2 + 2)
                t.wait_ge(pads_zero, 3)
                t.wait_ge(qk_norm, 3)
                for n in range(9):
                    m = nc.tensor.transpose(bank((6, 7, 5)[n // 4])[:, n % 4], VP[:, P * n:P * n + P], ident)
                m.then_inc(v_tr, 1)

            unit(0, 0, 0, norm_between(t, "qkv"), ready=(h_lo, 8 * H_FILL["qkv"]))
            unit(1, 1, 0, norm_steps(0, 0))
            unit(2, 0, 1, {4: v_transposes})
            t.wait_ge(v_tok, 3)
            unit(3, 1, 1, norm_steps(1, 0))
            with t.Fori(0, 3) as i:
                unit(2 * i + 4, 0, i + 2, norm_steps(2 * i + 2, 1))
                unit(2 * i + 5, 1, i + 2, norm_steps(2 * i + 3, 0))
            mean_square(8, 1)
            spread(8, 1)

        def qkv_act(act):
            u0, a0_ = STAGE["qkv"]

            def inverse_root(n, slot):
                act.wait_ge(qk_norm, 3 if at_start(n, 2) and n == 1 else n + 1)
                nc.scalar.activation(SQB[slot], STB[slot], ACT.Square).then_inc(qk_sq, 1)
                act.wait_ge(qk_ms, n + 1)
                nc.scalar.activation(QR[:, :], PS[:, 4, 0:2 * NT], ACT.Sqrt, bias=VT[:, 90:91], scale=1.0 / RH)\
                    .then_inc(qk_sd, 1)
                act.wait_ge(qk_rc, n + 1)
                nc.scalar.copy(SQB[slot].rearrange("p (a m) -> p a m", m=RH), QR[:, :].unsqueeze(2).to_broadcast(
                    [P, 2 * NT, RH])).then_inc(qk_ex, 1)

            def step(j, slot, i, n):
                split_hi(act, slot, u0 // 2 + i + 1, a0_ + j + 3)
                if n is not None:
                    act.wait_ge(acc_free[slot], a0_ // 2 + i + 2)
                    inverse_root(n, slot)

            split_hi(act, 1, u0 // 2, a0_ + 2)
            step(0, 0, 0, 0)
            step(1, 1, 0, None)
            step(2, 0, 1, 1)
            with act.Fori(0, 3) as i:
                step(2 * i + 3, 1, i + 1, 2 * i + 2)
                step(2 * i + 4, 0, i + 2, 2 * i + 3)
            act.wait_ge(acc_free[1], a0_ // 2 + 6)
            inverse_root(8, 1)

        def qkv_dve(dve):
            u0, a0_ = STAGE["qkv"]

            def stage(j, slot, n, dst):
                dve.wait_ge(acc_done, a0_ + j + 3)
                if n is not None:
                    dve.wait_ge(qk_norm, 3 if at_start(n, 2) and n == 1 else n + 1)
                scale_out(dve, dst, slot)

            def invert(n):
                dve.wait_ge(qk_sd, n + 1)
                nc.vector.reciprocal(QR[:, :], QR[:, :]).then_inc(qk_rc, 1)
                dve.wait_ge(qk_tr, n + 1)

            def norm(n, slot, dst):
                invert(n)
                nc.vector.scalar_tensor_tensor(dst, STB[slot], VT[:, V_QS:V_QS + 1], acc_banks67, ALU.mult,
                                               ALU.mult).then_inc(qk_norm, 1)

            def q(n):
                return Q[:, bass.ds(n, 1), :].rearrange("p a n -> p (a n)")

            split_lo(dve, 1, u0 + 1)
            stage(0, 0, 0, STB[0])
            split_lo(dve, 0, u0 + 2)
            invert(0)
            dve.wait_ge(pads_zero, 3)
            for kv in two:
                rows = slice(RH * kv, RH * kv + RH)
                m = nc.vector.scalar_tensor_tensor(K2[rows, kv, kv, RH:RH + S], STB[0][rows], VT[rows, V_KG:V_KG + 1],
                                                   acc_banks67[rows], ALU.mult, ALU.mult)
            m.then_inc(qk_norm, 1)
            stage(1, 1, None, VP[:, RH:RH + S])
            split_lo(dve, 1, u0 + 3)
            dve.wait_ge(v_tr, 1)
            for n in (0, 1, 2):
                rows = 4 if n < 2 else 1
                nc.vector.tensor_copy(VTOK[:, 4 * n:4 * n + rows], bank((6, 7, 5)[n])[:, 0:rows]).then_inc(v_tok, 1)
            stage(2, 0, 1, STB[0])
            split_lo(dve, 0, u0 + 4)
            norm(1, 0, Q[:, 0])
            with dve.Fori(0, 3) as i:
                stage(2 * i + 3, 1, 2 * i + 2, STB[1])
                split_lo(dve, 1, u0 + 2 * i + 5)
                norm(2 * i + 2, 1, q(2 * i + 1))
                stage(2 * i + 4, 0, 2 * i + 3, STB[0])
                split_lo(dve, 0, u0 + 2 * i + 6)
                norm(2 * i + 3, 0, q(2 * i + 2))
            stage(9, 1, 8, STB[1])
            norm(8, 1, Q[:, 7])

        q_pool = Track("q_tile_copied", ["q"])
        v_pool = Track("v_tile_copied", ["v"])
        p_pool = Track("probs_pool", ["p1", "p2", "p3"])
        sc_pe = Track("score_pe", [f"sc{g}" for g in range(4)])
        pv_pe = Track("value_pe", [f"t{w}{g}" for g in range(4) for w in "ab"] + ["pv"])
        sc_dve = Track("score_dve", [f"{w}{g}" for g in range(4) for w in ("b", "max", "neg")] + ["sink"])
        pv_dve = Track("value_dve", ["den", "rcp", "p0", "e0", "e1", "e2", "e3"])
        sc_act = Track("score_act", [f"e{g}" for g in range(4)] + ["sink"])
        pv_act = Track("value_act", [f"e{g}" for g in range(4)] + ["o0", "o1"])
        ptb_zero, nsnk_ok = sem("probs_rest_zero"), sem("minus_sinks_ready")
        slopes = [2.0 ** (-8.0 * (h + 1) / NQ) for h in range(NQ)]

        def score_banks(g):
            return PS[:, 2 * (g % 2):2 * (g % 2) + 2, 0:2 * WIN]

        def q_tile(pool, tile, s):
            if not at_start(tile, 2):
                sc_pe.wait(pool, tile - 2, "sc3")
                waited(pool, "pool")
            q_pool.done(nc.gpsimd.tensor_copy(QST[:, s], Q[:, :, bass.ds(tile * P, P)]), "q")

        def v_tile(pool, tile, s):
            if not at_start(tile, 2):
                pv_pe.wait(pool, tile - 2, "pv")
                waited(pool, "pool")
            v_pool.done(nc.gpsimd.tensor_copy(VST[:, s], VTOK[:, bass.ds(tile, 2), :]), "v")

        def score_products(t, tile, s, g):
            if g == 0:
                q_pool.wait(t, tile, "q")
            if g >= 2:
                sc_dve.wait(t, tile, f"b{g - 2}")
            elif not at_start(tile, 1):
                sc_dve.wait(t, tile - 1, f"b{g + 2}")
            for j in two:
                m = nc.tensor.matmul(score_banks(g)[:, j].rearrange("p (a m) -> p a m", a=2), QST[:, s, 2 * g + j],
                                     K2[:, g // 2, :, bass.ds(tile * P, WIN)], start=True, stop=True)
            sc_pe.done(m, f"sc{g}")

        def probs_transposes(t, tile, s, g):
            if g:
                p_pool.wait(t, tile, f"p{g}")
            else:
                pv_dve.wait(t, tile, f"p{g}")
            if g > 0:
                pv_act.wait(t, tile, f"e{g - 1}")
                pv_dve.wait(t, tile, f"e{g - 1}")
            for j in range(4):
                m = nc.tensor.transpose(bank(4)[:, j], PP[:, s, 4 * g + j, 0:P], ident)
            pv_pe.done(m, f"ta{g}")
            for j in range(4):
                m = nc.tensor.transpose(bank(5)[0:RH, j], PP[:, s, 4 * g + j, P:WIN], ident)
            pv_pe.done(m, f"tb{g}")

        def value_products(t, tile, s):
            pv_act.wait(t, tile, "e3")
            pv_dve.wait(t, tile, "e3")
            v_pool.wait(t, tile, "v")
            if at_start(tile, 1):
                t.wait_ge(ptb_zero, 1)
            else:
                pv_act.wait(t, tile - 1, "o1")
            for kv in range(NKV):
                for n, pt in enumerate((PTA, PTB)):
                    for par in two:
                        o = PS[RH * par:RH * par + RH, 6 + kv].rearrange("p (a m) -> p a m", m=P)
                        m = nc.tensor.matmul(o, VST[:, s, n, RH * kv:RH * kv + RH], pt[:, 8 * kv + par:8 * kv + 8:2],
                                             start=n == 0, stop=n == 1)
            pv_pe.done(m, "pv")

        def round_pe(t, new, old, s):
            for g in range(4):
                if new is not None and g < 3:
                    score_products(t, new, s, g + 1)
                if g == 3 and new is not None and not (isinstance(new, int) and new == NT - 1):
                    score_products(t, new + 1, 1 - s, 0)
                if old is not None:
                    probs_transposes(t, old, 1 - s, g)
            if old is not None:
                value_products(t, old, 1 - s)

        def round_dve(dve, new, old, s):
            o = 1 - s
            first = C_DIST + WIN if at_start(new, 1) else C_DIST
            dist = CON[:, first:first + WIN]
            for g in range(4):
                hs = slice(4 * g, 4 * g + 4)
                if new is not None:
                    sc_pe.wait(dve, new, f"sc{g}")
                    if not at_start(new, 2):
                        pv_pe.wait(dve, new - 2, f"tb{g}")
                    for j in range(4):
                        h = 4 * g + j
                        m = nc.vector.scalar_tensor_tensor(
                            PP[:, s, h], dist, -slopes[h],
                            score_banks(g)[:, j // 2, WIN * (j % 2):WIN * (j % 2) + WIN], ALU.mult, ALU.add)
                    sc_dve.done(m, f"b{g}")
                    sc_dve.wait(dve, new, f"b{g}")
                    sc_dve.done(nc.vector.tensor_reduce(STA[:, s, 0, hs], PP[:, s, hs], AXX, ALU.max), f"max{g}")
                    sc_dve.wait(dve, new, f"max{g}")
                    sc_dve.done(nc.vector.scalar_tensor_tensor(STA[:, s, 2, hs], STA[:, s, 0, hs], -1.0, NSNK[:, hs],
                                                               ALU.mult, ALU.min), f"neg{g}")
                if old is not None:
                    if g == 0:
                        sc_act.wait(dve, old, "sink")
                        pv_dve.done(nc.vector.tensor_tensor(STA[:, o, 4], STA[:, o, 4], STA[:, o, 5], ALU.add), "den")
                        pv_dve.wait(dve, old, "den")
                        pv_dve.done(nc.vector.reciprocal(STA[:, o, 4], STA[:, o, 4]), "rcp")
                        pv_dve.wait(dve, old, "rcp")
                    else:
                        rest_copy(dve, old, g - 1)
                    if g == 0:
                        pv_dve.done(nc.vector.tensor_tensor(
                            PP[:, o, hs], PP[:, o, hs], STA[:, o, 4, hs].unsqueeze(2).to_broadcast([P, 4, WIN]),
                            ALU.mult), f"p{g}")
            if new is not None:
                sc_dve.wait(dve, new, "neg3")
                sc_dve.done(nc.vector.tensor_tensor(STA[:, s, 3], SNK[:, :], STA[:, s, 2], ALU.add), "sink")
            if old is not None:
                rest_copy(dve, old, 3)

        def rest_copy(dve, tile, g):
            pv_pe.wait(dve, tile, f"tb{g}")
            if g == 0 and not at_start(tile, 1):
                pv_pe.wait(dve, tile - 1, "pv")
            pv_dve.done(nc.vector.tensor_copy(PTB[0:RH, 4 * g:4 * g + 4], bank(5)[0:RH]), f"e{g}")

        def round_act(act, new, old, s):
            for g in range(4):
                if new is not None:
                    sc_dve.wait(act, new, f"neg{g}")
                    for h in range(4 * g, 4 * g + 4):
                        m = nc.scalar.activation(PP[:, s, h], PP[:, s, h], ACT.Exp, bias=STA[:, s, 2, h:h + 1],
                                                 accum_out=STA[:, s, 4, h:h + 1])
                    sc_act.done(m, f"e{g}")
                    if g == 3:
                        sc_dve.wait(act, new, "sink")
                        sc_act.done(nc.scalar.activation(STA[:, s, 5], STA[:, s, 3], ACT.Exp), "sink")
                if old is not None:
                    pv_pe.wait(act, old, f"ta{g}")
                    pv_act.done(nc.scalar.copy(PTA[:, 4 * g:4 * g + 4], bank(4)), f"e{g}")
            if old is not None:
                pv_pe.wait(act, old, "pv")
                waited(act, "act")
                for kv in range(NKV):
                    pv_act.done(nc.scalar.copy(Q[:, 4 * kv:4 * kv + 4, bass.ds(old * P, P)], bank(6 + kv)), f"o{kv}")

        def round_pool(pool, new, old, s):
            o = 1 - s
            if new is not None and not (isinstance(new, int) and new == NT - 1):
                q_tile(pool, new + 1, o)
            if old is not None:
                pv_dve.wait(pool, old, "rcp")
                for g in (1, 2, 3):
                    hs = slice(4 * g, 4 * g + 4)
                    p_pool.done(nc.gpsimd.tensor_tensor(
                        PP[:, o, hs], PP[:, o, hs], STA[:, o, 4, hs].unsqueeze(2).to_broadcast([P, 4, WIN]),
                        ALU.mult), f"p{g}")
            if new is not None:
                v_tile(pool, new, s)

        def attention(engine, one_round):
            one_round(engine, 0, None, 0)
            one_round(engine, 1, 0, 1)
            with engine.Fori(0, (NT - 4) // 2) as i:
                for j in two:
                    one_round(engine, 2 * i + (2 + j), 2 * i + (1 + j), j)
            one_round(engine, NT - 2, NT - 3, 0)
            one_round(engine, NT - 1, NT - 2, 1)
            one_round(engine, None, NT - 1, 0)

        def attn_split(eng, act):
            for k in range(KD):
                if act:
                    if k == 0:
                        pv_act.wait(eng, NT - 1, "o1")
                    nc.scalar.copy(Hh[:, k], Q[:, k]).then_inc(h_hi, 1)
                else:
                    h_lo_split(eng, 4, k, Q[:, k])

        OT = at("out_chunk", [2, NT, P], 32)

        GX = [b[:, 0:S].rearrange("p (k n) -> p k n", k=KD) for b in (ST1, ST2)]

        def x_banks(tile):
            return PS[:, 2 * (tile % 2):2 * (tile % 2) + 2, :].rearrange("p b (k n) -> p (b k) n", n=P)

        PARAMETER_ROWS = [(V_MIX, norm_mix.rearrange("l (k p) -> (l k) p", p=P)),
                          (V_MLP, norm_mlp.rearrange("l (k p) -> (l k) p", p=P)),
                          (V_MU, shift_mu.rearrange("l (k p) -> (l k) p", p=P)),
                          (V_W0, w0.rearrange("l (k p) -> (l k) p", p=P)),
                          (V_A0, a0.rearrange("l (k p) -> (l k) p", p=P)),
                          (V_KK, k_k.rearrange("l (k p) -> (l k) p", p=P)),
                          (V_KA, k_a.rearrange("l (k p) -> (l k) p", p=P)),
                          (V_RK, r_k.rearrange("l (k h) n -> (l k) (h n)", h=2)),
                          (V_LW, lnx_w.rearrange("l (k p) -> (l k) p", p=P)),
                          (V_LB, lnx_b.rearrange("l (k p) -> (l k) p", p=P)),
                          (V_CW, conv_w.rearrange("l j (k p) -> (l j k) p", p=P))]

        @block.sync
        def _(sp):
            sp.dma_start(CON[:, 0:C_MU], consts[:, 0:C_MU]).then_inc(ident_in, 16)
            for row, src in PARAMETER_ROWS[0:7]:
                sp.dma_start(VROW[row:row + src.shape[0], :], src).then_inc(const_in, 16)
            with sp.Fori(0, 2) as i:
                for q in range(2):
                    for r in range(3):
                        load_unit(sp, (3 * q + r) % 2, 6 * i + 3 * q + r,
                                  win[:, :, bass.ds(i * 256 + (512 * r + P * q), P)])
            sp.dma_start(CON[:, C_MU:C_DIST], consts[:, C_MU:C_DIST]).then_inc(late_in, 16)
            sp.wait_ge(lora_zero, 1)
            sp.dma_start(LOR[0:RH, 0], w_decay2[0]).then_inc(late_in, 16)
            sp.dma_start(LOR[RH:P, 1], w_aaa2[0]).then_inc(late_in, 16)
            sp.dma_start(LOR[:, 2], w_gate2[0]).then_inc(late_in, 16)
            sp.dma_start(SNK[:, :], sinks.to_broadcast([P, NQ])).then_inc(late_in, 16)
            for j in two:
                load_unit(sp, j, 12 + j, win[:, :, 3072 + P * j:3072 + P * j + P])
            with sp.Fori(0, 6) as i:
                for j in two:
                    load_unit(sp, j, 14 + 2 * i + j, win[:, :, bass.ds(i * 256 + (1536 + P * j), P)])
            solve_pe.wait(sp, NT - 1, "p2_1")
            load_stage(sp, "out", wout, 8)
            load_mlp(sp, 0)
            u0 = STAGE["qkv"][0]
            sp.wait_ge(w_lo, STAGE["mlp0"][0] + 1)
            sp.dma_start(CON[:, C_DIST:], consts[:, C_DIST:]).then_inc(dist_in, 16)
            for j in two:
                load_unit(sp, j, u0 + j, wqkv[:, :, S + P * j:S + P * j + P])
            with sp.Fori(0, 4) as i:
                for j in two:
                    load_unit(sp, j, u0 + 2 + 2 * i + j, wqkv[:, :, bass.ds((2 * i + j) * P, P)])
            load_stage(sp, "wo", wo, 8)
            load_mlp(sp, 1)
            oo = out[0].rearrange("(t p) (k n) -> k p t n", p=P, n=P)
            for j in two:
                sp.sem_inc(out_dma[j], 16)
            with sp.Fori(0, KD // 2) as i:
                for j in two:
                    sp.wait_ge(out_st, 2 * i + (j + 3))
                    sp.dma_start(oo[bass.ds(2 * i + j, 1)].rearrange("a p t n -> p (a t) n"), OT[:, j])\
                        .then_inc(out_dma[j], 16)
            for j in two:
                sp.wait_ge(out_dma[j], 16 * (KD // 2 + 1))

        @block.gpsimd
        def _(pool):
            pool.sem_inc(gl_free, 1)
            nc.gpsimd.memset(VT[:, 90:91], EPS).then_inc(eps_set, 1)
            nc.gpsimd.memset(VT[:, 91:92], LNX_EPS).then_inc(eps_set, 1)
            nc.gpsimd.memset(LOR[:, 0:2], 0.0).then_inc(lora_zero, 1)
            xin = x[0].rearrange("(t p) (k n) -> t p k n", p=P, n=P)
            for tile in range(NT):
                if tile >= 4:
                    pool.wait_ge(x_tr, 2 + tile - 3)
                    pool.wait_ge(x_sq, tile - 3)
                pool.dma_start(XIN[:, tile % 4], xin[tile]).then_inc(x_in[tile % 4], 16)
            for g in range(4):
                pool.wait_ge(conv_done, g + 2)
                pool.dma_start(ya_dram[g], GL[:, :]).then_inc(ya_out, 16)
                pool.wait_ge(ya_out, 16 * g + 16)
                pool.sem_inc(gl_free, 1)
            pool.wait_ge(lora_act, 2)
            pool.wait_ge(late_in, 16 * N_LATE)

            def ya_read():
                prep_pool.wait(pool, NT - 1, "vc")
                pool.dma_start(RKV[:, 8:12], ya_dram.rearrange("g p n -> p g n")).then_inc(ya_back, 16)

            recurrence(pool, chunk_pool, prep_pool_step, out_pool_step, before_last=ya_read)
            norm_pool(pool, "mlp0")
            residual_done(pool, "mlp0")
            nc.gpsimd.memset(K2[:, :, :, :], 0.0).then_inc(pads_zero, 1)
            nc.gpsimd.memset(VP[:, 0:RH], 0.0).then_inc(pads_zero, 1)
            nc.gpsimd.memset(VP[:, RH + S:], 0.0).then_inc(pads_zero, 1)
            norm_pool(pool, "qkv")
            pool.wait_ge(qk_norm, 3)
            for kv in two:
                here, there = slice(RH * kv, RH * kv + RH), slice(RH * (1 - kv), RH * (1 - kv) + RH)
                pool.dma_start(K2[there, kv, 1 - kv, RH:RH + S], K2[here, kv, kv, RH:RH + S]).then_inc(k2_in, 16)
            pool.wait_ge(qk_norm, 2 + 9)
            q_tile(pool, 0, 0)
            q_pool.wait(pool, 0, "q")
            nc.gpsimd.memset(PTB[RH:P], 0.0).then_inc(ptb_zero, 1)
            pool.wait_ge(ptb_zero, 1)
            attention(pool, round_pool)
            norm_pool(pool, "mlp1")

        def x_high(act, tile):
            act.wait_ge(x_gain, tile + 1)
            nc.scalar.copy(Hh[:, :, tile * P:tile * P + P], GX[tile % 2]).then_inc(h_hi, 1)

        @block.scalar
        def _(act):
            for row, src in PARAMETER_ROWS[7:]:
                act.dma_start(VROW[row:row + src.shape[0], :], src).then_inc(const_in, 16)
            for half in two:
                act.dma_start(VROW[V_QG:V_QG + 1, RH * half:RH * half + RH], q_gain).then_inc(const_in, 16)
                act.dma_start(VROW[V_KG:V_KG + 1, RH * half:RH * half + RH], k_gain).then_inc(const_in, 16)
            for tile in range(NT):
                cols = slice(tile * P, tile * P + P)
                act.wait_ge(x_tr, tile + 3)
                nc.scalar.copy(X[:, :, cols], x_banks(tile)).then_inc(x_ev, 1)
                if tile == NT - 1:
                    x_high(act, tile)
                if tile:
                    act.wait_ge(x_sq, tile)
                nc.scalar.activation(ST0[:, 0:S], XIN[:, tile % 4], ACT.Square, accum_out=SSQ[:, tile:tile + 1])\
                    .then_inc(x_sq, 1)
                if tile < NT - 1:
                    x_high(act, tile)
                if tile == NT - 3:
                    split_hi(act, 0, 0, 1)
            act.wait_ge(eps_set, 2)
            act.wait_ge(x_sq, NT)
            rms_root(act, SSQ[:, :])
            rms_spread(act, 0)
            in_act(act)
            recurrence(act, chunk_act, prep_act_step, out_act_step, beside_last=beside(lambda k: mixed_act(act, k)))
            for k in range(4, KD):
                mixed_act(act, k)
            residual_act(act, "out", 8)
            norm_act(act, "mlp0", V_MLP)
            with act.Fori(0, NG) as g:
                mlp_act(act, 0, g)
            norm_act(act, "qkv", V_MIX + KD)
            qkv_act(act)
            attention(act, round_act)
            attn_split(act, True)
            residual_act(act, "wo", 8)
            norm_act(act, "mlp1", V_MLP + KD)
            with act.Fori(0, NG - 1) as g:
                mlp_act(act, 1, g)
            mlp_act(act, 1, NG - 1, last=True)
            for k in range(2, KD):
                out_copy(act, k)

        @block.tensor
        def _(t):
            t.sem_inc(acc_done, 2)
            t.sem_inc(x_tr, 2)
            t.wait_ge(ident_in, 16)
            for tile in range(NT):
                t.wait_ge(x_in[tile % 4], 16 * (tile // 4) + 16)
                t.wait_ge(x_ev, tile + 1)
                for k in range(KD):
                    m = nc.tensor.transpose(x_banks(tile)[:, k], XIN[:, tile % 4, k], ident)
                m.then_inc(x_tr, 1)
                if tile == 0:
                    t.wait_ge(const_in, 16 * N_EARLY)
                    nc.tensor.transpose(PS[:, 7, 0:V_ROWS], VROW[0:V_ROWS, :], ident[0:V_ROWS, 0:V_ROWS])\
                        .then_inc(vec_t, 1)
            t.wait_ge(h_lo, NT)
            product(t, 0, 0, 0, 0, 8, P, 0, Hh, Hl, between=norm_between(t, "in"))
            product(t, 1, 1, 0, 1, 8, P, 0, Hh, Hl)
            with t.Fori(1, 13) as i:
                for j in two:
                    product(t, j, j, i, 2 * i + j, 8, P, 0, Hh, Hl)
            t.wait_ge(late_in, 16 * N_LATE)
            recurrence(t, chunk_pe, prep_pe_step, out_pe_step)
            dense_pe(t, "out", 8)
            mlp_pe(t, 0)
            qkv_pe(t)
            t.wait_ge(k2_in, 32)
            score_products(t, 0, 0, 0)
            attention(t, round_pe)
            dense_pe(t, "wo", 8)
            mlp_pe(t, 1)

        @block.vector
        def _(dve):
            dve.sem_inc(w_lo, 2)
            for j in two:
                dve.sem_inc(acc_free[j], 1)
            dve.sem_inc(x_ev, 2)
            dve.sem_inc(out_st, 2)
            dve.sem_inc(conv_done, 1)
            dve.sem_inc(shift_done, 2)
            dve.sem_inc(act_lo, 1)
            dve.sem_inc(qk_norm, 2)
            dve.wait_ge(vec_t, 1)
            nc.vector.tensor_copy(VT[:, 0:V_ROWS], PS[:, 7, 0:V_ROWS]).then_inc(vec_ok, 1)
            dve.wait_ge(vec_ok, 1)
            nc.vector.tensor_scalar(VT[:, V_QS:V_QS + 1], VT[:, V_QG:V_QG + 1], float(RH) ** -0.5, None,
                                    ALU.mult).then_inc(vec_ok, 1)
            dve.wait_ge(vec_ok, 2)
            for tile in range(NT + 1):
                if tile < NT:
                    dve.wait_ge(x_ev, tile + 3)
                    if tile >= 2:
                        dve.wait_ge(h_lo, tile - 1)
                    nc.vector.tensor_tensor(GX[tile % 2], X[:, :, tile * P:tile * P + P], vb(V_MIX, KD),
                                            ALU.mult).then_inc(x_gain, 1)
                if tile == NT - 1:
                    split_lo(dve, 0, 0)
                if tile:
                    dve.wait_ge(h_hi, tile)
                    cols = slice((tile - 1) * P, tile * P)
                    nc.vector.tensor_tensor(Hl[:, :, cols], GX[(tile - 1) % 2], Hh[:, :, cols].bitcast(F32),
                                            ALU.subtract).then_inc(h_lo, 1)
            rms_invert(dve, 0)
            in_dve(dve)
            dve.wait_ge(late_in, 16 * N_LATE)
            recurrence(dve, chunk_dve, prep_dve_step, lambda e, o, place: out_dve_step(e, o, 1, place),
                       beside_last=beside(lambda k: mixed_dve(dve, k)))
            for k in range(4, KD):
                mixed_dve(dve, k)
            residual_dve(dve, "out", 8)
            norm_dve(dve, "mlp0", V_MLP)
            with dve.Fori(0, NG) as g:
                mlp_dve(dve, 0, g)
            norm_dve(dve, "qkv", V_MIX + KD)
            qkv_dve(dve)
            nc.vector.tensor_scalar(NSNK[:, :], SNK[:, :], -1.0, None, ALU.mult).then_inc(nsnk_ok, 1)
            dve.wait_ge(nsnk_ok, 1)
            dve.wait_ge(dist_in, 16)
            attention(dve, round_dve)
            attn_split(dve, False)
            residual_dve(dve, "wo", 8)
            norm_dve(dve, "mlp1", V_MLP + KD)
            with dve.Fori(0, NG - 1) as g:
                mlp_dve(dve, 1, g)
            mlp_dve(dve, 1, NG - 1, last=True)


_INS = ["x", "norm_mix", "norm_mlp", "mlp_up", "mlp_down", "w_in_ab", "conv_w", "shift_mu", "w0", "w_decay2",
        "a0", "w_aaa2", "w_gate2", "k_k", "k_a", "r_k", "lnx_w", "lnx_b", "w_out_ab", "w_qkv", "q_gain",
        "k_gain", "sinks", "w_o"]


def kernel(**inputs):
    import concourse.bacc as bacc
    from concourse.bass_utils import run_bass_kernel_spmd

    nc = bacc.Bacc("TRN2", target_bir_lowering=False, num_devices=1)
    arrays, args = {}, {}
    for name in _INS + ["consts"]:
        a = shape_constants() if name == "consts" else np.ascontiguousarray(inputs[name])
        arrays[f"in_{name}"] = a
        args[name] = nc.dram_tensor(f"in_{name}", a.shape, mybir.dt.from_np(a.dtype), kind="ExternalInput").ap()
    args["out"] = nc.dram_tensor("out_0", (1, S, D), F32, kind="ExternalOutput").ap()
    hybrid_trunk(nc, **args)
    r = run_bass_kernel_spmd(nc, [arrays], core_ids=[0])
    return r.results[0]["out_0"]
```
